# Optimizing a Trainium2 kernel written in Bass

```python
import math
import jax, jax.numpy as jnp
from jax import lax
import numpy as np

D_MODEL = 1024
BATCH = 1
SEQ = 512
DEPTH = 2

GRID_W = 64
CTX_LEN = 256
MIX_WIDTH = D_MODEL
NA_HEADS = 6
NA_HEAD_DIM = 64
NA_WIDTH = NA_HEADS * NA_HEAD_DIM
NA_WIN_H = 8
NA_WIN_W = 16
NA_QBLOCK = 16
NA_STRIP = NA_QBLOCK + NA_WIN_W
DIFF_HEADS = 4
DIFF_QK_DIM = 48
DIFF_V_DIM = 2 * DIFF_QK_DIM
DIFF_WIDTH = DIFF_HEADS * DIFF_V_DIM
DIFF_QBLOCK = 128
ROPE_BASE = 10000.0
CONV_WIDTH = MIX_WIDTH - NA_WIDTH - DIFF_WIDTH
CONV_TAPS = 31
COL_SPLITS = (NA_WIDTH, NA_WIDTH, DIFF_WIDTH, DIFF_WIDTH,
              NA_WIDTH, NA_WIDTH, DIFF_WIDTH, DIFF_WIDTH,
              CONV_WIDTH, CONV_WIDTH, CONV_WIDTH)
IN_COLS = 4 * NA_WIDTH + 4 * DIFF_WIDTH + 3 * CONV_WIDTH
EPS = 1e-6
NEG_INF = -1e30


def _rms(x, g):
    xf = x.astype(jnp.float32)
    y = xf * lax.rsqrt(jnp.mean(xf * xf, axis=-1, keepdims=True) + EPS)
    return (y * g.astype(jnp.float32)).astype(x.dtype)

def _layer_norm(x, g, b):
    xf = x.astype(jnp.float32)
    mu = jnp.mean(xf, axis=-1, keepdims=True)
    var = jnp.mean(jnp.square(xf - mu), axis=-1, keepdims=True)
    y = (xf - mu) * lax.rsqrt(var + EPS) * g.astype(jnp.float32) + b.astype(jnp.float32)
    return y.astype(x.dtype)

def _heads(z, n_heads):
    return z.reshape(z.shape[0], z.shape[1], n_heads, z.shape[-1] // n_heads)

def _split_cols(z, n):
    idx = np.cumsum(COL_SPLITS)[:n - 1].tolist()
    return jnp.split(z, idx, axis=-1)

def _rope_1d(x, pos):
    d = x.shape[-1]
    inv = ROPE_BASE ** (-jnp.arange(0, d, 2, dtype=jnp.float32) / d)
    ang = pos.astype(jnp.float32)[:, None] * inv[None, :]
    cos, sin = jnp.cos(ang)[:, None, :], jnp.sin(ang)[:, None, :]
    xf = x.astype(jnp.float32)
    x1, x2 = xf[..., :d // 2], xf[..., d // 2:]
    return jnp.concatenate([x1 * cos - x2 * sin, x2 * cos + x1 * sin], axis=-1).astype(x.dtype)

def _rope_2d(x, rows, cols):
    half = x.shape[-1] // 2
    return jnp.concatenate([_rope_1d(x[..., :half], rows), _rope_1d(x[..., half:], cols)], axis=-1)

def _na_tables():
    ncb = GRID_W // NA_QBLOCK
    qcols = np.arange(GRID_W).reshape(ncb, NA_QBLOCK)
    kstart = np.clip(np.arange(ncb) * NA_QBLOCK - NA_WIN_W // 2, 0, GRID_W - NA_STRIP)
    kcols = kstart[:, None] + np.arange(NA_STRIP)
    cstart = np.clip(qcols - NA_WIN_W // 2, 0, GRID_W - NA_WIN_W)
    kc = kcols[:, None, :]
    valid = (kc >= cstart[:, :, None]) & (kc < cstart[:, :, None] + NA_WIN_W)
    dc_idx = np.clip(kc - qcols[:, :, None] + NA_WIN_W - 1, 0, 2 * NA_WIN_W - 2)
    return kcols, valid, dc_idx

def _neighbourhood_attention(q, k, v, kc, vc, rpb):
    B, T, H, dh = q.shape
    n_rows = T // GRID_W
    wr = min(NA_WIN_H, n_rows)
    ncb = GRID_W // NA_QBLOCK
    nk = wr * NA_STRIP
    kcols, valid, dc_idx = _na_tables()
    mask = np.broadcast_to(valid[:, :, None, :], (ncb, NA_QBLOCK, wr, NA_STRIP)).reshape(ncb, NA_QBLOCK, nk)
    qg = (q * NA_HEAD_DIM ** -0.5).reshape(B, n_rows, GRID_W, H, dh)
    kg = k.reshape(B, n_rows, GRID_W, H, dh)
    vg = v.reshape(B, n_rows, GRID_W, H, dh)

    def row(r):
        rs = jnp.clip(r - wr // 2, 0, n_rows - wr)

        def strips(t):
            t = lax.dynamic_slice_in_dim(t, rs, wr, axis=1)[:, :, kcols]
            return t.transpose(0, 2, 1, 3, 4, 5).reshape(B, ncb, nk, H, dh)

        ks_, vs_ = strips(kg), strips(vg)
        qr = lax.dynamic_index_in_dim(qg, r, axis=1, keepdims=False).reshape(B, ncb, NA_QBLOCK, H, dh)
        dr_idx = rs + jnp.arange(wr) - r + (NA_WIN_H - 1)
        bias = rpb[:, dr_idx][:, :, dc_idx].transpose(0, 2, 3, 1, 4).reshape(H, ncb, NA_QBLOCK, nk)
        s_loc = jnp.einsum('bnqhd,bnkhd->bhnqk', qr, ks_).astype(jnp.float32) + bias.astype(jnp.float32)
        s_loc = jnp.where(mask, s_loc, NEG_INF)
        s_ctx = jnp.einsum('bnqhd,bkhd->bhnqk', qr, kc).astype(jnp.float32)
        p = jax.nn.softmax(jnp.concatenate([s_loc, s_ctx], axis=-1), axis=-1).astype(v.dtype)
        o = (jnp.einsum('bhnqk,bnkhd->bnqhd', p[..., :nk], vs_)
             + jnp.einsum('bhnqk,bkhd->bnqhd', p[..., nk:], vc))
        return o.reshape(B, GRID_W, H, dh)

    out = lax.map(row, jnp.arange(n_rows))
    return out.transpose(1, 0, 2, 3, 4).reshape(B, T, H * dh)

def _dense_attend(q, k, v):
    s = jnp.einsum('bqhd,bkhd->bhqk', q, k).astype(jnp.float32) * (q.shape[-1] ** -0.5)
    p = jax.nn.softmax(s, axis=-1).astype(v.dtype)
    return jnp.einsum('bhqk,bkhd->bqhd', p, v)

def _diff_attend(q1, q2, k1, k2, v, lam):
    B, Tq, H, d = q1.shape
    nb = Tq // DIFF_QBLOCK
    scale = d ** -0.5

    def to_blocks(t):
        return t.reshape(B, nb, DIFF_QBLOCK, H, d).swapaxes(0, 1)

    def blk(qs):
        a, b = qs
        s1 = jnp.einsum('bqhd,bkhd->bhqk', a, k1).astype(jnp.float32) * scale
        s2 = jnp.einsum('bqhd,bkhd->bhqk', b, k2).astype(jnp.float32) * scale
        w = jax.nn.softmax(s1, axis=-1) - lam * jax.nn.softmax(s2, axis=-1)
        return jnp.einsum('bhqk,bkhe->bqhe', w.astype(v.dtype), v)

    o = lax.map(blk, (to_blocks(q1), to_blocks(q2)))
    return o.swapaxes(0, 1).reshape(B, Tq, H, v.shape[-1])

def _diff_merge(o, subln_g, lam_init):
    return (_rms(o, subln_g) * (1.0 - lam_init)).reshape(o.shape[0], o.shape[1], -1)

def _conformer_conv(a, b, conv_w, conv_b, ln_g, ln_b):
    u = a * jax.nn.sigmoid(b)
    pad = CONV_TAPS // 2
    y = lax.conv_general_dilated(u, conv_w[:, None, :].astype(u.dtype), (1,), [(pad, pad)],
                                 dimension_numbers=('NWC', 'WIO', 'NWC'),
                                 feature_group_count=CONV_WIDTH) + conv_b
    return jax.nn.silu(_layer_norm(y, ln_g, ln_b))

def _layer(x, xc, c, c_ctx, w_mod, b_mod, g_pre, g_post, w_in, w_out, rpb,
           lq1, lk1, lq2, lk2, subln_g, conv_w, conv_b, ln_g, ln_b, layer_idx, update_ctx):
    B, T, _ = x.shape
    t = jnp.arange(T)
    rows, cols = t // GRID_W, t % GRID_W
    d = DIFF_QK_DIM

    shift, scale, gate = jnp.split((jax.nn.silu(c) @ w_mod + b_mod)[:, None, :], 3, axis=-1)
    n_mod = 3 if update_ctx else 2
    mod_c = jnp.split(jax.nn.silu(c_ctx) @ w_mod[:, :n_mod * D_MODEL] + b_mod[:n_mod * D_MODEL], n_mod)

    h = _rms(x, g_pre) * (1.0 + scale) + shift
    hc = _rms(xc, g_pre) * (1.0 + mod_c[1]) + mod_c[0]

    na_k, na_v, df_k, df_v, na_q, na_g, df_q, df_g, cv_a, cv_b, cv_g = _split_cols(h @ w_in, len(COL_SPLITS))
    n_cols = len(COL_SPLITS) if update_ctx else 4
    zc = _split_cols(hc @ w_in[:, :sum(COL_SPLITS[:n_cols])], n_cols)
    nak_c, nav_c, dfk_c, dfv_c = zc[:4]

    nak_c, nav_c = _heads(nak_c, NA_HEADS), _heads(nav_c, NA_HEADS)
    a_out = _neighbourhood_attention(_heads(na_q, NA_HEADS), _heads(na_k, NA_HEADS), _heads(na_v, NA_HEADS),
                                     nak_c, nav_c, rpb)

    lam_init = 0.8 - 0.6 * math.exp(-0.3 * layer_idx)
    lam = (jnp.exp(jnp.sum(lq1 * lk1).astype(jnp.float32))
           - jnp.exp(jnp.sum(lq2 * lk2).astype(jnp.float32)) + lam_init)
    rope = lambda z: _rope_2d(z, rows, cols)
    q, k = _heads(df_q, DIFF_HEADS), _heads(df_k, DIFF_HEADS)
    kc, vc = _heads(dfk_c, DIFF_HEADS), _heads(dfv_c, DIFF_HEADS)
    k1 = jnp.concatenate([rope(k[..., :d]), kc[..., :d]], axis=1)
    k2 = jnp.concatenate([rope(k[..., d:]), kc[..., d:]], axis=1)
    vd = jnp.concatenate([_heads(df_v, DIFF_HEADS), vc], axis=1)
    b_out = _diff_merge(_diff_attend(rope(q[..., :d]), rope(q[..., d:]), k1, k2, vd, lam), subln_g, lam_init)

    c_out = _conformer_conv(cv_a, cv_b, conv_w, conv_b, ln_g, ln_b)

    y = jnp.concatenate([a_out * jax.nn.silu(na_g), b_out * jax.nn.silu(df_g),
                         c_out * jax.nn.silu(cv_g)], axis=-1) @ w_out
    x_new = x + gate * _rms(y, g_post)

    if update_ctx:
        naq_c, nag_c, dfq_c, dfg_c, cva_c, cvb_c, cvg_c = zc[4:]
        a_c = _dense_attend(_heads(naq_c, NA_HEADS), nak_c, nav_c).reshape(B, -1, NA_WIDTH)
        qc = _heads(dfq_c, DIFF_HEADS)
        b_c = _diff_merge(_diff_attend(qc[..., :d], qc[..., d:], kc[..., :d], kc[..., d:], vc, lam),
                          subln_g, lam_init)
        c_c = _conformer_conv(cva_c, cvb_c, conv_w, conv_b, ln_g, ln_b)
        yc = jnp.concatenate([a_c * jax.nn.silu(nag_c), b_c * jax.nn.silu(dfg_c),
                              c_c * jax.nn.silu(cvg_c)], axis=-1) @ w_out
        xc = xc + mod_c[2] * _rms(yc, g_post)
    return x_new, xc

def first_inputs(seed: int = 0) -> dict:
    key = jax.random.key(seed)
    ks = jax.random.split(key, 20)
    f32 = jnp.float32

    def nrm(k, shape, s):
        return s * jax.random.normal(k, shape, f32)

    return {
        'x': nrm(ks[0], (BATCH, SEQ, D_MODEL), 1.0),
        'c': nrm(ks[1], (BATCH, D_MODEL), 1.0),
        'ctx': nrm(ks[2], (BATCH, CTX_LEN, D_MODEL), 1.0),
        'c_ctx': nrm(ks[3], (D_MODEL,), 1.0),
        'w_mod': nrm(ks[4], (DEPTH, D_MODEL, 3 * D_MODEL), 0.5 * D_MODEL ** -0.5),
        'b_mod': nrm(ks[5], (DEPTH, 3 * D_MODEL), 0.02),
        'g_pre': 1.0 + nrm(ks[6], (DEPTH, D_MODEL), 0.1),
        'g_post': 1.0 + nrm(ks[7], (DEPTH, D_MODEL), 0.1),
        'w_in': nrm(ks[8], (DEPTH, D_MODEL, IN_COLS), D_MODEL ** -0.5),
        'w_out': nrm(ks[9], (DEPTH, MIX_WIDTH, D_MODEL), MIX_WIDTH ** -0.5),
        'na_rpb': nrm(ks[10], (DEPTH, NA_HEADS, 2 * NA_WIN_H - 1, 2 * NA_WIN_W - 1), 0.1),
        'diff_lq1': nrm(ks[11], (DEPTH, DIFF_QK_DIM), 0.1),
        'diff_lk1': nrm(ks[12], (DEPTH, DIFF_QK_DIM), 0.1),
        'diff_lq2': nrm(ks[13], (DEPTH, DIFF_QK_DIM), 0.1),
        'diff_lk2': nrm(ks[14], (DEPTH, DIFF_QK_DIM), 0.1),
        'diff_subln_g': 1.0 + nrm(ks[15], (DEPTH, DIFF_V_DIM), 0.1),
        'conv_w': nrm(ks[16], (DEPTH, CONV_TAPS, CONV_WIDTH), CONV_TAPS ** -0.5),
        'conv_b': nrm(ks[17], (DEPTH, CONV_WIDTH), 0.02),
        'conv_ln_g': 1.0 + nrm(ks[18], (DEPTH, CONV_WIDTH), 0.1),
        'conv_ln_b': nrm(ks[19], (DEPTH, CONV_WIDTH), 0.02),
    }

def first_block(x, c, ctx, c_ctx, w_mod, b_mod, g_pre, g_post, w_in, w_out, na_rpb,
              diff_lq1, diff_lk1, diff_lq2, diff_lk2, diff_subln_g,
              conv_w, conv_b, conv_ln_g, conv_ln_b):
    xc = ctx
    for l in range(DEPTH):
        x, xc = _layer(x, xc, c, c_ctx, w_mod[l], b_mod[l], g_pre[l], g_post[l], w_in[l], w_out[l],
                       na_rpb[l], diff_lq1[l], diff_lk1[l], diff_lq2[l], diff_lk2[l], diff_subln_g[l],
                       conv_w[l], conv_b[l], conv_ln_g[l], conv_ln_b[l],
                       layer_idx=l, update_ctx=(l < DEPTH - 1))
    return x


CHUNK = 64
NORM_EPS = 1e-6
FFN_HALF = 0.5
D_FF = 2816

A_HEAD_DIM = 64
A_WIDTH = D_MODEL // 2
A_HEADS = A_WIDTH // A_HEAD_DIM
W_LORA = 64
A_LORA = 64
G_LORA = 128
GN_EPS = 64e-5
A_PROJ = 3 * A_WIDTH + W_LORA + A_LORA + G_LORA
A_SPLITS = (A_WIDTH, 2 * A_WIDTH, 3 * A_WIDTH, 3 * A_WIDTH + W_LORA,
            3 * A_WIDTH + W_LORA + A_LORA)

B_WIDTH = D_MODEL // 2
B_BLOCKS = 8
B_BLOCK_DIM = B_WIDTH // B_BLOCKS
CONV_WIDTH_2 = 4
LRU_C = 8.0

IN_PROJ = A_PROJ + 2 * B_WIDTH

C_HEAD_DIM = 64
C_HEADS = D_MODEL // C_HEAD_DIM
C_WIDTH = C_HEADS * C_HEAD_DIM
Q_BLOCK = 128


def rmsnorm(x, g):
    xf = x.astype(jnp.float32)
    y = xf * lax.rsqrt(jnp.mean(xf * xf, axis=-1, keepdims=True) + NORM_EPS)
    return (y * g.astype(jnp.float32)).astype(x.dtype)

def swiglu(x, w_in, w_out):
    gate, up = jnp.split(x @ w_in, 2, axis=-1)
    return (jax.nn.silu(gate) * up) @ w_out

def shift_right(x):
    return jnp.pad(x, ((0, 0), (1, 0), (0, 0)))[:, :-1]

def rwkv7_step(S, inp):
    r_t, w_t, k_t, v_t, kk_t, a_t = inp
    sa = jnp.einsum("bhvk,bhk->bhv", S, -kk_t)
    S = (S * w_t[:, :, None, :]
         + jnp.einsum("bhv,bhk->bhvk", sa, kk_t * a_t)
         + jnp.einsum("bhv,bhk->bhvk", v_t, k_t))
    y = jnp.einsum("bhvk,bhk->bhv", S, r_t)
    return S, y

def rwkv7_time_mix(pa, mu, w0, w2, a0, a2, g2, k_k, k_a, r_k, lnx_g, lnx_b):
    bsz, seqlen, _ = pa.shape
    dt = pa.dtype
    f32 = jnp.float32
    pa = pa + mu * (shift_right(pa) - pa)
    r, k, v, w_lo, a_lo, g_lo = jnp.split(pa, A_SPLITS, axis=-1)
    w_log = -jax.nn.softplus(-(w0 + jnp.tanh(w_lo) @ w2).astype(f32)) - 0.5
    decay = jnp.exp(-jnp.exp(w_log))
    a = jax.nn.sigmoid((a0 + a_lo @ a2).astype(f32))
    g = jax.nn.sigmoid(g_lo) @ g2

    def heads(t):
        return t.astype(f32).reshape(bsz, seqlen, A_HEADS, A_HEAD_DIM)

    kk = heads(k * k_k)
    kk = kk / jnp.maximum(jnp.sqrt(jnp.sum(kk * kk, axis=-1, keepdims=True)), 1e-12)
    a_h = heads(a)
    k_h = heads(k) * (1.0 + (a_h - 1.0) * k_a.astype(f32).reshape(A_HEADS, A_HEAD_DIM))
    r_h, v_h, w_h = heads(r), heads(v), heads(decay)

    S0 = jnp.zeros((bsz, A_HEADS, A_HEAD_DIM, A_HEAD_DIM), f32)
    xs = tuple(jnp.moveaxis(t, 1, 0) for t in (r_h, w_h, k_h, v_h, kk, a_h))
    _, y = lax.scan(rwkv7_step, S0, xs)
    y = jnp.moveaxis(y, 0, 1)

    mean = jnp.mean(y, axis=-1, keepdims=True)
    var = jnp.mean(jnp.square(y - mean), axis=-1, keepdims=True)
    yn = (y - mean) * lax.rsqrt(var + GN_EPS)
    yn = (yn * lnx_g.astype(f32).reshape(A_HEADS, A_HEAD_DIM)
          + lnx_b.astype(f32).reshape(A_HEADS, A_HEAD_DIM))
    bonus = jnp.sum(r_h * k_h * r_k.astype(f32), axis=-1, keepdims=True) * v_h
    return (yn + bonus).reshape(bsz, seqlen, A_WIDTH).astype(dt) * g

def lru_combine(c1, c2):
    a1, b1 = c1
    a2, b2 = c2
    return a1 * a2, a2 * b1 + b2

def rglru_mix(xb, gb, conv_w, conv_b, gate_a_w, gate_a_b, gate_x_w, gate_x_b, lam):
    bsz, seqlen, _ = xb.shape
    f32 = jnp.float32
    xp = jnp.pad(xb, ((0, 0), (CONV_WIDTH_2 - 1, 0), (0, 0)))
    xc = conv_b + sum(xp[:, i:i + seqlen] * conv_w[i] for i in range(CONV_WIDTH_2))
    blocks = xc.reshape(bsz, seqlen, B_BLOCKS, B_BLOCK_DIM)
    r = jax.nn.sigmoid((jnp.einsum("btni,nij->btnj", blocks, gate_a_w)
                        .reshape(bsz, seqlen, B_WIDTH) + gate_a_b).astype(f32))
    i_g = jax.nn.sigmoid((jnp.einsum("btni,nij->btnj", blocks, gate_x_w)
                          .reshape(bsz, seqlen, B_WIDTH) + gate_x_b).astype(f32))
    log_a = -LRU_C * r * jax.nn.softplus(-lam.astype(f32))
    a = jnp.exp(log_a)
    mult = jnp.sqrt(-jnp.expm1(2.0 * log_a))
    u = mult * i_g * xc.astype(f32)
    _, h = lax.associative_scan(lru_combine, (a, u), axis=1)
    return h.astype(xb.dtype) * jax.nn.gelu(gb)

def even_mixer(h, w_in, mu, w0, w2, a0, a2, g2, k_k, k_a, r_k, lnx_g, lnx_b,
               conv_w, conv_b, gate_a_w, gate_a_b, gate_x_w, gate_x_b, lam, w_out):
    proj = h @ w_in
    pa, xb, gb = jnp.split(proj, (A_PROJ, A_PROJ + B_WIDTH), axis=-1)
    ya = rwkv7_time_mix(pa, mu, w0, w2, a0, a2, g2, k_k, k_a, r_k, lnx_g, lnx_b)
    yb = rglru_mix(xb, gb, conv_w, conv_b, gate_a_w, gate_a_b, gate_x_w, gate_x_b, lam)
    return jnp.concatenate([ya, yb], axis=-1) @ w_out

def stick_breaking_mixer(h, w_qkv, w_out):
    bsz, seqlen, _ = h.shape
    q, k, v = jnp.split(h @ w_qkv, 3, axis=-1)
    q = q.reshape(bsz, seqlen, C_HEADS, C_HEAD_DIM)
    k = k.reshape(bsz, seqlen, C_HEADS, C_HEAD_DIM)
    v = v.reshape(bsz, seqlen, C_HEADS, C_HEAD_DIM)
    scale = 1.0 / math.sqrt(C_HEAD_DIM)
    outs = []
    for s0 in range(0, seqlen, Q_BLOCK):
        end = s0 + Q_BLOCK
        qb, kb, vb = q[:, s0:end], k[:, :end], v[:, :end]
        z = jnp.einsum("bqhd,bkhd->bhqk", qb, kb).astype(jnp.float32) * scale
        q_pos = s0 + jnp.arange(Q_BLOCK)
        k_pos = jnp.arange(end)
        mask = k_pos[None, :] < q_pos[:, None]
        log_1m = jnp.where(mask, jax.nn.log_sigmoid(-z), 0.0)
        between = lax.cumsum(log_1m, axis=3, reverse=True) - log_1m
        att = jnp.where(mask, jnp.exp(jax.nn.log_sigmoid(z) + between), 0.0)
        outs.append(jnp.einsum("bhqk,bkhd->bqhd", att.astype(vb.dtype), vb))
    o = jnp.concatenate(outs, axis=1).reshape(bsz, seqlen, C_WIDTH)
    return o @ w_out

def macaron_layer(x, mixer, ffn1_pre_g, ffn1_post_g, ffn1_w_in, ffn1_w_out,
                  mix_pre_g, mix_post_g, ffn2_pre_g, ffn2_post_g, ffn2_w_in, ffn2_w_out):
    x = x + FFN_HALF * rmsnorm(swiglu(rmsnorm(x, ffn1_pre_g), ffn1_w_in, ffn1_w_out), ffn1_post_g)
    x = x + rmsnorm(mixer(rmsnorm(x, mix_pre_g)), mix_post_g)
    x = x + FFN_HALF * rmsnorm(swiglu(rmsnorm(x, ffn2_pre_g), ffn2_w_in, ffn2_w_out), ffn2_post_g)
    return x

def second_inputs(seed: int = 0) -> dict:
    key = jax.random.key(seed)
    keys = iter(jax.random.split(key, 64))
    f32 = jnp.float32

    def nrm(shape, scale):
        return scale * jax.random.normal(next(keys), shape, f32)

    def gain(n):
        return 1.0 + nrm((n,), 0.05)

    def ffn_params(prefix, d):
        d[prefix + "_pre_g"] = gain(D_MODEL)
        d[prefix + "_post_g"] = gain(D_MODEL)
        d[prefix + "_w_in"] = nrm((D_MODEL, 2 * D_FF), D_MODEL ** -0.5)
        d[prefix + "_w_out"] = nrm((D_FF, D_MODEL), D_FF ** -0.5)

    d = {"x": nrm((BATCH, SEQ, D_MODEL), 1.0)}
    ffn_params("l0_ffn1", d)
    d["l0_mix_pre_g"] = gain(D_MODEL)
    d["l0_mix_post_g"] = gain(D_MODEL)
    d["l0_w_in"] = nrm((D_MODEL, IN_PROJ), D_MODEL ** -0.5)
    d["l0_mu"] = jax.random.uniform(next(keys), (A_PROJ,), f32, 0.0, 1.0)
    d["l0_w0"] = jnp.linspace(-6.0, -1.0, A_WIDTH, dtype=f32) + nrm((A_WIDTH,), 0.1)
    d["l0_w2"] = nrm((W_LORA, A_WIDTH), 0.1)
    d["l0_a0"] = nrm((A_WIDTH,), 0.1)
    d["l0_a2"] = nrm((A_LORA, A_WIDTH), A_LORA ** -0.5)
    d["l0_g2"] = nrm((G_LORA, A_WIDTH), G_LORA ** -0.5)
    d["l0_k_k"] = 0.85 + nrm((A_WIDTH,), 0.02)
    d["l0_k_a"] = 1.0 + nrm((A_WIDTH,), 0.02)
    d["l0_r_k"] = nrm((A_HEADS, A_HEAD_DIM), 0.1)
    d["l0_lnx_g"] = gain(A_WIDTH)
    d["l0_lnx_b"] = nrm((A_WIDTH,), 0.02)
    d["l0_conv_w"] = nrm((CONV_WIDTH_2, B_WIDTH), CONV_WIDTH_2 ** -0.5)
    d["l0_conv_b"] = nrm((B_WIDTH,), 0.02)
    d["l0_gate_a_w"] = nrm((B_BLOCKS, B_BLOCK_DIM, B_BLOCK_DIM), B_BLOCK_DIM ** -0.5)
    d["l0_gate_a_b"] = nrm((B_WIDTH,), 0.02)
    d["l0_gate_x_w"] = nrm((B_BLOCKS, B_BLOCK_DIM, B_BLOCK_DIM), B_BLOCK_DIM ** -0.5)
    d["l0_gate_x_b"] = nrm((B_WIDTH,), 0.02)
    a_pow = jax.random.uniform(next(keys), (B_WIDTH,), f32, 0.9, 0.999) ** (1.0 / LRU_C)
    d["l0_lambda"] = jnp.log(a_pow) - jnp.log1p(-a_pow)
    d["l0_w_out"] = nrm((A_WIDTH + B_WIDTH, D_MODEL), (A_WIDTH + B_WIDTH) ** -0.5)
    ffn_params("l0_ffn2", d)
    ffn_params("l1_ffn1", d)
    d["l1_mix_pre_g"] = gain(D_MODEL)
    d["l1_mix_post_g"] = gain(D_MODEL)
    d["l1_w_qkv"] = nrm((D_MODEL, 3 * C_WIDTH), D_MODEL ** -0.5)
    d["l1_w_out"] = nrm((C_WIDTH, D_MODEL), C_WIDTH ** -0.5)
    ffn_params("l1_ffn2", d)
    return d

def second_block(x,
              l0_ffn1_pre_g, l0_ffn1_post_g, l0_ffn1_w_in, l0_ffn1_w_out,
              l0_mix_pre_g, l0_mix_post_g, l0_w_in, l0_mu, l0_w0, l0_w2, l0_a0, l0_a2,
              l0_g2, l0_k_k, l0_k_a, l0_r_k, l0_lnx_g, l0_lnx_b, l0_conv_w, l0_conv_b,
              l0_gate_a_w, l0_gate_a_b, l0_gate_x_w, l0_gate_x_b, l0_lambda, l0_w_out,
              l0_ffn2_pre_g, l0_ffn2_post_g, l0_ffn2_w_in, l0_ffn2_w_out,
              l1_ffn1_pre_g, l1_ffn1_post_g, l1_ffn1_w_in, l1_ffn1_w_out,
              l1_mix_pre_g, l1_mix_post_g, l1_w_qkv, l1_w_out,
              l1_ffn2_pre_g, l1_ffn2_post_g, l1_ffn2_w_in, l1_ffn2_w_out):
    def layer0(t):
        mixer = lambda h: even_mixer(h, l0_w_in, l0_mu, l0_w0, l0_w2, l0_a0, l0_a2, l0_g2,
                                     l0_k_k, l0_k_a, l0_r_k, l0_lnx_g, l0_lnx_b,
                                     l0_conv_w, l0_conv_b, l0_gate_a_w, l0_gate_a_b,
                                     l0_gate_x_w, l0_gate_x_b, l0_lambda, l0_w_out)
        return macaron_layer(t, mixer, l0_ffn1_pre_g, l0_ffn1_post_g, l0_ffn1_w_in, l0_ffn1_w_out,
                             l0_mix_pre_g, l0_mix_post_g,
                             l0_ffn2_pre_g, l0_ffn2_post_g, l0_ffn2_w_in, l0_ffn2_w_out)

    def layer1(t):
        mixer = lambda h: stick_breaking_mixer(h, l1_w_qkv, l1_w_out)
        return macaron_layer(t, mixer, l1_ffn1_pre_g, l1_ffn1_post_g, l1_ffn1_w_in, l1_ffn1_w_out,
                             l1_mix_pre_g, l1_mix_post_g,
                             l1_ffn2_pre_g, l1_ffn2_post_g, l1_ffn2_w_in, l1_ffn2_w_out)

    layers = [layer0, layer1]
    for i in range(DEPTH):
        x = layers[i](x)
    return x


def setup_inputs(seed=0):
    out = dict(first_inputs(seed))
    for name, value in second_inputs(seed + 1).items():
        if name != "x":
            out[name + "_2"] = value
    return out


def reference(
    x, c, ctx, c_ctx, w_mod, b_mod, g_pre, g_post, w_in, w_out, na_rpb, diff_lq1, diff_lk1,
    diff_lq2, diff_lk2, diff_subln_g, conv_w, conv_b, conv_ln_g, conv_ln_b, l0_ffn1_pre_g_2,
    l0_ffn1_post_g_2, l0_ffn1_w_in_2, l0_ffn1_w_out_2, l0_mix_pre_g_2, l0_mix_post_g_2,
    l0_w_in_2, l0_mu_2, l0_w0_2, l0_w2_2, l0_a0_2, l0_a2_2, l0_g2_2, l0_k_k_2, l0_k_a_2,
    l0_r_k_2, l0_lnx_g_2, l0_lnx_b_2, l0_conv_w_2, l0_conv_b_2, l0_gate_a_w_2, l0_gate_a_b_2,
    l0_gate_x_w_2, l0_gate_x_b_2, l0_lambda_2, l0_w_out_2, l0_ffn2_pre_g_2, l0_ffn2_post_g_2,
    l0_ffn2_w_in_2, l0_ffn2_w_out_2, l1_ffn1_pre_g_2, l1_ffn1_post_g_2, l1_ffn1_w_in_2,
    l1_ffn1_w_out_2, l1_mix_pre_g_2, l1_mix_post_g_2, l1_w_qkv_2, l1_w_out_2, l1_ffn2_pre_g_2,
    l1_ffn2_post_g_2, l1_ffn2_w_in_2, l1_ffn2_w_out_2,
):
    x = first_block(
        x, c, ctx, c_ctx, w_mod, b_mod, g_pre, g_post, w_in, w_out, na_rpb, diff_lq1, diff_lk1,
        diff_lq2, diff_lk2, diff_subln_g, conv_w, conv_b, conv_ln_g, conv_ln_b,
    )
    return second_block(
        x, l0_ffn1_pre_g_2, l0_ffn1_post_g_2, l0_ffn1_w_in_2, l0_ffn1_w_out_2, l0_mix_pre_g_2,
        l0_mix_post_g_2, l0_w_in_2, l0_mu_2, l0_w0_2, l0_w2_2, l0_a0_2, l0_a2_2, l0_g2_2,
        l0_k_k_2, l0_k_a_2, l0_r_k_2, l0_lnx_g_2, l0_lnx_b_2, l0_conv_w_2, l0_conv_b_2,
        l0_gate_a_w_2, l0_gate_a_b_2, l0_gate_x_w_2, l0_gate_x_b_2, l0_lambda_2, l0_w_out_2,
        l0_ffn2_pre_g_2, l0_ffn2_post_g_2, l0_ffn2_w_in_2, l0_ffn2_w_out_2, l1_ffn1_pre_g_2,
        l1_ffn1_post_g_2, l1_ffn1_w_in_2, l1_ffn1_w_out_2, l1_mix_pre_g_2, l1_mix_post_g_2,
        l1_w_qkv_2, l1_w_out_2, l1_ffn2_pre_g_2, l1_ffn2_post_g_2, l1_ffn2_w_in_2,
        l1_ffn2_w_out_2,
    )


_drawn_inputs = setup_inputs


def setup_inputs(seed=0):
    import zlib

    import numpy as np

    out = dict(_drawn_inputs(seed))
    spreads = {}
    factors = {'na_rpb': 8.0,
     'diff_lq1': 3.847,
     'diff_lk1': 3.18,
     'conv_b': 3.907,
     'conv_ln_b': 6.978,
     'l0_k_k_2': 34.151,
     'l0_k_a_2': 4.872,
     'l0_lnx_b_2': 5.23,
     'l0_gate_a_b_2': 8.0,
     'l0_gate_x_b_2': 8.0,
     'l0_ffn2_post_g_2': 3.397,
     'l1_ffn1_post_g_2': 3.596,
     'l1_ffn2_pre_g_2': 3.256,
     'l1_ffn2_post_g_2': 4.622,
     'l1_mix_post_g_2': 3.031}
    for name, (base, spread) in spreads.items():
        noise = np.random.default_rng([zlib.crc32(name.encode()), seed]).standard_normal(out[name].shape)
        drawn = base * np.exp(spread * noise) if base else spread * noise
        out[name] = __import__('jax').numpy.asarray(drawn.astype(out[name].dtype))
    for name, factor in factors.items():
        out[name] = (out[name] * factor).astype(out[name].dtype)
    return out
```

```python
import math
from contextlib import ExitStack

import numpy as np
import concourse.bass as bass
from concourse import mybir

P = 128
D = 1024
DT = D // P
T = 512
TC = 256
TA = T + TC
DEPTH = 2
GRID_W = 64
NA_HEADS, NA_DH = 6, 64
NA_W = NA_HEADS * NA_DH
WIN_H, WIN_W = 8, 16
DF_HEADS, DF_QK = 4, 48
DF_V = 2 * DF_QK
GROUP = 384
IN_COLS = 3840
CONV_W, TAPS = 256, 31
PAD = TAPS // 2
CONV_TOK = PAD + T + PAD + TC + PAD
CONV_OUT = T + PAD + TC
BIAS_ROWS = 14
D_FF = 2816
FT = D_FF // P
A_W = 512
RW_HEADS = 8
HD = 64
CH = 128
NCH = T // CH
LEVELS = [1, 2, 4, 8, 16, 32, 64]
SB_HEADS = 16
EPS = 1e-6
GN_EPS = 64e-5
NEG = -1e30
SLOT = 2048
N_SLOTS = 6
ARENA = 25550

def column_table():
    names = []
    for l in range(DEPTH):
        names += [(f"b_mod{l}", 24), (f"g_pre{l}", 8), (f"g_post{l}", 8), (f"subln{l}", 1),
                  (f"conv_w{l}", 2 * TAPS), (f"conv_b{l}", 2), (f"ln_g{l}", 2), (f"ln_b{l}", 2),
                  (f"lq{l}", 2), (f"lk{l}", 2)]
    names += [("cond", 16)]
    for f in ("l0_ffn1", "l0_ffn2", "l1_ffn1", "l1_ffn2", "l0_mix", "l1_mix"):
        names += [(f + "_pre", 8), (f + "_post", 8)]
    names += [("mu", 14), ("w0", 4), ("a0", 4), ("k_k", 4), ("k_a", 4), ("r_k", 4), ("lnx_g", 4),
              ("lnx_b", 4), ("rconv_w", 16), ("rconv_b", 4), ("ga_b", 4), ("gx_b", 4), ("lam", 4)]
    at, out = 0, {}
    for name, n in names:
        out[name] = (at, n)
        at += n
    return out, at


COLUMNS, N_COLUMNS = column_table()

CONSTS, N_CONST = {}, 0
for _name, _n in (("ident", 128), ("ones", 128), ("head_ones", 128), ("rot", 96), ("half", 1), ("eps", 2),
                  ("cos", 512), ("sin", 512), ("na_mask", 64), ("upper", 256), ("lower", 128),
                  ("suffix", 128), ("minus", 128), ("turn", 128)):
    CONSTS[_name] = (N_CONST, _n)
    N_CONST += _n


def w_in_pieces():
    return [0, 1, 5, 4, 2, 3, 7, 6, 8, 9]


class Engine:

    def __init__(self, sem):
        self.sem, self.count, self.items, self.reached = sem, 0, [], {}

    def wait(self, after):
        for tok in after:
            if tok is None:
                continue
            sem, value = tok
            if self.reached.get(id(sem), 0) < value:
                self.reached[id(sem)] = value
                self.items.append(lambda e, s=sem, v=value: e.wait_ge(s, v))

    def do(self, fn, after=(), signal=True):
        self.wait(after)
        if signal:
            self.count += 1
            self.items.append(lambda e: fn(e).then_inc(self.sem, 1))
            return (self.sem, self.count)
        self.items.append(fn)
        return None

    @property
    def last(self):
        return (self.sem, self.count) if self.count else None

    def dma(self, out, in_, queue, after=()):
        self.wait(after)
        queue[1] += 16
        s = queue[0]
        self.items.append(lambda e: e.dma_start(out, in_).then_inc(s, 16))
        return (s, queue[1])

    def run(self, e):
        for item in self.items:
            item(e)


class Ring:

    def __init__(self, buffers):
        self.buffers, self.n, self.left = buffers, 0, [()] * len(buffers)

    def take(self):
        i = self.n % len(self.buffers)
        self.n += 1
        free, self.left[i] = self.left[i], None
        assert free is not None, "a buffer is taken before its last user has left"
        return i, self.buffers[i], list(free)

    def leave(self, i, *tokens):
        self.left[i] = tokens


def build(nc, ins, out_dram, upto=None, probe_dram=None):
    f32 = mybir.dt.float32
    ALU = mybir.AluOpType
    ACT = mybir.ActivationFunctionType
    X_AXIS = mybir.AxisListType.X
    ADD, SUB, MUL, MAX, MIN = ALU.add, ALU.subtract, ALU.mult, ALU.max, ALU.min
    ctx = ExitStack()
    with ctx:
        def sb(name, shape):
            return ctx.enter_context(nc.sbuf_tensor(name, shape, f32))

        def sem(name):
            return ctx.enter_context(nc.semaphore(name))

        x_sb = sb("x_sb", [P, DT, TA])
        h_sb = sb("h_sb", [P, DT, TA])
        w_sb = [sb(f"w_slot{i}", [P, SLOT]) for i in range(N_SLOTS)]
        const = sb("const", [P, N_CONST])
        par = sb("par", [P, N_COLUMNS])
        small = sb("small", [P, 320])
        arena = sb("arena", [P, ARENA])
        banks = Ring([ctx.enter_context(nc.psum_tensor(f"bank{i}", [P, 512], f32)) for i in range(8)])

        pe, dve, act, pool, sp = (Engine(sem(n)) for n in ("s_pe", "s_dve", "s_act", "s_pool", "s_sp"))
        slots = Ring(w_sb)
        slot_q = [[sem(f"s_slot{i}"), 0] for i in range(N_SLOTS)]
        const_q, par_q, x_q, out_q, rpb_q, gate_q = ([sem(n), 0] for n in
                                                    ("s_const", "s_par", "s_x", "s_out", "s_rpb", "s_gate"))

        def C(name, rows=P):
            at, n = CONSTS[name]
            return const[0:rows, at:at + n]

        def col(name, i=0, n=1, rows=P, base=0):
            at = COLUMNS[name][0] + i
            return par[base:base + rows, at:at + n]

        ident, ones, head_ones = C("ident"), C("ones"), C("head_ones")

        class Area:

            def __init__(self, start=0):
                self.at = start

            def take(self, *shape):
                n = int(np.prod(shape))
                v = arena[:, self.at:self.at + n]
                self.at += n
                assert self.at <= ARENA, self.at
                if len(shape) == 2:
                    v = v.rearrange("p (a b) -> p a b", a=shape[0])
                if len(shape) == 3:
                    v = v.rearrange("p (a b c) -> p a b c", a=shape[0], b=shape[1])
                return v

        def fence():
            ends = [e.last for e in (pe, dve, act, pool)]
            for e in (dve, act, pool):
                e.wait(ends)
            for q in (rpb_q, gate_q):
                for e in (dve, act, pool):
                    if q[1]:
                        e.wait([(q[0], q[1])])
            return ends

        const_in = sp.dma(const[:, :], ins["const"], const_q)
        par_in = sp.dma(par[:, :], ins["par"], par_q)
        x_in = sp.dma(x_sb[:, :, :], ins["xt"], x_q)
        loaded = [const_in, par_in]
        for e in (dve, act, pool, pe):
            e.wait(loaded)

        def load(dram):
            i, slot, free = slots.take()
            n = dram.shape[-1]
            tok = sp.dma(slot[:, 0:n], dram, slot_q[i], after=free)
            return i, slot, tok

        def mm(out, lhsT, rhs, first, last, after=(), signal=None):
            signal = last if signal is None else signal
            return pe.do(lambda e: e.matmul(out, lhsT, rhs, start=first, stop=last, skip_group_check=True),
                         after, signal)

        def tt(e, out, a, b, op, after=()):
            return e.do(lambda g: g.tensor_tensor(out, a, b, op), after)

        def ts(e, out, a, s1, op0, s2=None, op1=None, after=()):
            if op1 is None:
                return e.do(lambda g: g.tensor_scalar(out, a, s1, None, op0), after)
            return e.do(lambda g: g.tensor_scalar(out, a, s1, s2, op0, op1), after)

        def stt(out, a, s, b, op0, op1, after=()):
            return dve.do(lambda g: g.scalar_tensor_tensor(out, a, s, b, op0, op1), after)

        def copy(e, out, a, after=()):
            if e is act:
                return act.do(lambda g: g.activation(out, a, ACT.Copy), after)
            return e.do(lambda g: g.tensor_copy(out, a), after)

        def fn(out, a, f, after=(), scale=1.0, bias=None, accum=None):
            kw = {}
            if bias is not None:
                kw["bias"] = bias
            if accum is not None:
                kw["accum_out"] = accum
            return act.do(lambda g: g.activation(out, a, f, scale=scale, **kw), after)

        def memset(e, out, v, after=()):
            return e.do(lambda g: g.memset(out, v), after)

        def recip(out, a, after=()):
            return dve.do(lambda g: g.reciprocal(out, a), after)

        MODS, GS, GP, LAM, HALF_G, C8 = 0, 48, 64, 80, 96, 128
        mods = small[:, MODS:MODS + 48].rearrange("p (t s) -> p t s", t=24)
        gs = small[:, GS:GS + 16].rearrange("p (t s) -> p t s", t=8)
        gp = small[:, GP:GP + 16].rearrange("p (t s) -> p t s", t=8)
        lam_col = small[:, LAM:LAM + 4]
        half_g = small[:, HALF_G:HALF_G + 8]
        stat = small[:, 160:320]

        def spans(total):
            return [(0, T), (T, TA)] if total == TA else [(0, total)]

        def mean_square(tiles, c0, c1, n_feat, area_sq, after, rows=P, stationary=None, eps=0):
            i, bank, free = banks.take()
            n = c1 - c0
            for j, tile in enumerate(tiles):
                k, sq, sfree = area_sq.take()
                t_sq = fn(sq[0:rows, 0:n], tile[:, c0:c1], ACT.Square, after=list(after) + sfree)
                st = ones[0:rows, 0:rows] if stationary is None else stationary
                t_mm = mm(bank[0:rows, 0:n], st, sq[0:rows, 0:n], j == 0, j == len(tiles) - 1,
                          after=[t_sq] + (free if j == 0 else []), signal=True)
                area_sq.leave(k, t_mm)
            return i, bank, t_mm

        def rstd_of(out, i, bank, t_mm, n, n_feat, after=(), rows=P, eps=0):
            eps_ap = const[0:rows, CONSTS["eps"][0] + eps:CONSTS["eps"][0] + eps + 1]
            t = fn(out, bank[0:rows, 0:n], ACT.Sqrt, after=[t_mm] + list(after), scale=1.0 / n_feat, bias=eps_ap)
            banks.leave(i, t)
            return recip(out, out, after=[t])

        def norm(total, gain, shift=None, after=()):
            area = Area()
            sq = Ring([area.take(T) for _ in range(3)])
            rs = area.take(total)
            toks = []
            for s, (c0, c1) in enumerate(spans(total)):
                b = mean_square([x_sb[:, j, :] for j in range(DT)], c0, c1, D, sq, after)
                t = rstd_of(rs[:, c0:c1], *b, c1 - c0, D)
                for j in range(DT):
                    t2 = stt(h_sb[:, j, c0:c1], x_sb[:, j, c0:c1], gain(j, s), rs[:, c0:c1], MUL, MUL, after=[t])
                    if shift is not None:
                        t2 = fn(h_sb[:, j, c0:c1], h_sb[:, j, c0:c1], ACT.Identity, after=[t2], bias=shift(j, s))
                toks.append(t2)
            return toks

        def add_normed(total, gain, after):
            area = Area()
            sq = Ring([area.take(T) for _ in range(3)])
            rs = area.take(total)
            tmp = area.take(2, T)
            prev = [None, None]
            for s, (c0, c1) in enumerate(spans(total)):
                b = mean_square([h_sb[:, j, :] for j in range(DT)], c0, c1, D, sq, after)
                t = rstd_of(rs[:, c0:c1], *b, c1 - c0, D)
                for j in range(DT):
                    t1 = stt(tmp[:, j % 2, 0:c1 - c0], h_sb[:, j, c0:c1], gain(j, s), rs[:, c0:c1],
                             MUL, MUL, after=[t, prev[j % 2]])
                    prev[j % 2] = tt(pool, x_sb[:, j, c0:c1], x_sb[:, j, c0:c1], tmp[:, j % 2, 0:c1 - c0], ADD,
                                     after=[t1])
                x_done = prev
            return [x_done[0], x_done[1], pool.last]

        def project(pieces, widths, total, consume, after):
            got = [load(d) for d in pieces]
            n_k = DT // len(pieces)
            cols = sum(widths)
            at = 0
            for m, w in enumerate(widths):
                for (c0, c1) in spans(total):
                    i, bank, free = banks.take()
                    for k in range(DT):
                        s, slot, tok = got[k // n_k]
                        o = (k % n_k) * cols + at
                        t = mm(bank[0:w, 0:c1 - c0], slot[:, o:o + w], h_sb[:, k, c0:c1], k == 0, k == DT - 1,
                               after=[tok] + (free + list(after) if k == 0 else []))
                    banks.leave(i, consume(m, c0, c1, bank[0:w, 0:c1 - c0], t))
                at += w
            for s, slot, tok in got:
                slots.leave(s, pe.last)

        def project_tokens(pieces, width, n_tok, consume, after):
            got = [load(d) for d in pieces]
            n_k = DT // len(pieces)
            for m in range(n_tok // P):
                i, bank, free = banks.take()
                for k in range(DT):
                    s, slot, tok = got[k // n_k]
                    o = (k % n_k) * width
                    t = mm(bank[:, 0:width], h_sb[:, k, m * P:(m + 1) * P], slot[:, o:o + width], k == 0,
                           k == DT - 1, after=[tok] + (free + list(after) if k == 0 else []))
                banks.leave(i, consume(m, bank[:, 0:width], t))
            for s, slot, tok in got:
                slots.leave(s, pe.last)

        def project_out(pieces_of, k_tiles, total, after, rows=None):
            n_k = len(k_tiles)
            for m in range(DT):
                pieces = pieces_of(m)
                got = [load(d) for d in pieces]
                per = n_k // len(pieces)
                for (c0, c1) in spans(total):
                    i, bank, free = banks.take()
                    for k, z in enumerate(k_tiles):
                        s, slot, tok = got[k // per]
                        r = z.shape[0]
                        o = (k % per) * P
                        t = mm(bank[:, 0:c1 - c0], slot[0:r, o:o + P], z[:, c0:c1], k == 0, k == n_k - 1,
                               after=[tok] + (free + list(after) if k == 0 else []))
                    e = act if m % 2 else dve
                    banks.leave(i, copy(e, h_sb[:, m, c0:c1], bank[:, 0:c1 - c0], after=[t]))
                for s, slot, tok in got:
                    slots.leave(s, pe.last)
            return [act.last, dve.last]

        def transpose(out, in_, after=(), signal=False):
            k = in_.shape[0]
            return pe.do(lambda e: e.transpose(out, in_, ident[0:k, 0:k]), after, signal)

        def modulation(l, total):
            area = Area()
            cond = area.take(8, 2)
            t_c = fn(cond, col("cond", 0, 16).rearrange("p (k s) -> p k s", k=8), ACT.Silu)
            i, bank, free = banks.take()
            for c in range(12):
                s, slot, tok = load(ins[f"w_mod{l}"][c])
                for m in range(2):
                    o = 2 * (2 * c + m)
                    for k in range(DT):
                        t = mm(bank[:, o:o + 2], slot[:, k * 256 + m * P:k * 256 + (m + 1) * P], cond[:, k, :],
                               k == 0, k == DT - 1, after=[t_c, tok] + free)
                slots.leave(s, pe.last)
            b = col(f"b_mod{l}", 0, 24)
            for s in range(2):
                t = tt(dve, mods[:, :, s], bank[:, 0:48].rearrange("p (t s) -> p t s", t=24)[:, :, s], b, ADD,
                       after=[t])
            banks.leave(i, t)
            for s in range(2):
                t1 = ts(dve, gs[:, :, s], mods[:, 8:16, s], 1.0, ADD, after=[t])
                t1 = tt(dve, gs[:, :, s], gs[:, :, s], col(f"g_pre{l}", 0, 8), MUL, after=[t1])
                t2 = tt(dve, gp[:, :, s], mods[:, 16:24, s], col(f"g_post{l}", 0, 8), MUL)
            prod = area.take(2)
            t3 = tt(dve, prod[0:DF_QK], col(f"lq{l}", 0, 2, DF_QK), col(f"lk{l}", 0, 2, DF_QK), MUL)
            i, bank, free = banks.take()
            t3 = mm(bank[:, 0:2], ones[0:DF_QK, :], prod[0:DF_QK], True, True, after=[t3] + free)
            t3 = fn(lam_col[:, 0:2], bank[:, 0:2], ACT.Exp, after=[t3])
            banks.leave(i, t3)
            t3 = tt(dve, lam_col[:, 2:3], lam_col[:, 0:1], lam_col[:, 1:2], SUB, after=[t3])
            lam_init = 0.8 - 0.6 * math.exp(-0.3 * l)
            t3 = ts(dve, lam_col[:, 3:4], lam_col[:, 2:3], -1.0, MUL, -lam_init, ADD, after=[t3])
            t4 = ts(dve, lam_col[:, 0:1], col(f"subln{l}"), 1.0 - lam_init, MUL, after=[t3])
            return [t1, t2, t3, t4]

        def softmax_rows(s_ap, n, st, scale, after):
            t = dve.do(lambda g: g.reduce_max(st[:, 0:1], s_ap, X_AXIS), after)
            t = ts(dve, st[:, 0:1], st[:, 0:1], -scale, MUL, after=[t])
            return fn(s_ap, s_ap, ACT.Exp, after=[t], scale=scale, bias=st[:, 0:1], accum=st[:, 1:2])

        def transposed_values(p_tiles, n_keys, pt, v_of, out_rows, out_base, key0, finish, t_p, pt_free):
            nq = len(p_tiles)
            for j in range(n_keys):
                i, bank, free = banks.take()
                for q, ptile in enumerate(p_tiles):
                    t = transpose(bank[:, q * P:(q + 1) * P], ptile[:, j * P:(j + 1) * P], after=free + t_p,
                                  signal=(q == nq - 1))
                e = act if j % 2 else dve
                banks.leave(i, copy(e, pt[:, j, 0:nq * P], bank[:, 0:nq * P], after=[t] + pt_free))
            t_in = [act.last, dve.last]
            i, bank, free = banks.take()
            o = bank[out_base:out_base + out_rows, 0:nq * P]
            for j in range(n_keys):
                t = mm(o, v_of(key0 + j), pt[:, j, 0:nq * P], j == 0, j == n_keys - 1, after=t_in + free)
            banks.leave(i, finish(o, t))
            return t

        def na_stage(l, total, area0, mix, h_ready):
            area = Area(area0)
            kT, qT, v = area.take(3, TA), area.take(3, TA), area.take(6, NA_W)
            bias = area.take(NA_HEADS * BIAS_ROWS, GRID_W)
            w_in = ins[f"w_in{l}"]

            def pieces(g):
                return [w_in[2 * g], w_in[2 * g + 1]]

            p_sb = area.take(4, TA)
            pt = area.take(6, T)
            flipped = arena[:, area.at - 6144:area.at - 6144 + NA_HEADS * BIAS_ROWS * GRID_W]
            rows = flipped.rearrange("p (a b) -> p a b", b=GRID_W)
            table = ins[f"rpb{l}"]
            for r2 in range(2):
                for hh in range(NA_HEADS):
                    src = bass.AP(tensor=table.tensor, offset=table.offset + (hh * 15 + 1 - r2) * P,
                                  ap=[[1, GRID_W], [P, BIAS_ROWS], [1, GRID_W]])
                    dst = rows[r2 * 64:(r2 + 1) * 64, hh * BIAS_ROWS:(hh + 1) * BIAS_ROWS, :]
                    t_b = sp.dma(dst, src, rpb_q, after=stage_ends)
            mask, n_rows = C("na_mask"), NA_HEADS * BIAS_ROWS
            for a_ in range(0, n_rows, 8):
                n = min(8, n_rows - a_)
                i, bank, free = banks.take()
                w = n * GRID_W
                t = mm(bank[:, 0:w], C("turn"), flipped[:, a_ * GRID_W:a_ * GRID_W + w], True, True, after=free + [t_b])
                t_bias = tt(dve, bias[:, a_:a_ + n, :], bank[:, 0:w].rearrange("p (a b) -> p a b", a=n),
                            mask.rearrange("p (a b) -> p a b", a=1).broadcast_to((P, n, GRID_W)), ADD, after=[t])
                banks.leave(i, t_bias)

            project(pieces(0), [P] * 3, TA, lambda m, c0, c1, b, t: copy(act, kT[:, m, c0:c1], b, after=[t]), h_ready)
            project_tokens(pieces(1), NA_W, TA, lambda m, b, t: copy(dve, v[:, m, :], b, after=[t]), h_ready)
            project(pieces(5), [P] * 3, total,
                    lambda m, c0, c1, b, t: fn(mix[:, m, c0:c1], b, ACT.Silu, after=[t]), h_ready)
            project(pieces(4), [P] * 3, total,
                    lambda m, c0, c1, b, t: ts(dve, qT[:, m, c0:c1], b, NA_DH ** -0.5, MUL, after=[t]), h_ready)
            ready = [act.last, dve.last]

            pt_free = []
            p_free = []
            for h in range(NA_HEADS):
                p, b0 = h // 2, 64 * (h % 2)
                jobs = [([0, 1, 2, 3], True)] + ([([4, 5], False)] if total == TA else [])
                for tiles, local in jobs:
                    t_p = []
                    for n, q in enumerate(tiles):
                        st = stat[:, 4 * n:4 * n + 4]
                        s = p_sb[:, n, :] if local else p_sb[:, n, T:TA]
                        if local:
                            i, bank, free = banks.take()
                            t = mm(bank[:, :], qT[b0:b0 + 64, p, q * P:(q + 1) * P], kT[b0:b0 + 64, p, 0:T],
                                   True, True, after=free + ready)
                            j0 = 6 - 2 * q
                            bs = bias[:, h * BIAS_ROWS + j0:h * BIAS_ROWS + j0 + 8, :]
                            t = tt(dve, s[:, 0:T].rearrange("p (a b) -> p a b", a=8),
                                   bank[:, :].rearrange("p (a b) -> p a b", a=8), bs, ADD, after=[t] + p_free)
                            banks.leave(i, t)
                        i, bank, free = banks.take()
                        t2 = mm(bank[:, 0:TC], qT[b0:b0 + 64, p, q * P:(q + 1) * P], kT[b0:b0 + 64, p, T:TA],
                                True, True, after=free + ready)
                        t2 = copy(act, p_sb[:, n, T:TA], bank[:, 0:TC], after=[t2] + p_free)
                        banks.leave(i, t2)
                        t = softmax_rows(s, s.shape[-1], st, 1.0, [t2, dve.last])
                        t = recip(st[:, 2:3], st[:, 1:2], after=[t])
                        t_p.append(ts(dve, s, s, st[:, 2:3], MUL, after=[t]))
                    c0 = tiles[0] * P
                    n_q = len(tiles) * P
                    src = [p_sb[:, n, :] if local else p_sb[:, n, T:TA] for n in range(len(tiles))]

                    def finish(o, t):
                        m = mix[b0:b0 + 64, p, c0:c0 + n_q]
                        return tt(dve, m, o, m, MUL, after=[t])
                    t = transposed_values(src, 6 if local else 2, pt, lambda j: v[:, j, h * 64:(h + 1) * 64], 64, b0,
                                          0 if local else 4, finish, t_p, pt_free)
                    pt_free = [t]
                    p_free = [pe.last]

        def diff_stage(l, total, area0, mix, h_ready):
            area = Area(area0)
            kd, qd = area.take(4, TA), area.take(4, TA)
            v = area.take(6, NA_W)
            raw = Ring([area.take(T) for _ in range(2)])
            tmp = Ring([area.take(T) for _ in range(2)])
            q2 = area.take(TA)
            w_in = ins[f"w_in{l}"]
            rot, cos, sin = C("rot", 96), C("cos", 96), C("sin", 96)

            def pieces(g):
                return [w_in[2 * g], w_in[2 * g + 1]]

            def roped(dst):
                def consume(m, c0, c1, b, t):
                    if c0 >= T:
                        return copy(act, dst[0:96, m, c0:c1], b, after=[t])
                    r, raw_t, rfree = raw.take()
                    u, tmp_t, ufree = tmp.take()
                    t_raw = copy(act, raw_t[0:96], b, after=[t] + rfree)
                    i, bank, free = banks.take()
                    t1 = mm(bank[0:96, 0:T], rot, raw_t[0:96], True, True, after=[t_raw] + free)
                    t1 = tt(dve, tmp_t[0:96], bank[0:96, 0:T], sin, MUL, after=[t1] + ufree)
                    banks.leave(i, t1)
                    t2 = tt(dve, dst[0:96, m, 0:T], raw_t[0:96], cos, MUL, after=[t_raw])
                    raw.leave(r, t2, t1)
                    t3 = tt(dve, dst[0:96, m, 0:T], dst[0:96, m, 0:T], tmp_t[0:96], ADD, after=[t1, t2])
                    tmp.leave(u, t3)
                    return t_raw
                return consume

            project(pieces(2), [DF_V] * 4, TA, roped(kd), h_ready)
            project_tokens(pieces(3), NA_W, TA, lambda m, b, t: copy(act, v[:, m, :], b, after=[t]), h_ready)
            project(pieces(7), [DF_V] * 4, total,
                    lambda m, c0, c1, b, t: fn(mix[0:96, 3 + m, c0:c1], b, ACT.Silu, after=[t]), h_ready)
            project(pieces(6), [DF_V] * 4, total, roped(qd), h_ready)
            ready = [act.last, dve.last]
            p1 = area.take(4, TA)
            p2 = Ring([area.take(TA)])
            pt = area.take(6, T)
            sq = Ring([tmp.buffers[0]])
            rs, o_sb = raw.buffers[0], raw.buffers[1]
            half = const[0:96, CONSTS["half"][0]:CONSTS["half"][0] + 1]
            scale = DF_QK ** -0.5
            pt_free, p_free = [], []
            for h in range(DF_HEADS):
                t_q2 = ts(dve, q2[0:96, 0:total], qd[0:96, h, 0:total], half, MUL, after=ready + [pe.last])
                jobs = [([0, 1, 2, 3], True)] + ([([4, 5], False)] if total == TA else [])
                for tiles, local in jobs:
                    t_p = []
                    k0 = 0 if local else T
                    for n, q in enumerate(tiles):
                        st = stat[:, 4 * n:4 * n + 4]
                        st2 = stat[:, 16 + 4 * n:20 + 4 * n]
                        pi, p2_t, p2_free = p2.take()
                        s1, s2 = p1[:, n, k0:TA], p2_t[:, k0:TA]
                        done = []
                        for dst, qq, kk, fr in ((s1, qd[0:48, h], kd[0:48, h], p_free), (s2, q2[0:96], kd[0:96, h], p2_free)):
                            for (a, b) in ([(0, T)] if local else []) + [(T, TA)]:
                                i, bank, free = banks.take()
                                t = mm(bank[:, 0:b - a], qq[:, q * P:(q + 1) * P], kk[:, a:b], True, True,
                                       after=free + ready + [t_q2])
                                t = copy(act, dst[:, a - k0:b - k0], bank[:, 0:b - a], after=[t] + list(fr))
                                banks.leave(i, t)
                                done.append(t)
                        ta = softmax_rows(s1, 0, st, scale, done)
                        tb = softmax_rows(s2, 0, st2, scale, done)
                        t = recip(st[:, 2:3], st[:, 1:2], after=[ta])
                        t = ts(dve, s1, s1, st[:, 2:3], MUL, after=[t])
                        t2 = recip(st2[:, 2:3], st2[:, 1:2], after=[tb])
                        t2 = tt(dve, st2[:, 3:4], st2[:, 2:3], lam_col[:, 3:4], MUL, after=[t2])
                        t = stt(s1, s2, st2[:, 3:4], s1, MUL, ADD, after=[t, t2])
                        p2.leave(pi, t)
                        t_p.append(t)
                    c0, n_q = tiles[0] * P, len(tiles) * P

                    def finish(o, t):
                        t_o = copy(act, o_sb[0:96, 0:n_q], o, after=[t, dve.last])
                        b = mean_square([o_sb[0:96, :]], 0, n_q, DF_V, sq, [t_o], rows=96)
                        t2 = rstd_of(rs[0:96, 0:n_q], *b, n_q, DF_V, rows=96)
                        t2 = stt(rs[0:96, 0:n_q], o_sb[0:96, 0:n_q], lam_col[0:96, 0:1], rs[0:96, 0:n_q], MUL, MUL,
                                 after=[t2])
                        m = mix[0:96, 3 + h, c0:c0 + n_q]
                        tt(dve, m, rs[0:96, 0:n_q], m, MUL, after=[t2])
                        return t_o
                    t = transposed_values([p1[:, n, k0:TA] for n in range(len(tiles))], 6 if local else 2, pt,
                                          lambda j: v[:, j, h * 96:(h + 1) * 96], 96, 0, 0 if local else 4,
                                          finish, t_p, pt_free)
                    pt_free, p_free = [t], [t]

        def conv_stage(l, total, area0, mix, h_ready):
            area = Area(area0)
            u = area.take(2, CONV_TOK)
            y = area.take(2, CONV_OUT)
            sg = area.take(2, TA)
            w_in = ins[f"w_in{l}"]
            t0 = memset(dve, u, 0.0)
            starts = {0: PAD, T: PAD + T + PAD}

            def consume(base):
                def go(m, c0, c1, b, t):
                    m += base
                    at = starts[c0]
                    if m < 2:
                        return copy(act, u[:, m, at:at + c1 - c0], b, after=[t, t0])
                    if m < 4:
                        t1 = fn(sg[:, m - 2, c0:c1], b, ACT.Sigmoid, after=[t])
                        tt(dve, u[:, m - 2, at:at + c1 - c0], u[:, m - 2, at:at + c1 - c0], sg[:, m - 2, c0:c1],
                           MUL, after=[t1])
                        return t1
                    return fn(mix[:, 3 + m, c0:c1], b, ACT.Silu, after=[t])
                return go
            project([w_in[16], w_in[17]], [P] * 3, total, consume(0), h_ready)
            project([w_in[18], w_in[19]], [P] * 3, total, consume(3), h_ready)
            n = T if total == T else CONV_OUT
            for m in range(2):
                t = ts(dve, y[:, m, 0:n], u[:, m, 0:n], col(f"conv_w{l}", m * TAPS), MUL,
                       col(f"conv_b{l}", m), ADD, after=[dve.last])
                for k in range(1, TAPS):
                    t = stt(y[:, m, 0:n], u[:, m, k:k + n], col(f"conv_w{l}", m * TAPS + k), y[:, m, 0:n], MUL, ADD,
                            after=[t])
            sq = Ring([area.take(T) for _ in range(2)])
            rs = area.take(T)
            for (c0, c1) in spans(total):
                w = c1 - c0
                at = 0 if c0 == 0 else T + PAD
                i, bank, free = banks.take()
                for m in range(2):
                    tm = mm(bank[:, 0:w], ones, y[:, m, at:at + w], m == 0, m == 1, after=[dve.last] + free)
                ts_ = []
                for m in range(2):
                    ts_.append(stt(y[:, m, at:at + w], bank[:, 0:w], -1.0 / CONV_W, y[:, m, at:at + w], MUL, ADD,
                                   after=[tm]))
                banks.leave(i, ts_[1])
                b = mean_square([y[:, m, at:at + w] for m in range(2)], 0, w, CONV_W, sq, ts_)
                t = rstd_of(rs[:, 0:w], *b, w, CONV_W, after=[dve.last])
                for m in range(2):
                    yy = y[:, m, at:at + w]
                    t1 = stt(yy, yy, col(f"ln_g{l}", m), rs[:, 0:w], MUL, MUL, after=[t])
                    t1 = fn(yy, yy, ACT.Silu, after=[t1], bias=col(f"ln_b{l}", m))
                    tt(dve, mix[:, 7 + m, c0:c1], yy, mix[:, 7 + m, c0:c1], MUL, after=[t1])

        def first_layer(l, total):
            nonlocal stage_ends
            fence()
            t_mod = modulation(l, total)
            stage_ends = fence()
            h_ready = norm(TA, lambda j, s: gs[:, j, s:s + 1], lambda j, s: mods[:, j, s:s + 1], after=[x_in] + t_mod)
            mix_area = Area()
            mix = mix_area.take(9, TA)
            stage_ends = fence()
            na_stage(l, total, mix_area.at, mix, h_ready)
            stage_ends = fence()
            diff_stage(l, total, mix_area.at, mix, h_ready)
            stage_ends = fence()
            conv_stage(l, total, mix_area.at, mix, h_ready)
            ends = fence()
            k_tiles = [mix[:, i, :] for i in range(3)] + [mix[0:96, 3 + i, :] for i in range(4)] + \
                      [mix[:, 7 + i, :] for i in range(2)]
            t_y = project_out(lambda m: [ins[f"w_out{l}"][m]], k_tiles, total, ends)
            fence()
            add_normed(total, lambda j, s: gp[:, j, s:s + 1], t_y)

        def half_gain(name):
            return ts(dve, half_g, col(name, 0, 8), 0.5, MUL, after=[pool.last, dve.last])

        def ffn(name):
            ends = fence()
            h_ready = norm(T, lambda j, s: col(name + "_pre", j))
            fence()
            area = Area()
            a = area.take(FT, T)
            sg = Ring([area.take(T) for _ in range(3)])
            w = ins[name + "_w_in"]
            for c in range(FT // 2):
                g_l, u_l = load(w[2 * c]), load(w[2 * c + 1])
                for m in range(2):
                    i1, bank1, free1 = banks.take()
                    i2, bank2, free2 = banks.take()
                    for (s, slot, tok), bank, free in ((g_l, bank1, free1), (u_l, bank2, free2)):
                        for k in range(DT):
                            t = mm(bank[:, :], slot[:, k * 256 + m * P:k * 256 + (m + 1) * P], h_sb[:, k, 0:T],
                                   k == 0, k == DT - 1, after=[tok] + free + h_ready)
                        if bank is bank1:
                            r, sg_t, sfree = sg.take()
                            t1 = fn(sg_t, bank1[:, :], ACT.Silu, after=[t] + sfree)
                            banks.leave(i1, t1)
                        else:
                            t2 = tt(dve, a[:, 2 * c + m, :], bank2[:, :], sg_t, MUL, after=[t, t1])
                            banks.leave(i2, t2)
                            sg.leave(r, t2)
                slots.leave(g_l[0], pe.last)
                slots.leave(u_l[0], pe.last)
            half_gain(name + "_post")
            w2 = ins[name + "_w_out"]
            t_y = project_out(lambda m: [w2[2 * m], w2[2 * m + 1]], [a[:, k, :] for k in range(FT)], T, [dve.last])
            fence()
            add_normed(T, lambda j, s: half_g[:, j:j + 1], t_y)

        def even_mixer():
            fence()
            h_ready = norm(T, lambda j, s: col("l0_mix_pre", j))
            fence()
            w = ins["l0_w_in"]
            area = Area()
            pa = area.take(14, T + 1)
            mixed = area.take(8, T)
            z = memset(pool, pa[:, :, 0:1], 0.0)
            at = area.at
            tmp = Ring([area.take(T) for _ in range(2)])

            def into_pa(base):
                def go(m, c0, c1, b, t):
                    i = base + m
                    t = copy(act, pa[:, i, 1:T + 1], b, after=[t])
                    r, d, free = tmp.take()
                    t1 = tt(pool, d, pa[:, i, 0:T], pa[:, i, 1:T + 1], SUB, after=[t, z] + free)
                    t2 = stt(pa[:, i, 1:T + 1], d, col("mu", i), pa[:, i, 1:T + 1], MUL, ADD, after=[t1])
                    tmp.leave(r, t2)
                    return t
                return go
            for c in range(7):
                project([w[c]], [P] * 2, T, into_pa(2 * c), h_ready)
            for c in range(7, 11):
                project([w[c]], [P] * 2, T, lambda m, c0, c1, b, t, c=c:
                        copy(act, mixed[:, 2 * (c - 7) + m, :], b, after=[t]), h_ready)
            t_pa = [act.last, dve.last, pool.last]

            area = Area(at)
            xc, a_t, u_t, tm = area.take(T), area.take(T), area.take(T), area.take(T)
            gw = area.take(2, 4 * HD)
            t_gw = sp.dma(gw.rearrange("p a b -> p (a b)"), ins["gate_w"], gate_q, after=t_pa)
            lam = col("lam", 0, 4)
            c8 = small[:, C8:C8 + 16]
            t = fn(c8[:, 0:4], lam, ACT.Abs)
            t = fn(c8[:, 0:4], c8[:, 0:4], ACT.Exp, after=[t], scale=-1.0)
            t = fn(c8[:, 0:4], c8[:, 0:4], ACT.Ln, after=[t], bias=ones[:, 0:1])
            t1 = ts(dve, c8[:, 4:8], lam, -1.0, MUL, 0.0, MAX)
            t1 = tt(dve, c8[:, 8:12], c8[:, 0:4], c8[:, 4:8], ADD, after=[t, t1])
            t_c8 = ts(dve, c8[:, 12:16], c8[:, 8:12], -8.0, MUL, after=[t1])
            for p in range(4):
                xb = mixed[:, p, :]
                t = ts(dve, xc, xb, col("rconv_w", 4 * p + 3), MUL, col("rconv_b", p), ADD,
                       after=t_pa + [act.last, dve.last, pe.last])
                for k in range(3):
                    s = 3 - k
                    t = stt(xc[:, s:T], xb[:, 0:T - s], col("rconv_w", 4 * p + k), xc[:, s:T], MUL, ADD, after=[t])
                outs = []
                for g, bias in ((0, "ga_b"), (1, "gx_b")):
                    i, bank, free = banks.take()
                    for b0 in (0, 64):
                        tg = mm(bank[b0:b0 + 64, :], gw[b0:b0 + 64, g, p * HD:(p + 1) * HD], xc[b0:b0 + 64], True, True,
                                after=[t, t_gw] + free)
                    dst = a_t if g == 0 else u_t
                    tg = fn(dst, bank[:, :], ACT.Sigmoid, after=[tg, dve.last], bias=col(bias, p))
                    banks.leave(i, tg)
                    outs.append(tg)
                t1 = ts(dve, a_t, a_t, c8[:, 12 + p:13 + p], MUL, after=outs + [t_c8])
                t2 = fn(tm, a_t, ACT.Tanh, after=[t1], scale=-1.0)
                t3 = fn(a_t, a_t, ACT.Exp, after=[t2])
                t4 = tt(dve, xb, a_t, a_t, MUL, after=[t3])
                t4 = stt(tm, xb, 1.0, tm, ADD, MUL, after=[t4, t2])
                t4 = fn(tm, tm, ACT.Sqrt, after=[t4])
                t5 = tt(dve, u_t, u_t, xc, MUL, after=[outs[1]])
                t5 = tt(dve, u_t, u_t, tm, MUL, after=[t4, t5])
                t5 = dve.do(lambda g_, o=xb, a=a_t, b=u_t: g_.tensor_tensor_scan(o, a, b, 0.0, MUL, ADD),
                            [t5, t3])
                gb = mixed[:, 4 + p, :]
                t6 = fn(tm, gb, ACT.Square, after=[t5])
                t6 = ts(dve, tm, tm, 0.044715, MUL, 1.0, ADD, after=[t6])
                t6 = tt(dve, tm, tm, gb, MUL, after=[t6])
                t6 = fn(tm, tm, ACT.Tanh, after=[t6], scale=math.sqrt(2.0 / math.pi))
                t6 = stt(tm, tm, 1.0, gb, ADD, MUL, after=[t6])
                t6 = stt(gb, tm, 0.5, xb, MUL, MUL, after=[t6])

            ends = fence()
            area = Area(at)
            ar = h_sb[:, :, 0:T].rearrange("p (i q) n -> p i q n", i=2)

            def v_tok(c, h):
                o = T + (h % 4) * HD
                return h_sb[:, 2 * c + h // 4, o:o + HD]
            s_l, lora, tok_l = load(ins["lora"])
            w2, a2, g2 = lora[0:64, 0:512], lora[64:128, 0:512], lora[:, 512:1024]
            glo = area.take(T)
            tot = area.take(4, 2 * NCH)
            b_t, k_t = area.take(4, T), area.take(4, T)
            chunk_at = area.at
            lo = area.take(T)
            sc = [area.take(T) for _ in range(4)]
            pb = area.take(NCH, CH + 1)
            ones_row = area.take(CH)
            t = fn(lo[0:64], pa[0:64, 12, 1:T + 1], ACT.Tanh)
            t = copy(act, lo[64:128], pa[64:128, 12, 1:T + 1])
            t = fn(glo, pa[:, 13, 1:T + 1], ACT.Sigmoid)
            t_one = memset(pool, ones_row, 1.0)
            t_pb = memset(pool, pb[:, :, 0:1], 1.0)
            ready = [t, t_one, t_pb]

            def by_chunk(v):
                return v.rearrange("p (c n) -> p c n", c=NCH)
            t_first = None
            for p in range(4):
                r, k, v = (pa[:, 4 * q + p, 1:T + 1] for q in range(3))
                wt, at_, kk, km = sc
                i, bank, free = banks.take()
                tm_ = mm(bank[:, :], w2[:, p * P:(p + 1) * P], lo[0:64], True, True, after=free + [tok_l] + ready)
                t1 = fn(wt, bank[:, :], ACT.Sigmoid, after=[tm_, dve.last, pool.last], bias=col("w0", p))
                banks.leave(i, t1)
                i, bank, free = banks.take()
                tm_ = mm(bank[:, :], a2[:, p * P:(p + 1) * P], lo[64:128], True, True, after=free)
                t2 = fn(at_, bank[:, :], ACT.Sigmoid, after=[tm_], bias=col("a0", p))
                banks.leave(i, t2)
                t1 = fn(wt, wt, ACT.Exp, after=[t1], scale=-math.exp(-0.5))
                t3 = ts(dve, kk, k, col("k_k", p), MUL, after=[t1, pe.last])
                t4 = fn(km, kk, ACT.Square, after=[t3])
                i, bank, free = banks.take()
                t4 = mm(bank[:, :], head_ones, km, True, True, after=free + [t4])
                t4 = fn(km, bank[:, :], ACT.Sqrt, after=[t4])
                banks.leave(i, t4)
                t4 = ts(dve, km, km, 1e-12, MAX, after=[t4])
                t4 = recip(km, km, after=[t4])
                t4 = tt(dve, kk, kk, km, MUL, after=[t4])
                for c in range(NCH):
                    t5 = dve.do(lambda g, c=c: g.tensor_tensor_scan(pb[:, c, 1:CH + 1], wt[:, c * CH:(c + 1) * CH],
                                                                    ones_row, 1.0, MUL, MUL),
                                [t1, t_one, t_pb] + ([t_first] if t_first else []))
                t5 = copy(dve, tot[:, p, 0:NCH], pb[:, :, CH // 2], after=[t5])
                t5 = recip(tot[:, p, NCH:2 * NCH], tot[:, p, 0:NCH], after=[t5])
                for c in range(NCH):
                    t6 = ts(dve, pb[:, c, :], pb[:, c, :], tot[:, p, NCH + c:NCH + c + 1], MUL, after=[t5])
                t7 = copy(dve, tot[:, p, NCH:2 * NCH], pb[:, :, CH], after=[t6])
                t8 = stt(by_chunk(ar[:, 0, p, :]), by_chunk(kk), -1.0, pb[:, :, 0:CH], MUL, MUL, after=[t4, t7])
                t9 = tt(dve, by_chunk(ar[:, 1, p, :]), by_chunk(r), pb[:, :, 1:CH + 1], MUL, after=[t7])
                t10 = recip(pb[:, :, 1:CH + 1], pb[:, :, 1:CH + 1], after=[t9, t8])
                t11 = tt(dve, kk, kk, at_, MUL, after=[t8, t2])
                t12 = tt(dve, by_chunk(b_t[:, p, :]), by_chunk(kk), pb[:, :, 1:CH + 1], MUL, after=[t10, t11])
                t13 = ts(dve, at_, at_, -1.0, ADD, col("k_a", p), MUL, after=[t11])
                t13 = stt(k, at_, 1.0, k, ADD, MUL, after=[t13, t3])
                t14 = tt(dve, by_chunk(k_t[:, p, :]), by_chunk(k), pb[:, :, 1:CH + 1], MUL, after=[t10, t13])
                t_first = memset(dve, pb[:, :, 0:1], 1.0, after=[t14])
                t15 = stt(r, r, col("r_k", p), k, MUL, MUL, after=[t13, t9])
                i, bank, free = banks.take()
                t15 = mm(bank[:, :], head_ones, r, True, True, after=free + [t15])
                t15 = tt(dve, r, bank[:, :], v, MUL, after=[t15])
                banks.leave(i, t15)
            ends = fence()
            area = Area(chunk_at)
            x_m, xt_m, m_ab_t, m_ak_t, m_rb_t, m_rk_t, t1_m = (area.take(8, P) for _ in range(7))
            k_area = pa[:, 4:8, 1:T + 1]
            b_tok, k_tok = k_area[:, 0, :], k_area[:, 1, :]
            sa, rhs = k_area[:, 2, :], k_area[:, 3, :]
            m_off = Ring([area.take(4, P) for _ in range(2)])
            state, state_mid = area.take(4, HD), area.take(4, HD)
            level = [area.take(P) for _ in range(0)]
            upper = C("upper").rearrange("p (a b) -> p a b", a=2)
            lower = C("lower")
            s_v, levels, tok_v = load(ins["levels"])
            for e in (dve, pool):
                e.wait([tok_v])
            lv = lambda n, tr: levels[:, 0:14 * P].rearrange("p (n i b) -> p n i b", n=7, i=2)[:, n, tr, :]
            t_s = memset(dve, state, 0.0)

            def slot_of(h):
                return 4 * (h % 2) + h // 2

            def rep(m, n):
                return m.rearrange("p (a b) -> p a b", a=1).broadcast_to((P, n, P))

            for c in range(NCH):
                cs = slice(c * CH, (c + 1) * CH)
                gate_c = [act.last, dve.last, pool.last, pe.last]
                for e in (act, dve, pool):
                    e.wait(gate_c)
                for src, dst in ((lambda p: pa[:, 8 + p, 1 + c * CH:1 + (c + 1) * CH], None),
                                 (lambda p: b_t[:, p, cs], b_tok), (lambda p: k_t[:, p, cs], k_tok)):
                    i, bank, free = banks.take()
                    for p in range(4):
                        t = transpose(bank[:, p * P:(p + 1) * P], src(p), after=free + ends, signal=(p == 3))
                    if dst is None:
                        for half in range(2):
                            t2 = copy(act, h_sb[:, 2 * c + half, T:TA], bank[:, 256 * half:256 * half + 256], after=[t])
                    else:
                        t2 = copy(act, dst, bank[:, :], after=[t])
                    banks.leave(i, t2)
                for half in range(2):
                    for left, m1, m2 in ((b_t, m_ab_t, m_rb_t), (k_t, m_ak_t, m_rk_t)):
                        for odd in range(2):
                            i, bank, free = banks.take()
                            b0 = 64 * odd
                            for n in range(2):
                                pair = 2 * half + n
                                t = mm(bank[:, n * 256:(n + 1) * 256].rearrange("p (a b) -> p a b", a=2),
                                       left[b0:b0 + 64, pair, cs], ar[b0:b0 + 64, :, pair, cs], True, True,
                                       after=free + ends)
                            v4 = bank[:, :].rearrange("p (n a b) -> p n a b", n=2, a=2)
                            at4 = 4 * odd + 2 * half
                            for a_, m in ((0, m1), (1, m2)):
                                t2 = tt(dve, m[:, at4:at4 + 2, :], v4[:, :, a_, :], rep(upper[:, a_, :], 2), MUL,
                                        after=[t])
                            banks.leave(i, t2)
                for g in range(2):
                    i, bank, free = banks.take()
                    for n in range(4):
                        b0 = 64 * g
                        t = mm(bank[:, n * P:(n + 1) * P], ar[b0:b0 + 64, 0, n, cs], b_t[b0:b0 + 64, n, cs],
                               True, True, after=free)
                    xs, xts = x_m[:, 4 * g:4 * g + 4, :], xt_m[:, 4 * g:4 * g + 4, :]
                    t = tt(dve, xs, bank[:, :].rearrange("p (n b) -> p n b", n=4), rep(lv(0, 0), 4), MUL, after=[t])
                    banks.leave(i, t)
                    t = tt(dve, xs, xs, rep(ident, 4), ADD, after=[t])
                    t = tt(dve, xts, m_ab_t[:, 4 * g:4 * g + 4, :], rep(lv(0, 1), 4), MUL, after=[dve.last])
                    t_x = tt(dve, xts, xts, rep(ident, 4), ADD, after=[t])
                t_xs = [t_x, t_x]
                for n_l in range(1, 7):
                    for g in range(2):
                        gs4 = slice(4 * g, 4 * g + 4)
                        r_, off, ofree = m_off.take()
                        t_off = tt(pool, off, m_ab_t[:, gs4, :], rep(lv(n_l, 1), 4), MUL, after=[t_x] + ofree)
                        i, bank, free = banks.take()
                        for n in range(4):
                            t = mm(bank[:, n * P:(n + 1) * P], off[:, n, :], x_m[:, 4 * g + n, :], True, True,
                                   after=free + [t_off, t_xs[g]])
                        m_off.leave(r_, pe.last)
                        tc1 = copy(act, t1_m[:, gs4, :], bank[:, :].rearrange("p (n b) -> p n b", n=4),
                                   after=[t])
                        banks.leave(i, tc1)
                        outs = []
                        i2, bank2, free2 = banks.take()
                        for n in range(4):
                            t = mm(bank2[:, n * P:(n + 1) * P], t1_m[:, 4 * g + n, :], xt_m[:, 4 * g + n, :], True, True,
                                   after=free2 + [tc1])
                        if n_l < 6:
                            i3, bank3, free3 = banks.take()
                            for n in range(4):
                                t3_ = mm(bank3[:, n * P:(n + 1) * P], xt_m[:, 4 * g + n, :], t1_m[:, 4 * g + n, :],
                                         True, True, after=free3)
                            t4_ = tt(dve, x_m[:, gs4, :], x_m[:, gs4, :],
                                     bank3[:, :].rearrange("p (n b) -> p n b", n=4), ADD, after=[t3_, dve.last])
                            banks.leave(i3, t4_)
                        t_xs[g] = tt(dve, xt_m[:, gs4, :], xt_m[:, gs4, :],
                                     bank2[:, :].rearrange("p (n b) -> p n b", n=4), ADD, after=[pe.last])
                        banks.leave(i2, t_xs[g])
                for p in range(4):
                    t_sm = ts(dve, state_mid[:, p, :], state[:, p, :], tot[:, p, c:c + 1], MUL, after=[t_s])
                for odd in range(2):
                    i, bank, free = banks.take()
                    b0 = 64 * odd
                    for n in range(4):
                        o = bank[:, n * HD:(n + 1) * HD]
                        mm(o, ar[b0:b0 + 64, 0, n, cs], state_mid[b0:b0 + 64, n, :], True, False,
                           after=free + [t_sm, act.last])
                        t = mm(o, m_ak_t[:, 4 * odd + n, :], v_tok(c, 2 * n + odd), False, True)
                    t = copy(act, rhs[:, 256 * odd:256 * odd + 256], bank[:, 0:256], after=[t])
                    banks.leave(i, t)
                i, bank, free = banks.take()
                for h in range(8):
                    t2 = mm(bank[:, h * HD:(h + 1) * HD], xt_m[:, h, :], rhs[:, h * HD:(h + 1) * HD], True, True,
                            after=free + [t] + t_xs)
                t_sa = copy(act, sa, bank[:, :], after=[t2])
                banks.leave(i, t_sa)
                i, bank, free = banks.take()
                for h in range(8):
                    b0 = 64 * (h % 2)
                    o = bank[b0:b0 + 64, (h // 2) * P:(h // 2 + 1) * P]
                    mm(o, state_mid[b0:b0 + 64, h // 2, :], ar[b0:b0 + 64, 1, h // 2, cs], True, False,
                       after=free + [t_sa])
                    m_h = slot_of(h)
                    mm(o, sa[:, m_h * HD:(m_h + 1) * HD], m_rb_t[:, m_h, :], False, False)
                    t_y = mm(o, v_tok(c, h), m_rk_t[:, m_h, :], False, True)
                i2, bank2, free2 = banks.take()
                for h in range(8):
                    b0 = 64 * (h % 2)
                    o = bank2[b0:b0 + 64, (h // 2) * HD:(h // 2 + 1) * HD]
                    m_h = slot_of(h)
                    mm(o, b_tok[:, h * HD:(h + 1) * HD], sa[:, m_h * HD:(m_h + 1) * HD], True, False, after=free2)
                    t_n = mm(o, k_tok[:, h * HD:(h + 1) * HD], v_tok(c, h), False, True)
                t_s = tt(dve, state, state_mid, bank2[:, 0:256].rearrange("p (a b) -> p a b", a=4), ADD, after=[t_n])
                banks.leave(i2, t_s)
                for p in range(4):
                    t_s2 = ts(dve, state[:, p, :], state[:, p, :], tot[:, p, NCH + c:NCH + c + 1], MUL, after=[t_s])
                t_s = t_s2
                y_c, sq_c = x_m[:, 0:4, :], x_m[:, 4:8, :]
                t = copy(act, y_c, bank[:, :].rearrange("p (a b) -> p a b", a=4), after=[t_y, dve.last])
                banks.leave(i, t)
                i, bank, free = banks.take()
                flat = lambda v: v.rearrange("p a b -> p (a b)")
                t = mm(bank[:, :], head_ones, flat(y_c), True, True, after=free + [t])
                t = stt(flat(y_c), bank[:, :], -1.0 / HD, flat(y_c), MUL, ADD, after=[t])
                banks.leave(i, t)
                t2 = fn(flat(sq_c), flat(y_c), ACT.Square, after=[t])
                i, bank, free = banks.take()
                t2 = mm(bank[:, :], head_ones, flat(sq_c), True, True, after=free + [t2])
                t2 = rstd_of(flat(sq_c), i, bank, t2, 512, HD, eps=1)
                tt(dve, mixed[:, 0:4, cs], y_c, sq_c, MUL, after=[t2])
            for p in range(4):
                m = mixed[:, p, :]
                t = ts(dve, m, m, col("lnx_g", p), MUL, col("lnx_b", p), ADD, after=[dve.last])
                t = tt(dve, m, m, pa[:, p, 1:T + 1], ADD, after=[t])
                i, bank, free = banks.take()
                t2 = mm(bank[:, :], g2[:, p * P:(p + 1) * P], glo, True, True, after=free)
                t = tt(dve, m, bank[:, :], m, MUL, after=[t, t2])
                banks.leave(i, t)
            slots.leave(s_l, pe.last)
            slots.leave(s_v, dve.last, pool.last)
            ends = fence()
            t_y = project_out(lambda m: [ins["l0_w_out"][m]], [mixed[:, k, :] for k in range(8)], T, ends)
            fence()
            add_normed(T, lambda j, s: col("l0_mix_post", j), t_y)

        def stick_breaking():
            fence()
            h_ready = norm(T, lambda j, s: col("l1_mix_pre", j))
            fence()
            area = Area()
            qk, v, o_t = area.take(16, T), area.take(4, D), area.take(8, T)
            w = ins["w_qkv"]
            for c in range(8):
                scale = HD ** -0.5 if c < 4 else 1.0
                project([w[c]], [P] * 2, T, lambda m, c0, c1, b, t, c=c, scale=scale:
                        ts(dve, qk[:, 2 * c + m, :], b, scale, MUL, after=[t]), h_ready)
            for c in range(8, 12):
                project_tokens([w[c]], 256, T, lambda m, b, t, c=c:
                               copy(act, v[:, m, (c - 8) * 256:(c - 7) * 256], b, after=[t]), h_ready)
            ready = [act.last, dve.last]
            e_r = Ring([area.take(T) for _ in range(3)])
            sp_r = Ring([area.take(T) for _ in range(3)])
            at_r = Ring([area.take(T) for _ in range(3)])
            sums = Ring([area.take(T) for _ in range(2)])
            suffix, minus = C("suffix"), C("minus")

            def strictly_before(v, after):
                return pool.do(lambda g: g.affine_select(out=v, in_=v, compare_op=ALU.is_gt, fill=0.0, base=0,
                                                         pattern=[[1, P]], channel_multiplier=-1), after)
            for h in range(SB_HEADS):
                b0, tile = 64 * (h % 2), h // 2
                i_s, acc, afree = sums.take()
                t_acc = memset(pool, acc, 0.0, after=afree)
                i_o, bank_o, free_o = banks.take()
                for j in range(3, -1, -1):
                    q0, n = j * P, T - j * P
                    i, bank, free = banks.take()
                    z = bank[:, 0:n]
                    t = mm(z, qk[b0:b0 + 64, 8 + tile, q0:q0 + P], qk[b0:b0 + 64, tile, q0:T], True, True,
                           after=free + ready)
                    ie, e_t, efree = e_r.take()
                    isp, sp_t, spfree = sp_r.take()
                    t = fn(e_t[:, 0:n], z, ACT.Abs, after=[t] + efree)
                    t = fn(e_t[:, 0:n], e_t[:, 0:n], ACT.Exp, after=[t], scale=-1.0)
                    t = fn(e_t[:, 0:n], e_t[:, 0:n], ACT.Ln, after=[t], bias=ones[:, 0:1])
                    t = stt(sp_t[:, 0:n], z, 0.0, e_t[:, 0:n], MAX, ADD, after=[t] + spfree)
                    e_r.leave(ie, t)
                    t_sp = strictly_before(sp_t[:, 0:P], [t])
                    t = mm(z, suffix, sp_t[:, 0:n], False, j == 3, after=[t_sp], signal=True)
                    if j < 3:
                        t = mm(z[:, P:n], minus, acc[:, q0 + P:T], False, True, after=[t_acc])
                    ia, at_t, atfree = at_r.take()
                    t_acc = tt(pool, acc[:, q0:T], acc[:, q0:T], sp_t[:, 0:n], ADD, after=[t, t_acc, t_sp])
                    sp_r.leave(isp, t_acc, t)
                    t = fn(at_t[:, 0:n], z, ACT.Exp, after=[t] + atfree)
                    banks.leave(i, t)
                    t = strictly_before(at_t[:, 0:P], [t])
                    t = mm(bank_o[b0:b0 + 64, q0:T], v[:, j, h * HD:(h + 1) * HD], at_t[:, 0:n], j == 3, j == 0,
                           after=[t] + free_o, signal=True)
                    at_r.leave(ia, t)
                sums.leave(i_s, t, t_acc)
                t = copy(dve, o_t[b0:b0 + 64, tile, :], bank_o[b0:b0 + 64, :], after=[t])
                banks.leave(i_o, t)
            t_y = project_out(lambda m: [ins["l1_w_out"][m]], [o_t[:, k, :] for k in range(8)], T, [dve.last])
            fence()
            add_normed(T, lambda j, s: col("l1_mix_post", j), t_y)

        stage_ends = []
        plan = [("L0", lambda: first_layer(0, TA)), ("L1", lambda: first_layer(1, T)),
                ("F1", lambda: ffn("l0_ffn1")), ("M0", even_mixer), ("F2", lambda: ffn("l0_ffn2")),
                ("F3", lambda: ffn("l1_ffn1")), ("M1", stick_breaking), ("F4", lambda: ffn("l1_ffn2"))]
        for name, go in plan:
            go()
            if upto == name:
                break
        toks = [e.last for e in (pe, dve, act, pool)]
        done = sp.dma(out_dram, x_sb[:, :, 0:T], out_q, after=toks)
        sp.wait([done])

        with nc.Block() as block:
            @block.sync
            def _(e):
                sp.run(e)

            @block.tensor
            def _(e):
                pe.run(e)

            @block.vector
            def _(e):
                dve.run(e)

            @block.scalar
            def _(e):
                act.run(e)

            @block.gpsimd
            def _(e):
                pool.run(e)


def constants():
    f = np.float32
    out = np.zeros((P, N_CONST), f)

    def put(name, v):
        at, n = CONSTS[name]
        out[:v.shape[0], at:at + n] = v
    put("ident", np.eye(P, dtype=f))
    put("ones", np.ones((P, P), f))
    h = np.arange(P) // HD
    put("head_ones", (h[:, None] == h[None, :]).astype(f))
    rot = np.zeros((96, 96), f)
    half = 24
    for b in range(0, 96, half):
        for i in range(12):
            rot[b + 12 + i, b + i] = -1.0
            rot[b + i, b + 12 + i] = 1.0
    put("rot", rot)
    put("half", (np.arange(96) >= DF_QK).astype(f)[:, None])
    put("eps", np.tile(np.array([[EPS, GN_EPS]], f), (P, 1)))
    t = np.arange(T)
    inv = (f(10000.0) ** (-np.arange(0, 24, 2, dtype=f) / f(24))).astype(f)
    cs, sn = np.zeros((96, T), f), np.zeros((96, T), f)
    for q in range(2):
        for part, pos in ((0, t // GRID_W), (1, t % GRID_W)):
            ang = (pos.astype(f)[None, :] * inv[:, None]).astype(f)
            for hh in range(2):
                o = q * 48 + part * 24 + hh * 12
                cs[o:o + 12], sn[o:o + 12] = np.cos(ang), np.sin(ang)
    put("cos", cs)
    put("sin", sn)
    qc = np.arange(P) % GRID_W
    st = np.clip(qc - WIN_W // 2, 0, GRID_W - WIN_W)
    kc = np.arange(GRID_W)
    ok = (kc[None, :] >= st[:, None]) & (kc[None, :] < st[:, None] + WIN_W)
    put("na_mask", np.where(ok, f(0), f(NEG)).astype(f))
    i, j = np.arange(P)[:, None], np.arange(P)[None, :]
    put("upper", np.concatenate([(i < j), (i <= j)], 1).astype(f))
    put("lower", (j < i).astype(f))
    put("suffix", -(i >= j).astype(f))
    put("turn", np.kron(np.eye(2), np.eye(GRID_W)[::-1]).astype(f))
    put("minus", -np.ones((P, P), f))
    return out


def level_mask(n):
    i, j = np.arange(P)[:, None] // n, np.arange(P)[None, :] // n
    m = ((i % 2 == 1) & (j == i - 1)).astype(np.float32)
    return m, m.T


def lay_out(inp):
    f = np.float32
    I = {k: np.asarray(v) for k, v in inp.items()}
    arr = {}
    xt = np.concatenate([I["x"][0], I["ctx"][0]], 0).T
    arr["xt"] = xt.reshape(DT, P, TA).transpose(1, 0, 2)
    par = np.zeros((P, N_COLUMNS), f)

    def put(name, v, rows=P):
        at, n = COLUMNS[name]
        par[:v.shape[0], at:at + n] = v

    def cols(v):
        return v.reshape(-1, P).T
    for l in range(DEPTH):
        put(f"b_mod{l}", cols(I["b_mod"][l]))
        put(f"g_pre{l}", cols(I["g_pre"][l]))
        put(f"g_post{l}", cols(I["g_post"][l]))
        put(f"subln{l}", I["diff_subln_g"][l][:, None])
        put(f"conv_w{l}", I["conv_w"][l].reshape(TAPS, 2, P).transpose(2, 1, 0).reshape(P, 2 * TAPS))
        put(f"conv_b{l}", cols(I["conv_b"][l]))
        put(f"ln_g{l}", cols(I["conv_ln_g"][l]))
        put(f"ln_b{l}", cols(I["conv_ln_b"][l]))
        put(f"lq{l}", np.stack([I["diff_lq1"][l], I["diff_lq2"][l]], 1))
        put(f"lk{l}", np.stack([I["diff_lk1"][l], I["diff_lk2"][l]], 1))
        arr[f"w_mod{l}"] = by_columns(I["w_mod"][l], 256)
        arr[f"w_in{l}"] = by_columns(I["w_in"][l], GROUP, 2)
        wo = I["w_out"][l]
        padded = np.zeros((9, P, D), f)
        padded[0:3] = wo[0:384].reshape(3, P, D)
        padded[3:7, 0:96] = wo[384:768].reshape(4, 96, D)
        padded[7:9] = wo[768:1024].reshape(2, P, D)
        arr[f"w_out{l}"] = padded.reshape(9, P, 8, P).transpose(2, 1, 0, 3).reshape(8, P, 9 * P)
        rp = np.zeros((NA_HEADS * 15, P), f)
        rp[:, 48:79] = I["na_rpb"][l].reshape(NA_HEADS * 15, 31)
        arr[f"rpb{l}"] = rp
    put("cond", np.stack([cols(I["c"][0]), cols(I["c_ctx"])], 2).reshape(P, 16))
    for n in ("l0_ffn1", "l0_ffn2", "l1_ffn1", "l1_ffn2", "l0_mix", "l1_mix"):
        put(n + "_pre", cols(I[n + "_pre_g_2"]))
        put(n + "_post", cols(I[n + "_post_g_2"]))
    for n in ("l0_ffn1", "l0_ffn2", "l1_ffn1", "l1_ffn2"):
        w = I[n + "_w_in_2"]
        g, u = by_columns(w[:, :D_FF], 256), by_columns(w[:, D_FF:], 256)
        arr[n + "_w_in"] = np.stack([g, u], 1).reshape(2 * g.shape[0], P, -1)
        w = I[n + "_w_out_2"]
        arr[n + "_w_out"] = w.reshape(2, 11, P, 8, P).transpose(3, 0, 2, 1, 4).reshape(16, P, 11 * P)
    put("mu", cols(I["l0_mu_2"]))
    for a, b in (("w0", "l0_w0_2"), ("a0", "l0_a0_2"), ("k_k", "l0_k_k_2"), ("k_a", "l0_k_a_2"),
                 ("r_k", "l0_r_k_2"), ("lnx_g", "l0_lnx_g_2"), ("lnx_b", "l0_lnx_b_2"), ("rconv_b", "l0_conv_b_2"),
                 ("ga_b", "l0_gate_a_b_2"), ("gx_b", "l0_gate_x_b_2"), ("lam", "l0_lambda_2")):
        put(a, cols(I[b]))
    put("rconv_w", I["l0_conv_w_2"].reshape(4, 4, P).transpose(2, 1, 0).reshape(P, 16))
    arr["l0_w_in"] = by_columns(I["l0_w_in_2"], 256)
    arr["l0_w_out"] = by_columns(I["l0_w_out_2"], P)
    arr["lora"] = np.concatenate([np.concatenate([I["l0_w2_2"], I["l0_a2_2"]], 0), I["l0_g2_2"]], 1)
    gates = [I[n].reshape(4, 2, HD, HD).transpose(1, 2, 0, 3).reshape(P, 4 * HD)
             for n in ("l0_gate_a_w_2", "l0_gate_x_w_2")]
    arr["gate_w"] = np.concatenate(gates, 1)
    arr["w_qkv"] = by_columns(I["l1_w_qkv_2"], 256)
    arr["l1_w_out"] = by_columns(I["l1_w_out_2"], P)
    arr["par"] = par
    arr["const"] = constants()
    arr["levels"] = np.concatenate([m for n in LEVELS for m in level_mask(n)], 1)
    return {k: np.ascontiguousarray(v) for k, v in arr.items()}


def by_columns(w, width, parts=1):
    k, n = w.shape
    v = w.reshape(parts, k // P // parts, P, n // width, width).transpose(3, 0, 2, 1, 4)
    return v.reshape(n // width * parts, P, -1)


def kernel(**inputs):
    import concourse.bacc as bacc
    from concourse.bass_utils import run_bass_kernel_spmd

    arrays = lay_out(inputs)
    nc = bacc.Bacc("TRN2", target_bir_lowering=False, num_devices=1)
    ins = {n: nc.dram_tensor(f"in_{n}", a.shape, mybir.dt.float32, kind="ExternalInput").ap()
           for n, a in arrays.items()}
    out = nc.dram_tensor("out", (P, DT, T), mybir.dt.float32, kind="ExternalOutput").ap()
    build(nc, ins, out, UPTO)
    r = run_bass_kernel_spmd(nc, [{f"in_{n}": a for n, a in arrays.items()}], core_ids=[0])
    y = r.results[0]["out"]
    return np.ascontiguousarray(y.transpose(1, 0, 2).reshape(D, T).T)[None]


UPTO = None
```

```python
import math
from contextlib import ExitStack

import numpy as np
import concourse.bass as bass
from concourse import mybir

P = 128
D = 1024
DT = D // P
T = 512
TC = 256
TA = T + TC
DEPTH = 2
GRID_W = 64
NA_HEADS, NA_DH = 6, 64
NA_W = NA_HEADS * NA_DH
WIN_H, WIN_W = 8, 16
DF_HEADS, DF_QK = 4, 48
DF_V = 2 * DF_QK
GROUP = 384
IN_COLS = 3840
CONV_W, TAPS = 256, 31
PAD = TAPS // 2
CONV_TOK = PAD + T + PAD + TC + PAD
CONV_OUT = T + PAD + TC
BIAS_ROWS = 14
D_FF = 2816
FT = D_FF // P
A_W = 512
RW_HEADS = 8
HD = 64
CH = 128
NCH = T // CH
LEVELS = [1, 2, 4, 8, 16, 32, 64]
SB_HEADS = 16
EPS = 1e-6
GN_EPS = 64e-5
NEG = -1e30
SLOT = 1024
N_RAW, N_SPLIT = 3, 3
AHEAD = 2
WORK = 22300
W_OUT_K = (5, 4)
FFN_K = (6, 5)

def column_table():
    names = []
    for l in range(DEPTH):
        names += [(f"b_mod{l}", 24), (f"g_pre{l}", 8), (f"g_post{l}", 8), (f"subln{l}", 1),
                  (f"conv_w{l}", 2 * TAPS), (f"conv_b{l}", 2), (f"ln_g{l}", 2), (f"ln_b{l}", 2),
                  (f"lq{l}", 2), (f"lk{l}", 2)]
    names += [("cond", 16)]
    for f in ("l0_ffn1", "l0_ffn2", "l1_ffn1", "l1_ffn2", "l0_mix", "l1_mix"):
        names += [(f + "_pre", 8), (f + "_post", 8)]
    names += [("mu", 14), ("w0", 4), ("a0", 4), ("k_k", 4), ("k_a", 4), ("r_k", 4), ("lnx_g", 4),
              ("lnx_b", 4), ("rconv_w", 16), ("rconv_b", 4), ("ga_b", 4), ("gx_b", 4), ("lam", 4)]
    at, out = 0, {}
    for name, n in names:
        out[name] = (at, n)
        at += n
    return out, at


COLUMNS, N_COLUMNS = column_table()

CONSTS, N_CONST = {}, 0
for _name, _n in (("ident", 128), ("ones", 128), ("head_ones", 128), ("rot", 96), ("half", 1), ("eps", 2),
                  ("cos", 512), ("sin", 512), ("na_mask", 64), ("upper", 256), ("lower", 128),
                  ("suffix", 128), ("minus", 128), ("turn", 128)):
    CONSTS[_name] = (N_CONST, _n)
    N_CONST += _n


def weight_order():
    def groups(l, gs, ctx):
        for g in gs:
            for m in range(4 if g in (2, 6, 7) else 3):
                yield (f"w_in{l}", IN_PIECE[g][m], True)
    for l in range(DEPTH):
        if l == 0:
            for c in range(24):
                yield (f"w_mod{l}", c, False)
        yield from groups(l, NA_GROUPS, l == 0)
        yield from groups(l, LATE_GROUPS, l == 0)
        if l == 0:
            for c in range(24):
                yield ("w_mod1", c, False)
        for c in range(16):
            yield (f"w_out{l}", c, True)
    for name in ("l0_ffn1", "mix0", "l0_ffn2", "l1_ffn1", "mix1", "l1_ffn2"):
        if name == "mix0":
            for c in range(22):
                yield ("l0_w_in", c, True)
            for c in range(8):
                yield ("l0_w_out", c, True)
        elif name == "mix1":
            for c in range(24):
                yield ("w_qkv", c, True)
            for c in range(8):
                yield ("l1_w_out", c, True)
        else:
            for half in range(2):
                for c in range(FT):
                    yield (name + "_w_in", half * FT + c, True)
                for c in range(16):
                    yield (name + f"_w_out{half}", c, True)


IN_PIECE, _n = {}, 0
for _g in range(10):
    IN_PIECE[_g] = list(range(_n, _n + (4 if _g in (2, 6, 7) else 3)))
    _n += len(IN_PIECE[_g])
NA_GROUPS = (0, 1, 5, 4)
LATE_GROUPS = (8, 9, 2, 3, 7, 6)


class Engine:

    def __init__(self, sem):
        self.sem, self.count, self.items, self.reached = sem, 0, [], {}

    def wait(self, after):
        for tok in after:
            if tok is None:
                continue
            sem, value = tok
            if self.reached.get(id(sem), 0) < value:
                self.reached[id(sem)] = value
                self.items.append(lambda e, s=sem, v=value: e.wait_ge(s, v))

    def do(self, fn, after=(), signal=True):
        self.wait(after)
        if signal:
            self.count += 1
            self.items.append(lambda e: fn(e).then_inc(self.sem, 1))
            return (self.sem, self.count)
        self.items.append(fn)
        return None

    @property
    def last(self):
        return (self.sem, self.count) if self.count else None

    def dma(self, out, in_, queue, after=()):
        self.wait(after)
        queue[1] += 16
        s = queue[0]
        self.items.append(lambda e: e.dma_start(out, in_).then_inc(s, 16))
        return (s, queue[1])

    def run(self, e):
        for item in self.items:
            item(e)


class Ring:

    def __init__(self, buffers):
        self.buffers, self.n, self.left = buffers, 0, [()] * len(buffers)

    def take(self):
        held = 0
        while self.left[self.n % len(self.buffers)] is None:
            self.n += 1
            held += 1
            assert held < len(self.buffers), "every buffer is held"
        i = self.n % len(self.buffers)
        self.n += 1
        free, self.left[i] = self.left[i], None
        return i, self.buffers[i], list(free)

    def leave(self, i, *tokens):
        self.left[i] = tokens

    def free(self):
        return self.left[self.n % len(self.buffers)] is not None


def build(nc, ins, out_dram, upto=None, probe_dram=None):
    f32, f32r = mybir.dt.float32, mybir.dt.float32r
    ALU = mybir.AluOpType
    ACT = mybir.ActivationFunctionType
    X_AXIS = mybir.AxisListType.X
    ADD, SUB, MUL, MAX, MIN = ALU.add, ALU.subtract, ALU.mult, ALU.max, ALU.min
    ctx = ExitStack()
    with ctx:
        def sb(name, shape, dtype=f32):
            return ctx.enter_context(nc.sbuf_tensor(name, shape, dtype))

        def sem(name):
            return ctx.enter_context(nc.semaphore(name))

        x_sb = sb("x_sb", [P, DT, TA])
        raw_sb = [sb(f"w_raw{i}", [P, SLOT]) for i in range(N_RAW)]
        split_sb = [(sb(f"w_hi{i}", [P, SLOT], f32r), sb(f"w_lo{i}", [P, SLOT], f32r)) for i in range(N_SPLIT)]
        const = sb("const", [P, N_CONST])
        par = sb("par", [P, N_COLUMNS])
        small = sb("small", [P, 480])
        h_at = nc.sbuf_base
        sb("h_region", [P, 2 * DT * TA])
        work_at = nc.sbuf_base
        sb("work_region", [P, WORK])
        pairs = [ctx.enter_context(nc.psum_tensor(f"banks{i}", [P, 1024], f32)) for i in range(4)]
        banks = Ring([pairs[i // 2][:, 512 * (i % 2):512 * (i % 2) + 512] for i in range(8)])


        pe, dve, act, pool, sp = (Engine(sem(n)) for n in ("s_pe", "s_dve", "s_act", "s_pool", "s_sp"))
        raws, splits = Ring(raw_sb), Ring(split_sb)
        raw_q = [[sem(f"s_raw{i}"), 0] for i in range(N_RAW)]
        const_q, par_q, x_q, out_q, gate_q, lora_q, level_q = (
            [sem(n), 0] for n in ("s_const", "s_par", "s_x", "s_out", "s_gate", "s_lora", "s_levels"))
        rpb_q = [[sem(f"s_rpb{i}"), 0] for i in range(2)]

        def C(name, rows=P):
            at, n = CONSTS[name]
            return const[0:rows, at:at + n]

        def col(name, i=0, n=1, rows=P, base=0):
            at = COLUMNS[name][0] + i
            return par[base:base + rows, at:at + n]

        ident, ones, head_ones = C("ident"), C("ones"), C("head_ones")

        class Area:
            made = 0

            def __init__(self, at=None, size=WORK):
                self.at = work_at if at is None else at
                self.end = (h_at + 4 * 2 * DT * TA) if at is not None and at < work_at else work_at + 4 * WORK

            def take(self, *shape, dtype=f32):
                Area.made += 1
                t = nc.alloc_sbuf_tensor_at(f"area{Area.made}", [P, *shape], dtype, offset=self.at)
                self.at += 4 * int(np.prod(shape))
                self.at += -self.at % 32
                assert self.at <= self.end, (self.at - self.end) / 4
                return t[tuple(slice(None) for _ in range(len(shape) + 1))]

        def h_tensors():
            area = Area(h_at)
            return area.take(DT, TA, dtype=f32r), area.take(DT, TA, dtype=f32r)

        def fence():
            ends = [e.last for e in (pe, dve, act, pool)]
            for e in (dve, act, pool):
                e.wait(ends)
            return ends

        const_in = sp.dma(const[:, :], ins["const"], const_q)
        par_in = sp.dma(par[:, :], ins["par"], par_q)
        x_in = sp.dma(x_sb[:, :, :], ins["xt"], x_q)
        loaded = [const_in, par_in]
        for e in (dve, act, pool, pe):
            e.wait(loaded)

        order = list(weight_order())
        at = {"dma": 0, "split": 0, "use": 0}
        arriving, prepared = {}, {}

        def issue_loads():
            while at["dma"] < len(order) and raws.free():
                name, index, _ = order[at["dma"]]
                dram = ins[name][index]
                i, slot, free = raws.take()
                arriving[at["dma"]] = (i, slot, sp.dma(slot[:, 0:dram.shape[-1]], dram, raw_q[i], after=free))
                at["dma"] += 1

        def split_next():
            n = at["split"]
            issue_loads()
            i, raw, tok = arriving.pop(n)
            if not order[n][2]:
                prepared[n] = ("raw", i, raw, None, [tok])
            else:
                w = ins[order[n][0]].shape[-1]
                k, (hi, lo), free = splits.take()
                t_hi = copy(act, hi[:, 0:w], raw[:, 0:w], after=[tok] + free)
                t_lo = tt(pool, lo[:, 0:w], raw[:, 0:w], hi[:, 0:w].bitcast(f32), SUB, after=[t_hi, tok] + free)
                raws.leave(i, t_lo)
                prepared[n] = ("split", k, hi, lo, [t_hi, t_lo])
            at["split"] += 1

        def load(name, index):
            n = at["use"]
            assert order[n][:2] == (name, index), (order[n], name, index)
            while at["split"] < min(n + AHEAD + 1, len(order)):
                split_next()
            issue_loads()
            at["use"] += 1
            return prepared.pop(n)

        def used(piece):
            (raws if piece[0] == "raw" else splits).leave(piece[1], pe.last)

        def mm(out, lhsT, rhs, first, last, after=(), signal=None):
            signal = last if signal is None else signal
            return pe.do(lambda e: e.matmul(out, lhsT, rhs, start=first, stop=last, skip_group_check=True),
                         after, signal)

        def mm3(out, w_hi, w_lo, z_hi, z_lo, first, last, after=(), signal=None):
            mm(out, w_hi, z_hi, first, False, after)
            mm(out, w_hi, z_lo, False, False)
            return mm(out, w_lo, z_hi, False, last, signal=signal)

        later = []

        def run_later(n=0):
            while len(later) > n:
                later.pop(0)()

        def tt(e, out, a, b, op, after=()):
            return e.do(lambda g: g.tensor_tensor(out, a, b, op), after)

        def ts(e, out, a, s1, op0, s2=None, op1=None, after=()):
            if op1 is None:
                return e.do(lambda g: g.tensor_scalar(out, a, s1, None, op0), after)
            return e.do(lambda g: g.tensor_scalar(out, a, s1, s2, op0, op1), after)

        def stt(out, a, s, b, op0, op1, after=()):
            return dve.do(lambda g: g.scalar_tensor_tensor(out, a, s, b, op0, op1), after)

        def copy(e, out, a, after=()):
            if e is act:
                return act.do(lambda g: g.activation(out, a, ACT.Copy), after)
            return e.do(lambda g: g.tensor_copy(out, a), after)

        def fn(out, a, f, after=(), scale=1.0, bias=None, accum=None):
            kw = {}
            if bias is not None:
                kw["bias"] = bias
            if accum is not None:
                kw["accum_out"] = accum
            return act.do(lambda g: g.activation(out, a, f, scale=scale, **kw), after)

        def memset(e, out, v, after=()):
            return e.do(lambda g: g.memset(out, v), after)

        def recip(out, a, after=()):
            return dve.do(lambda g: g.reciprocal(out, a), after)

        mods, gs, gp, lam_cols = [], [], [], []
        for l in range(DEPTH):
            o = 96 * l
            mods.append(small[:, o:o + 48].rearrange("p (t s) -> p t s", t=24))
            gs.append(small[:, o + 48:o + 64].rearrange("p (t s) -> p t s", t=8))
            gp.append(small[:, o + 64:o + 80].rearrange("p (t s) -> p t s", t=8))
            lam_cols.append(small[:, o + 80:o + 84])
        half_g, C8 = small[:, 192:224].rearrange("p (f j) -> p f j", f=4), 224
        stat = small[:, 256:480]

        def spans(total):
            return [(0, T), (T, TA)] if total == TA else [(0, total)]

        def mean_square(tiles, n, ring, after, rows=P):
            i, bank, free = banks.take()
            for j, tile in enumerate(tiles):
                k, sq, sfree = ring.take()
                t_sq = fn(sq[0:rows, 0:n], tile, ACT.Square, after=list(after) + sfree)
                t_mm = mm(bank[0:rows, 0:n], ones[0:rows, 0:rows], sq[0:rows, 0:n], j == 0, j == len(tiles) - 1,
                          after=[t_sq] + (free if j == 0 else []), signal=True)
                ring.leave(k, t_mm)
            return i, bank, t_mm

        def rstd_of(out, i, bank, t_mm, n, n_feat, after=(), rows=P, eps=0):
            eps_ap = const[0:rows, CONSTS["eps"][0] + eps:CONSTS["eps"][0] + eps + 1]
            t = fn(out, bank[0:rows, 0:n], ACT.Sqrt, after=[t_mm] + list(after), scale=1.0 / n_feat, bias=eps_ap)
            banks.leave(i, t)
            return recip(out, out, after=[t])

        def norm(total, gain, shift, x_toks, after, area):
            hi, lo = h_tensors()
            sq = Ring([area.take(T) for _ in range(2)])
            rs = area.take(TA)
            full = Ring([area.take(T) for _ in range(3)])
            ready = [[] for _ in range(DT)]
            for s, (c0, c1) in enumerate(spans(total)):
                w = c1 - c0
                i, bank, free = banks.take()
                for j in range(DT):
                    k, sq_t, sfree = sq.take()
                    t_sq = fn(sq_t[:, 0:w], x_sb[:, j, c0:c1], ACT.Square, after=x_toks[j] + sfree)
                    t_mm = mm(bank[:, 0:w], ones, sq_t[:, 0:w], j == 0, j == DT - 1, after=[t_sq] + free, signal=True)
                    sq.leave(k, t_mm)
                t = rstd_of(rs[:, c0:c1], i, bank, t_mm, w, D)
                for j in range(DT):
                    k, f, ffree = full.take()
                    t2 = stt(f[:, 0:w], x_sb[:, j, c0:c1], gain(j, s), rs[:, c0:c1], MUL, MUL,
                             after=[t] + x_toks[j] + ffree)
                    if shift is not None:
                        t2 = fn(f[:, 0:w], f[:, 0:w], ACT.Identity, after=[t2], bias=shift(j, s))
                    t_hi = copy(act, hi[:, j, c0:c1], f[:, 0:w], after=[t2] + list(after))
                    e = dve if j % 2 else pool
                    t_lo = tt(e, lo[:, j, c0:c1], f[:, 0:w], hi[:, j, c0:c1].bitcast(f32), SUB, after=[t_hi])
                    full.leave(k, t_lo)
                    ready[j] += [t_hi, t_lo]
            return (hi, lo), ready

        def add_normed(total, gain, y, sums, area):
            rs = area.take(TA)
            tmp = Ring([area.take(T) for _ in range(3)])
            toks = [[] for _ in range(DT)]
            for s, (c0, c1) in enumerate(spans(total)):
                t = rstd_of(rs[:, c0:c1], *sums[s], c1 - c0, D)
                for j in range(DT):
                    k, u, free = tmp.take()
                    t1 = stt(u[:, 0:c1 - c0], y[:, j, c0:c1], gain(j, s), rs[:, c0:c1], MUL, MUL, after=[t] + free)
                    e = dve if j % 3 == 0 else pool
                    t2 = tt(e, x_sb[:, j, c0:c1], x_sb[:, j, c0:c1], u[:, 0:c1 - c0], ADD, after=[t1])
                    tmp.leave(k, t2)
                    toks[j].append(t2)
            return toks

        def project(names, width, h, h_ready, total, consume):
            hi, lo = h
            for m, (name, index) in enumerate(names):
                piece = load(name, index)
                _, _, w_hi, w_lo, toks = piece
                for (c0, c1) in spans(total):
                    i, bank, free = banks.take()
                    out = bank[0:width, 0:c1 - c0]
                    for k in range(DT):
                        o = k * width
                        t = mm3(out, w_hi[:, o:o + width], w_lo[:, o:o + width], hi[:, k, c0:c1], lo[:, k, c0:c1],
                                k == 0, k == DT - 1, after=toks + h_ready[k] + (free if k == 0 else []))
                    run_later()
                    banks.leave(i, consume(m, c0, c1, out, t))
                used(piece)
            run_later()

        def to_tokens(v, width, n_tok, ring):
            def consume(m, c0, c1, b, t):
                k, vt, free = ring.take()
                t_v = copy(act, vt[0:width, 0:c1 - c0], b, after=[t] + free)

                def turn():
                    n = (c1 - c0) // P
                    i, bank, free = banks.take()
                    for q in range(n):
                        t = transpose(bank[:, q * width:(q + 1) * width], vt[0:width, q * P:(q + 1) * P],
                                      after=[t_v] + free, signal=(q == n - 1))
                    ring.leave(k, t)
                    o = v[:, c0 // P:c1 // P, m * width:(m + 1) * width]
                    banks.leave(i, copy(dve, o, bank[:, 0:n * width].rearrange("p (q w) -> p q w", q=n), after=[t]))
                later.append(turn)
                return t_v
            return consume

        def split_into(hi, lo, src, after, e_hi=None, e_lo=None):
            t_hi = copy(e_hi or act, hi, src, after=after)
            return [t_hi, tt(e_lo or pool, lo, src, hi.bitcast(f32), SUB, after=[t_hi] + list(after))]

        def project_out(names_of, k_tiles, total, y, sq, after, add=False, last=True):
            held = [banks.take() for _ in spans(total)] if last else None
            sums = [None] * len(spans(total))
            for m in range(DT):
                outs = [banks.take() for _ in spans(total)]
                k = 0
                for (name, index, n_k) in names_of(m):
                    piece = load(name, index)
                    _, _, w_hi, w_lo, toks = piece
                    for (c0, c1), (i, bank, free) in zip(spans(total), outs):
                        for kk in range(n_k):
                            z_hi, z_lo = k_tiles[k + kk]
                            r = z_hi.shape[0]
                            w = slice(kk * P, (kk + 1) * P)
                            t = mm3(bank[:, 0:c1 - c0], w_hi[0:r, w], w_lo[0:r, w], z_hi[:, c0:c1], z_lo[:, c0:c1],
                                    k + kk == 0, k + kk == len(k_tiles) - 1,
                                    after=toks + (free + list(after) if k == 0 else []), signal=(kk == n_k - 1))
                    k += n_k
                    used(piece)
                run_later()
                for s, ((c0, c1), (i, bank, free)) in enumerate(zip(spans(total), outs)):
                    yy, b = y[:, m, c0:c1], bank[:, 0:c1 - c0]
                    if add:
                        t_y = tt(dve, yy, yy, b, ADD, after=[pe.last])
                    else:
                        t_y = copy(dve, yy, b, after=[pe.last])
                    banks.leave(i, t_y)
                    if last:
                        q, sq_t, sfree = sq.take()
                        t_sq = fn(sq_t[:, 0:c1 - c0], yy, ACT.Square, after=[t_y] + sfree)

                        def add_up(m=m, s=s, n=c1 - c0, sq_t=sq_t, q=q, t_sq=t_sq):
                            i, bank, free = held[s]
                            t = mm(bank[:, 0:n], ones, sq_t[:, 0:n], m == 0, m == DT - 1, after=[t_sq] + free,
                                   signal=True)
                            sq.leave(q, t)
                            sums[s] = (i, bank, t)
                        later.append(add_up)
            run_later()
            return sums

        def transpose(out, in_, after=(), signal=False):
            k = in_.shape[0]
            return pe.do(lambda e: e.transpose(out, in_, ident[0:k, 0:k]), after, signal)

        def modulation(l, area, filler=None):
            cond = area.take(8, 2)
            m_l, lam_col = mods[l], lam_cols[l]
            t_c = fn(cond, col("cond", 0, 16).rearrange("p (k s) -> p k s", k=8), ACT.Silu)
            for c in range(24):
                i, bank, free = banks.take()
                piece = load(f"w_mod{l}", c)
                for k in range(DT):
                    t = mm(bank[:, 0:2], piece[2][:, k * P:(k + 1) * P], cond[:, k, :],
                           k == 0, k == DT - 1, after=[t_c] + piece[4] + free)
                used(piece)
                t = ts(dve, m_l[:, c, :], bank[:, 0:2], col(f"b_mod{l}", c), ADD, after=[t])
                banks.leave(i, t)
                yield
            for s in range(2):
                t1 = ts(dve, gs[l][:, :, s], m_l[:, 8:16, s], 1.0, ADD, after=[t])
                t1 = tt(dve, gs[l][:, :, s], gs[l][:, :, s], col(f"g_pre{l}", 0, 8), MUL, after=[t1])
                t2 = tt(dve, gp[l][:, :, s], m_l[:, 16:24, s], col(f"g_post{l}", 0, 8), MUL)
            prod = area.take(2)
            t3 = tt(dve, prod[0:DF_QK], col(f"lq{l}", 0, 2, DF_QK), col(f"lk{l}", 0, 2, DF_QK), MUL)
            i, bank, free = banks.take()
            t3 = mm(bank[:, 0:2], ones[0:DF_QK, :], prod[0:DF_QK], True, True, after=[t3] + free)
            t3 = fn(lam_col[:, 0:2], bank[:, 0:2], ACT.Exp, after=[t3])
            banks.leave(i, t3)
            t3 = tt(dve, lam_col[:, 2:3], lam_col[:, 0:1], lam_col[:, 1:2], SUB, after=[t3])
            lam_init = 0.8 - 0.6 * math.exp(-0.3 * l)
            t3 = ts(dve, lam_col[:, 3:4], lam_col[:, 2:3], -1.0, MUL, -lam_init, ADD, after=[t3])
            t4 = ts(dve, lam_col[:, 0:1], col(f"subln{l}"), 1.0 - lam_init, MUL, after=[t3])
            mod_done[l] = [t1, t2, t3, t4]

        def softmax_rows(s_ap, n, st, scale, after):
            t = dve.do(lambda g: g.reduce_max(st[:, 0:1], s_ap, X_AXIS), after)
            t = ts(dve, st[:, 0:1], st[:, 0:1], -scale, MUL, after=[t])
            return fn(s_ap, s_ap, ACT.Exp, after=[t], scale=scale, bias=st[:, 0:1], accum=st[:, 1:2])

        def banks_for_rows():
            if banks.n % 2:
                i, _, free = banks.take()
                banks.leave(i, *free)
            i, _, f1 = banks.take()
            i2, _, f2 = banks.take()
            assert i2 == i + 1 and i % 2 == 0
            return i, i2, pairs[i // 2], f1 + f2

        def transposed_values(p_tiles, n_keys, pt, v_of, out_rows, out_base, key0, finish, t_p, pt_free):
            nq = len(p_tiles)
            for j in range(n_keys):
                i, bank, free = banks.take()
                for q, ptile in enumerate(p_tiles):
                    t = transpose(bank[:, q * P:(q + 1) * P], ptile[:, j * P:(j + 1) * P], after=free + t_p,
                                  signal=(q == nq - 1))
                e = act if j % 2 else dve
                banks.leave(i, copy(e, pt[:, j, 0:nq * P], bank[:, 0:nq * P], after=[t] + pt_free))
            t_in = [act.last, dve.last]
            i, bank, free = banks.take()
            o = bank[out_base:out_base + out_rows, 0:nq * P]
            for j in range(n_keys):
                t = mm(o, v_of(key0 + j), pt[:, j, 0:nq * P], j == 0, j == n_keys - 1, after=t_in + free)
            banks.leave(i, finish(o, t))
            return t

        def na_stage(l, total, area, mix, h, h_ready):
            kT, qT, v = area.take(3, TA), area.take(3, TA), area.take(6, NA_W)
            table = ins[f"rpb{l}"]
            flipped = Ring([area.take(BIAS_ROWS, GRID_W) for _ in range(2)])
            mask = C("na_mask").rearrange("p (a b) -> p a b", a=1).broadcast_to((P, BIAS_ROWS, GRID_W))
            bias_of = {}

            def fetch_bias(hh):
                i, rows, free = flipped.take()
                for r2 in range(2):
                    src = bass.AP(tensor=table.tensor, offset=table.offset + (hh * 15 + 1 - r2) * P,
                                  ap=[[1, GRID_W], [P, BIAS_ROWS], [1, GRID_W]])
                    t = pool.dma(rows[r2 * 64:(r2 + 1) * 64], src, rpb_q[i], after=free + stage_ends)
                bias_of[hh] = (i, rows, tt(pool, rows, rows, mask, ADD, after=[t]))
            fetch_bias(0)
            fetch_bias(1)
            p_sb = area.take(4, TA)
            vt = Ring([p_sb[:, n, 0:T] for n in range(2)])
            pt = area.take(6, T)
            names = lambda g: [(f"w_in{l}", i) for i in IN_PIECE[g]]
            project(names(0), P, h, h_ready, TA, lambda m, c0, c1, b, t: copy(act, kT[:, m, c0:c1], b, after=[t]))
            project(names(1), P, h, h_ready, TA, to_tokens(v, P, TA, vt))
            project(names(5), P, h, h_ready, total,
                    lambda m, c0, c1, b, t: fn(mix[:, m, c0:c1], b, ACT.Silu, after=[t]))
            project(names(4), P, h, h_ready, total,
                    lambda m, c0, c1, b, t: ts(dve, qT[:, m, c0:c1], b, NA_DH ** -0.5, MUL, after=[t]))
            ready = [act.last, dve.last, pe.last]
            pt_free = []
            for h_ in range(NA_HEADS):
                p, b0 = h_ // 2, 64 * (h_ % 2)
                i_b, rows, t_bias = bias_of.pop(h_)
                flat = rows.rearrange("p a b -> p (a b)")
                jobs = [([0, 1, 2, 3], True)] + ([([4, 5], False)] if total == TA else [])
                for tiles, local in jobs:
                    t_p = []
                    for n, q in enumerate(tiles):
                        st = stat[:, 4 * n:4 * n + 4]
                        i1, i2, two, free = banks_for_rows()
                        k0 = 0 if local else T
                        qq = qT[b0:b0 + 64, p, q * P:(q + 1) * P]
                        if local:
                            mm(two[:, 0:T], C("turn"), flat[:, (6 - 2 * q) * GRID_W:(14 - 2 * q) * GRID_W], True, False,
                               after=free + ready + [t_bias])
                            mm(two[:, 0:T], qq, kT[b0:b0 + 64, p, 0:T], False, True)
                        t = mm(two[:, T:TA], qq, kT[b0:b0 + 64, p, T:TA], True, True, after=free + ready)
                        s = p_sb[:, n, k0:TA]
                        t = dve.do(lambda g, st=st, s_=two[:, k0:TA]: g.reduce_max(st[:, 0:1], s_, X_AXIS),
                                   [t] + ready)
                        t = ts(dve, st[:, 3:4], st[:, 0:1], -1.0, MUL, after=[t])
                        t = fn(s, two[:, k0:TA], ACT.Exp, after=[t] + pt_free, bias=st[:, 3:4], accum=st[:, 1:2])
                        banks.leave(i1, t)
                        banks.leave(i2, t)
                        t = recip(st[:, 2:3], st[:, 1:2], after=[t])
                        t_p.append(ts(dve, s, s, st[:, 2:3], MUL, after=[t]))
                    if local:
                        flipped.leave(i_b, pe.last)
                        if h_ + 2 < NA_HEADS:
                            fetch_bias(h_ + 2)
                    c0 = tiles[0] * P
                    n_q = len(tiles) * P
                    src = [p_sb[:, n, :] if local else p_sb[:, n, T:TA] for n in range(len(tiles))]

                    def finish(o, t):
                        m = mix[b0:b0 + 64, p, c0:c0 + n_q]
                        return tt(dve, m, o, m, MUL, after=[t])
                    t = transposed_values(src, 6 if local else 2, pt, lambda j: v[:, j, h_ * 64:(h_ + 1) * 64], 64, b0,
                                          0 if local else 4, finish, t_p, pt_free)
                    pt_free = [t]

        def late_stage(l, total, area, mix, h, h_ready, mod_area):
            kd, qd = area.take(4, TA), area.take(4, TA)
            v = area.take(6, NA_W)
            u = area.take(2, CONV_TOK)
            raw = Ring([area.take(T) for _ in range(2)])
            tmp = Ring([area.take(T) for _ in range(2)])
            names = lambda g: [(f"w_in{l}", i) for i in IN_PIECE[g]]
            rot, cos, sin = C("rot", 96), C("cos", 96), C("sin", 96)
            lam_col = lam_cols[l]
            t0 = memset(dve, u, 0.0)
            starts = {0: PAD, T: PAD + T + PAD}

            def glu(base):
                def go(m, c0, c1, b, t):
                    m += base
                    at_ = starts[c0]
                    n = c1 - c0
                    if m < 2:
                        return copy(dve, u[:, m, at_:at_ + n], b, after=[t, t0])
                    if m < 4:
                        k, sg, free = raw.take()
                        t1 = fn(sg[:, 0:n], b, ACT.Sigmoid, after=[t] + free)
                        uu = u[:, m - 2, at_:at_ + n]
                        raw.leave(k, tt(dve, uu, uu, sg[:, 0:n], MUL, after=[t1, dve.last]))
                        return t1
                    return fn(mix[:, 3 + m, c0:c1], b, ACT.Silu, after=[t])
                return go

            def roped(dst):
                def consume(m, c0, c1, b, t):
                    if c0 >= T:
                        return copy(act, dst[0:96, m, c0:c1], b, after=[t])
                    r, raw_t, rfree = raw.take()
                    t_raw = copy(act, raw_t[0:96], b, after=[t] + rfree)

                    def turn():
                        k, tmp_t, ufree = tmp.take()
                        i, bank, free = banks.take()
                        t1 = mm(bank[0:96, 0:T], rot, raw_t[0:96], True, True, after=[t_raw] + free)
                        t1 = tt(dve, tmp_t[0:96], bank[0:96, 0:T], sin, MUL, after=[t1] + ufree)
                        banks.leave(i, t1)
                        t2 = tt(pool, dst[0:96, m, 0:T], raw_t[0:96], cos, MUL, after=[t_raw])
                        raw.leave(r, t2, t1)
                        t3 = tt(pool, dst[0:96, m, 0:T], dst[0:96, m, 0:T], tmp_t[0:96], ADD, after=[t1, t2])
                        tmp.leave(k, t3)
                    later.append(turn)
                    return t_raw
                return consume

            project(names(8), P, h, h_ready, total, glu(0))
            project(names(9), P, h, h_ready, total, glu(3))
            t_u = [dve.last]
            project(names(2), DF_V, h, h_ready, TA, roped(kd))
            project(names(3), P, h, h_ready, TA, to_tokens(v, P, TA, raw))
            project(names(7), DF_V, h, h_ready, total,
                    lambda m, c0, c1, b, t: fn(mix[0:96, 3 + m, c0:c1], b, ACT.Silu, after=[t]))
            project(names(6), DF_V, h, h_ready, total, roped(qd))
            ready = [act.last, dve.last, pool.last, pe.last]
            area = Area(h_at)
            p1, p2 = area.take(4, TA), Ring([area.take(TA) for _ in range(2)])
            pt, q2, y = area.take(6, T), area.take(TA), area.take(2, CONV_OUT)
            sq = Ring([tmp.buffers[0]])
            rs, o_sb = raw.buffers[0], raw.buffers[1]
            half = const[0:96, CONSTS["half"][0]:CONSTS["half"][0] + 1]
            scale = DF_QK ** -0.5
            n_y = T if total == T else CONV_OUT
            other = modulation(1, mod_area) if l == 0 else iter(())

            def taps():
                last = [None, None]
                for k in range(TAPS):
                    for m in range(2):
                        yy = y[:, m, 0:n_y]
                        if k == 0:
                            last[m] = ts(dve, yy, u[:, m, 0:n_y], col(f"conv_w{l}", m * TAPS), MUL,
                                         col(f"conv_b{l}", m), ADD, after=t_u + ready)
                        else:
                            last[m] = stt(yy, u[:, m, k:k + n_y], col(f"conv_w{l}", m * TAPS + k), yy, MUL, ADD,
                                          after=[last[m]])
                        yield
            taps = taps()

            def fill(n):
                for _ in range(n):
                    next(taps, None)

            pt_free, p_free = [], []
            for h_ in range(DF_HEADS):
                t_q2 = ts(dve, q2[0:96, 0:total], qd[0:96, h_, 0:total], half, MUL, after=ready + [pe.last])
                jobs = [([0, 1, 2, 3], True)] + ([([4, 5], False)] if total == TA else [])
                for tiles, local in jobs:
                    t_p = []
                    k0 = 0 if local else T
                    for n, q in enumerate(tiles):
                        done = []
                        pi, p2_t, p2_free = p2.take()
                        s1, s2 = p1[:, n, k0:TA], p2_t[:, k0:TA]
                        for w_, (dst, qq, kk, fr) in enumerate(((s1, qd[0:48, h_], kd[0:48, h_], p_free),
                                                                (s2, q2[0:96], kd[0:96, h_], p2_free))):
                            st = stat[:, 32 * w_ + 4 * n:32 * w_ + 4 * n + 4]
                            i1, i2, two, free = banks_for_rows()
                            for (a, b) in ([(0, T)] if local else []) + [(T, TA)]:
                                t = mm(two[:, a:b], qq[:, q * P:(q + 1) * P], kk[:, a:b], True, True,
                                       after=free + ready + [t_q2])
                            t = dve.do(lambda g, st=st, s_=two[:, k0:TA]: g.reduce_max(st[:, 0:1], s_, X_AXIS), [t])
                            t = ts(dve, st[:, 3:4], st[:, 0:1], -scale, MUL, after=[t])
                            t = fn(dst, two[:, k0:TA], ACT.Exp, after=[t] + list(fr), scale=scale, bias=st[:, 3:4],
                                   accum=st[:, 1:2])
                            banks.leave(i1, t)
                            banks.leave(i2, t)
                            fill(1)
                            done.append(recip(st[:, 2:3], st[:, 1:2], after=[t]))
                        st, st2 = stat[:, 4 * n:4 * n + 4], stat[:, 32 + 4 * n:36 + 4 * n]
                        t = ts(dve, s1, s1, st[:, 2:3], MUL, after=[done[0]])
                        t2 = tt(dve, st2[:, 3:4], st2[:, 2:3], lam_col[:, 3:4], MUL, after=[done[1]])
                        t = stt(s1, s2, st2[:, 3:4], s1, MUL, ADD, after=[t, t2])
                        p2.leave(pi, t)
                        t_p.append(t)
                        next(other, None)
                    c0, n_q = tiles[0] * P, len(tiles) * P

                    def finish(o, t):
                        t_o = copy(act, o_sb[0:96, 0:n_q], o, after=[t, dve.last])
                        b = mean_square([o_sb[0:96, 0:n_q]], n_q, sq, [t_o], rows=96)
                        t2 = rstd_of(rs[0:96, 0:n_q], *b, n_q, DF_V, rows=96)
                        t2 = stt(rs[0:96, 0:n_q], o_sb[0:96, 0:n_q], lam_col[0:96, 0:1], rs[0:96, 0:n_q], MUL, MUL,
                                 after=[t2])
                        m = mix[0:96, 3 + h_, c0:c0 + n_q]
                        tt(dve, m, rs[0:96, 0:n_q], m, MUL, after=[t2])
                        return t_o
                    t = transposed_values([p1[:, n, k0:TA] for n in range(len(tiles))], 6 if local else 2, pt,
                                          lambda j: v[:, j, h_ * 96:(h_ + 1) * 96], 96, 0, 0 if local else 4,
                                          finish, t_p, pt_free)
                    pt_free, p_free = [t], [t]
            for _ in other:
                pass
            fill(2 * TAPS)
            sq = Ring(tmp.buffers)
            rs = raw.buffers[0]
            for (c0, c1) in spans(total):
                w = c1 - c0
                at_ = 0 if c0 == 0 else T + PAD
                i, bank, free = banks.take()
                for m in range(2):
                    tm = mm(bank[:, 0:w], ones, y[:, m, at_:at_ + w], m == 0, m == 1, after=[dve.last] + free)
                ts_ = []
                for m in range(2):
                    ts_.append(stt(y[:, m, at_:at_ + w], bank[:, 0:w], -1.0 / CONV_W, y[:, m, at_:at_ + w], MUL, ADD,
                                   after=[tm]))
                banks.leave(i, ts_[1])
                b = mean_square([y[:, m, at_:at_ + w] for m in range(2)], w, sq, ts_ + [dve.last])
                t = rstd_of(rs[:, 0:w], *b, w, CONV_W, after=[dve.last])
                for m in range(2):
                    yy = y[:, m, at_:at_ + w]
                    t1 = stt(yy, yy, col(f"ln_g{l}", m), rs[:, 0:w], MUL, MUL, after=[t])
                    t1 = fn(yy, yy, ACT.Silu, after=[t1], bias=col(f"ln_b{l}", m))
                    tt(dve, mix[:, 7 + m, c0:c1], yy, mix[:, 7 + m, c0:c1], MUL, after=[t1])

        def first_layer(l, total, x_toks):
            nonlocal stage_ends
            stage_ends = fence()
            base = Area()
            mod_area = Area(base.at)
            mod_area.take(8, 2), mod_area.take(2)
            base.at = mod_area.at
            if l == 0:
                for _ in modulation(0, Area()):
                    pass
            mix = base.take(9, TA)
            h, h_ready = norm(TA, lambda j, s: gs[l][:, j, s:s + 1], lambda j, s: mods[l][:, j, s:s + 1],
                              [t + mod_done[l] for t in x_toks], stage_ends, Area(base.at))
            stage_ends = fence()
            na_stage(l, total, Area(base.at), mix, h, h_ready)
            stage_ends = fence()
            late_stage(l, total, Area(base.at), mix, h, h_ready, Area())
            ends = fence()
            h_area = Area(h_at)
            rows = [P] * 3 + [96] * 4 + [P] * 2
            m_hi, m_lo = h_area.take(9, total, dtype=f32r), None
            if h_area.at + 4 * 9 * total <= h_area.end:
                m_lo = h_area.take(9, total, dtype=f32r)
            area = Area(base.at)
            if m_lo is None:
                m_lo = area.take(9, total, dtype=f32r)
            y = area.take(DT, total)
            sq = Ring([area.take(T) for _ in range(2)])
            k_tiles, t_in = [], []
            for i, r in enumerate(rows):
                t_in += split_into(m_hi[0:r, i, :], m_lo[0:r, i, :], mix[0:r, i, 0:total], ends,
                                   e_lo=dve if i % 2 else pool)
                k_tiles.append((m_hi[0:r, i, :], m_lo[0:r, i, :]))

            def names_of(m):
                return [(f"w_out{l}", 2 * m, W_OUT_K[0]), (f"w_out{l}", 2 * m + 1, W_OUT_K[1])]
            sums = project_out(names_of, k_tiles, total, y, sq, t_in)
            return add_normed(total, lambda j, s: gp[l][:, j, s:s + 1], y, sums, Area(base.at - 4 * 9 * TA))

        def ffn(name, f, x_toks):
            ends = fence()
            t_half = ts(dve, half_g[:, f, :], col(name + "_post", 0, 8), 0.5, MUL)
            area = Area()
            n_half = FT // 2
            a_hi, a_lo, y = area.take(n_half, T, dtype=f32r), area.take(n_half, T, dtype=f32r), area.take(DT, T)
            mark = area.at
            h, h_ready = norm(T, lambda j, s: col(name + "_pre", j), None, x_toks, ends, Area())
            hi, lo = h
            ends = fence()
            area = Area(mark)
            sg = Ring([area.take(T) for _ in range(2)])
            act_r = Ring([area.take(T) for _ in range(2)])
            sq = Ring([area.take(T) for _ in range(2)])
            for half in range(2):
                gate = {}

                def consume(m, c0, c1, b, t):
                    j = m // 2
                    if m % 2 == 0:
                        r, sg_t, free = sg.take()
                        gate[j] = (r, sg_t, fn(sg_t, b, ACT.Silu, after=[t] + free))
                        return gate[j][2]
                    r, sg_t, t1 = gate.pop(j)
                    k, a_t, free = act_r.take()
                    t2 = tt(dve, a_t, b, sg_t, MUL, after=[t, t1] + free)
                    sg.leave(r, t2)
                    t_hi = copy(dve, a_hi[:, j, :], a_t, after=[t2] + a_free)
                    t_lo = tt(dve, a_lo[:, j, :], a_t, a_hi[:, j, :].bitcast(f32), SUB, after=[t_hi] + a_free)
                    act_r.leave(k, t_lo)
                    return t2
                a_free = [pe.last]
                project([(name + "_w_in", half * FT + c) for c in range(FT)], P, h, h_ready, T, consume)
                sums = project_out(lambda m: [(name + f"_w_out{half}", 2 * m, FFN_K[0]),
                                              (name + f"_w_out{half}", 2 * m + 1, FFN_K[1])],
                                   [(a_hi[:, k, :], a_lo[:, k, :]) for k in range(n_half)], T, y, sq, [dve.last],
                                   add=(half == 1), last=(half == 1))
            return add_normed(T, lambda j, s: half_g[:, f, j:j + 1], y, sums, Area(mark))

        def even_mixer(x_toks):
            ends = fence()
            h, h_ready = norm(T, lambda j, s: col("l0_mix_pre", j), None, x_toks, ends, Area())
            fence()
            area = Area()
            pa = area.take(14, T + 1)
            mixed = area.take(8, T)
            z = memset(pool, pa[:, :, 0:1], 0.0)
            at_rw = area.at
            tmp = Ring([area.take(T) for _ in range(2)])

            def into_pa(base):
                def go(m, c0, c1, b, t):
                    i = base + m
                    t = copy(act, pa[:, i, 1:T + 1], b, after=[t])
                    r, d, free = tmp.take()
                    t1 = tt(pool, d, pa[:, i, 0:T], pa[:, i, 1:T + 1], SUB, after=[t, z] + free)
                    t2 = stt(pa[:, i, 1:T + 1], d, col("mu", i), pa[:, i, 1:T + 1], MUL, ADD, after=[t1])
                    tmp.leave(r, t2)
                    return t
                return go
            names = [("l0_w_in", c) for c in range(22)]
            project(names[:14], P, h, h_ready, T, into_pa(0))
            project(names[14:], P, h, h_ready, T,
                    lambda m, c0, c1, b, t: copy(act if m % 2 else dve, mixed[:, m, :], b, after=[t]))
            t_pa = [act.last, dve.last, pool.last]

            area = Area(at_rw)
            xc, a_t, u_t, tm = area.take(T), area.take(T), area.take(T), area.take(T)
            gw = area.take(2, 4 * HD)
            t_gw = sp.dma(gw.rearrange("p a b -> p (a b)"), ins["gate_w"], gate_q, after=t_pa)
            lam = col("lam", 0, 4)
            c8 = small[:, C8:C8 + 16]
            t = fn(c8[:, 0:4], lam, ACT.Abs)
            t = fn(c8[:, 0:4], c8[:, 0:4], ACT.Exp, after=[t], scale=-1.0)
            t = fn(c8[:, 0:4], c8[:, 0:4], ACT.Ln, after=[t], bias=ones[:, 0:1])
            t1 = ts(dve, c8[:, 4:8], lam, -1.0, MUL, 0.0, MAX)
            t1 = tt(dve, c8[:, 8:12], c8[:, 0:4], c8[:, 4:8], ADD, after=[t, t1])
            t_c8 = ts(dve, c8[:, 12:16], c8[:, 8:12], -8.0, MUL, after=[t1])
            for p in range(4):
                xb = mixed[:, p, :]
                t = ts(dve, xc, xb, col("rconv_w", 4 * p + 3), MUL, col("rconv_b", p), ADD,
                       after=t_pa + [act.last, dve.last, pe.last])
                for k in range(3):
                    s = 3 - k
                    t = stt(xc[:, s:T], xb[:, 0:T - s], col("rconv_w", 4 * p + k), xc[:, s:T], MUL, ADD, after=[t])
                outs = []
                for g, bias in ((0, "ga_b"), (1, "gx_b")):
                    i, bank, free = banks.take()
                    for b0 in (0, 64):
                        tg = mm(bank[b0:b0 + 64, :], gw[b0:b0 + 64, g, p * HD:(p + 1) * HD], xc[b0:b0 + 64], True, True,
                                after=[t, t_gw] + free)
                    dst = a_t if g == 0 else u_t
                    tg = fn(dst, bank[:, :], ACT.Sigmoid, after=[tg, dve.last], bias=col(bias, p))
                    banks.leave(i, tg)
                    outs.append(tg)
                t1 = ts(dve, a_t, a_t, c8[:, 12 + p:13 + p], MUL, after=outs + [t_c8])
                t2 = fn(tm, a_t, ACT.Tanh, after=[t1], scale=-1.0)
                t3 = fn(a_t, a_t, ACT.Exp, after=[t2])
                t4 = tt(dve, xb, a_t, a_t, MUL, after=[t3])
                t4 = stt(tm, xb, 1.0, tm, ADD, MUL, after=[t4, t2])
                t4 = fn(tm, tm, ACT.Sqrt, after=[t4])
                t5 = tt(dve, u_t, u_t, xc, MUL, after=[outs[1]])
                t5 = tt(dve, u_t, u_t, tm, MUL, after=[t4, t5])
                t5 = dve.do(lambda g_, o=xb, a=a_t, b=u_t: g_.tensor_tensor_scan(o, a, b, 0.0, MUL, ADD),
                            [t5, t3])
                gb = mixed[:, 4 + p, :]
                t6 = fn(tm, gb, ACT.Square, after=[t5])
                t6 = ts(dve, tm, tm, 0.044715, MUL, 1.0, ADD, after=[t6])
                t6 = tt(dve, tm, tm, gb, MUL, after=[t6])
                t6 = fn(tm, tm, ACT.Tanh, after=[t6], scale=math.sqrt(2.0 / math.pi))
                t6 = stt(tm, tm, 1.0, gb, ADD, MUL, after=[t6])
                t6 = stt(gb, tm, 0.5, xb, MUL, MUL, after=[t6])

            ends = fence()
            h_area = Area(h_at)
            ar = h_area.take(2, 4, T)
            b_t, k_t = h_area.take(4, T), h_area.take(4, T)
            v_all = h_area.take(NCH, A_W)
            lora = h_area.take(2, T)
            tok_l = sp.dma(lora.rearrange("p a b -> p (a b)"), ins["lora"], lora_q, after=ends)
            w2, a2, g2 = lora[0:64, 0, :], lora[64:128, 0, :], lora[:, 1, :]

            def v_tok(c, h):
                return v_all[:, c, h * HD:(h + 1) * HD]
            area = Area(at_rw)
            glo = area.take(T)
            tot = area.take(4, 2 * NCH)
            levels = area.take(14, P)
            tok_v = sp.dma(levels.rearrange("p a b -> p (a b)"), ins["levels"], level_q, after=ends)
            chunk_at = area.at
            lo = area.take(T)
            sc = [area.take(T) for _ in range(4)]
            pb = area.take(NCH, CH + 1)
            ones_row = area.take(CH)
            t = fn(lo[0:64], pa[0:64, 12, 1:T + 1], ACT.Tanh)
            t = copy(act, lo[64:128], pa[64:128, 12, 1:T + 1])
            t = fn(glo, pa[:, 13, 1:T + 1], ACT.Sigmoid)
            t_one = memset(pool, ones_row, 1.0)
            t_pb = memset(pool, pb[:, :, 0:1], 1.0)
            ready = [t, t_one, t_pb]

            def by_chunk(v):
                return v.rearrange("p (c n) -> p c n", c=NCH)
            t_first = None
            for p in range(4):
                r, k, v = (pa[:, 4 * q + p, 1:T + 1] for q in range(3))
                wt, at_, kk, km = sc
                i, bank, free = banks.take()
                tm_ = mm(bank[:, :], w2[:, p * P:(p + 1) * P], lo[0:64], True, True, after=free + [tok_l] + ready)
                t1 = fn(wt, bank[:, :], ACT.Sigmoid, after=[tm_, dve.last, pool.last], bias=col("w0", p))
                banks.leave(i, t1)
                i, bank, free = banks.take()
                tm_ = mm(bank[:, :], a2[:, p * P:(p + 1) * P], lo[64:128], True, True, after=free)
                t2 = fn(at_, bank[:, :], ACT.Sigmoid, after=[tm_], bias=col("a0", p))
                banks.leave(i, t2)
                t1 = fn(wt, wt, ACT.Exp, after=[t1], scale=-math.exp(-0.5))
                t3 = ts(dve, kk, k, col("k_k", p), MUL, after=[t1, pe.last])
                t4 = fn(km, kk, ACT.Square, after=[t3])
                i, bank, free = banks.take()
                t4 = mm(bank[:, :], head_ones, km, True, True, after=free + [t4])
                t4 = fn(km, bank[:, :], ACT.Sqrt, after=[t4])
                banks.leave(i, t4)
                t4 = ts(dve, km, km, 1e-12, MAX, after=[t4])
                t4 = recip(km, km, after=[t4])
                t4 = tt(dve, kk, kk, km, MUL, after=[t4])
                for c in range(NCH):
                    t5 = dve.do(lambda g, c=c: g.tensor_tensor_scan(pb[:, c, 1:CH + 1], wt[:, c * CH:(c + 1) * CH],
                                                                    ones_row, 1.0, MUL, MUL),
                                [t1, t_one, t_pb] + ([t_first] if t_first else []))
                t5 = copy(dve, tot[:, p, 0:NCH], pb[:, :, CH // 2], after=[t5])
                t5 = recip(tot[:, p, NCH:2 * NCH], tot[:, p, 0:NCH], after=[t5])
                for c in range(NCH):
                    t6 = ts(dve, pb[:, c, :], pb[:, c, :], tot[:, p, NCH + c:NCH + c + 1], MUL, after=[t5])
                t7 = copy(dve, tot[:, p, NCH:2 * NCH], pb[:, :, CH], after=[t6])
                t8 = stt(by_chunk(ar[:, 0, p, :]), by_chunk(kk), -1.0, pb[:, :, 0:CH], MUL, MUL, after=[t4, t7])
                t9 = tt(dve, by_chunk(ar[:, 1, p, :]), by_chunk(r), pb[:, :, 1:CH + 1], MUL, after=[t7])
                t10 = recip(pb[:, :, 1:CH + 1], pb[:, :, 1:CH + 1], after=[t9, t8])
                t11 = tt(dve, kk, kk, at_, MUL, after=[t8, t2])
                t12 = tt(dve, by_chunk(b_t[:, p, :]), by_chunk(kk), pb[:, :, 1:CH + 1], MUL, after=[t10, t11])
                t13 = ts(dve, at_, at_, -1.0, ADD, col("k_a", p), MUL, after=[t11])
                t13 = stt(k, at_, 1.0, k, ADD, MUL, after=[t13, t3])
                t14 = tt(dve, by_chunk(k_t[:, p, :]), by_chunk(k), pb[:, :, 1:CH + 1], MUL, after=[t10, t13])
                t_first = memset(dve, pb[:, :, 0:1], 1.0, after=[t14])
                t15 = stt(r, r, col("r_k", p), k, MUL, MUL, after=[t13, t9])
                i, bank, free = banks.take()
                t15 = mm(bank[:, :], head_ones, r, True, True, after=free + [t15])
                t15 = tt(dve, r, bank[:, :], v, MUL, after=[t15])
                banks.leave(i, t15)
            ends = fence()
            area = Area(chunk_at)
            x_m, xt_m, m_ab_t, m_ak_t, m_rb_t, m_rk_t, t1_m = (area.take(8, P) for _ in range(7))
            k_area = pa[:, 4:8, 1:T + 1]
            b_tok, k_tok = k_area[:, 0, :], k_area[:, 1, :]
            sa, rhs = k_area[:, 2, :], k_area[:, 3, :]
            m_off = Ring([area.take(4, P) for _ in range(2)])
            state, state_mid = h_area.take(4, HD), h_area.take(4, HD)
            upper = C("upper").rearrange("p (a b) -> p a b", a=2)
            lower = C("lower")
            for e in (dve, pool):
                e.wait([tok_v])
            lv = lambda n, tr: levels[:, 2 * n + tr, :]
            t_s = memset(dve, state, 0.0)

            def slot_of(h):
                return 4 * (h % 2) + h // 2

            def rep(m, n):
                return m.rearrange("p (a b) -> p a b", a=1).broadcast_to((P, n, P))

            for c in range(NCH):
                cs = slice(c * CH, (c + 1) * CH)
                gate_c = [act.last, dve.last, pool.last, pe.last]
                for e in (act, dve, pool):
                    e.wait(gate_c)
                for src, dst in ((lambda p: pa[:, 8 + p, 1 + c * CH:1 + (c + 1) * CH], None),
                                 (lambda p: b_t[:, p, cs], b_tok), (lambda p: k_t[:, p, cs], k_tok)):
                    i, bank, free = banks.take()
                    for p in range(4):
                        t = transpose(bank[:, p * P:(p + 1) * P], src(p), after=free + ends, signal=(p == 3))
                    t2 = copy(act, v_all[:, c, :] if dst is None else dst, bank[:, :], after=[t])
                    banks.leave(i, t2)
                for half in range(2):
                    for left, m1, m2 in ((b_t, m_ab_t, m_rb_t), (k_t, m_ak_t, m_rk_t)):
                        for odd in range(2):
                            i, bank, free = banks.take()
                            b0 = 64 * odd
                            for n in range(2):
                                pair = 2 * half + n
                                t = mm(bank[:, n * 256:(n + 1) * 256].rearrange("p (a b) -> p a b", a=2),
                                       left[b0:b0 + 64, pair, cs], ar[b0:b0 + 64, :, pair, cs], True, True,
                                       after=free + ends)
                            v4 = bank[:, :].rearrange("p (n a b) -> p n a b", n=2, a=2)
                            at4 = 4 * odd + 2 * half
                            for a_, m in ((0, m1), (1, m2)):
                                t2 = tt(dve, m[:, at4:at4 + 2, :], v4[:, :, a_, :], rep(upper[:, a_, :], 2), MUL,
                                        after=[t])
                            banks.leave(i, t2)
                for g in range(2):
                    i, bank, free = banks.take()
                    for n in range(4):
                        b0 = 64 * g
                        t = mm(bank[:, n * P:(n + 1) * P], ar[b0:b0 + 64, 0, n, cs], b_t[b0:b0 + 64, n, cs],
                               True, True, after=free)
                    xs, xts = x_m[:, 4 * g:4 * g + 4, :], xt_m[:, 4 * g:4 * g + 4, :]
                    t = tt(dve, xs, bank[:, :].rearrange("p (n b) -> p n b", n=4), rep(lv(0, 0), 4), MUL, after=[t])
                    banks.leave(i, t)
                    t = tt(dve, xs, xs, rep(ident, 4), ADD, after=[t])
                    t = tt(dve, xts, m_ab_t[:, 4 * g:4 * g + 4, :], rep(lv(0, 1), 4), MUL, after=[dve.last])
                    t_x = tt(dve, xts, xts, rep(ident, 4), ADD, after=[t])
                t_xs = [t_x, t_x]
                for n_l in range(1, 7):
                    for g in range(2):
                        gs4 = slice(4 * g, 4 * g + 4)
                        r_, off, ofree = m_off.take()
                        t_off = tt(pool, off, m_ab_t[:, gs4, :], rep(lv(n_l, 1), 4), MUL, after=[t_x] + ofree)
                        i, bank, free = banks.take()
                        for n in range(4):
                            t = mm(bank[:, n * P:(n + 1) * P], off[:, n, :], x_m[:, 4 * g + n, :], True, True,
                                   after=free + [t_off, t_xs[g]])
                        m_off.leave(r_, pe.last)
                        tc1 = copy(act, t1_m[:, gs4, :], bank[:, :].rearrange("p (n b) -> p n b", n=4),
                                   after=[t])
                        banks.leave(i, tc1)
                        outs = []
                        i2, bank2, free2 = banks.take()
                        for n in range(4):
                            t = mm(bank2[:, n * P:(n + 1) * P], t1_m[:, 4 * g + n, :], xt_m[:, 4 * g + n, :], True, True,
                                   after=free2 + [tc1])
                        if n_l < 6:
                            i3, bank3, free3 = banks.take()
                            for n in range(4):
                                t3_ = mm(bank3[:, n * P:(n + 1) * P], xt_m[:, 4 * g + n, :], t1_m[:, 4 * g + n, :],
                                         True, True, after=free3)
                            t4_ = tt(dve, x_m[:, gs4, :], x_m[:, gs4, :],
                                     bank3[:, :].rearrange("p (n b) -> p n b", n=4), ADD, after=[t3_, dve.last])
                            banks.leave(i3, t4_)
                        t_xs[g] = tt(dve, xt_m[:, gs4, :], xt_m[:, gs4, :],
                                     bank2[:, :].rearrange("p (n b) -> p n b", n=4), ADD, after=[pe.last])
                        banks.leave(i2, t_xs[g])
                for p in range(4):
                    t_sm = ts(dve, state_mid[:, p, :], state[:, p, :], tot[:, p, c:c + 1], MUL, after=[t_s])
                for odd in range(2):
                    i, bank, free = banks.take()
                    b0 = 64 * odd
                    for n in range(4):
                        o = bank[:, n * HD:(n + 1) * HD]
                        mm(o, ar[b0:b0 + 64, 0, n, cs], state_mid[b0:b0 + 64, n, :], True, False,
                           after=free + [t_sm, act.last])
                        t = mm(o, m_ak_t[:, 4 * odd + n, :], v_tok(c, 2 * n + odd), False, True)
                    t = copy(act, rhs[:, 256 * odd:256 * odd + 256], bank[:, 0:256], after=[t])
                    banks.leave(i, t)
                i, bank, free = banks.take()
                for h in range(8):
                    t2 = mm(bank[:, h * HD:(h + 1) * HD], xt_m[:, h, :], rhs[:, h * HD:(h + 1) * HD], True, True,
                            after=free + [t] + t_xs)
                t_sa = copy(act, sa, bank[:, :], after=[t2])
                banks.leave(i, t_sa)
                i, bank, free = banks.take()
                for h in range(8):
                    b0 = 64 * (h % 2)
                    o = bank[b0:b0 + 64, (h // 2) * P:(h // 2 + 1) * P]
                    mm(o, state_mid[b0:b0 + 64, h // 2, :], ar[b0:b0 + 64, 1, h // 2, cs], True, False,
                       after=free + [t_sa])
                    m_h = slot_of(h)
                    mm(o, sa[:, m_h * HD:(m_h + 1) * HD], m_rb_t[:, m_h, :], False, False)
                    t_y = mm(o, v_tok(c, h), m_rk_t[:, m_h, :], False, True)
                i2, bank2, free2 = banks.take()
                for h in range(8):
                    b0 = 64 * (h % 2)
                    o = bank2[b0:b0 + 64, (h // 2) * HD:(h // 2 + 1) * HD]
                    m_h = slot_of(h)
                    mm(o, b_tok[:, h * HD:(h + 1) * HD], sa[:, m_h * HD:(m_h + 1) * HD], True, False, after=free2)
                    t_n = mm(o, k_tok[:, h * HD:(h + 1) * HD], v_tok(c, h), False, True)
                t_s = tt(dve, state, state_mid, bank2[:, 0:256].rearrange("p (a b) -> p a b", a=4), ADD, after=[t_n])
                banks.leave(i2, t_s)
                for p in range(4):
                    t_s2 = ts(dve, state[:, p, :], state[:, p, :], tot[:, p, NCH + c:NCH + c + 1], MUL, after=[t_s])
                t_s = t_s2
                y_c, sq_c = x_m[:, 0:4, :], x_m[:, 4:8, :]
                t = copy(act, y_c, bank[:, :].rearrange("p (a b) -> p a b", a=4), after=[t_y, dve.last])
                banks.leave(i, t)
                i, bank, free = banks.take()
                flat = lambda v: v.rearrange("p a b -> p (a b)")
                t = mm(bank[:, :], head_ones, flat(y_c), True, True, after=free + [t])
                t = stt(flat(y_c), bank[:, :], -1.0 / HD, flat(y_c), MUL, ADD, after=[t])
                banks.leave(i, t)
                t2 = fn(flat(sq_c), flat(y_c), ACT.Square, after=[t])
                i, bank, free = banks.take()
                t2 = mm(bank[:, :], head_ones, flat(sq_c), True, True, after=free + [t2])
                t2 = rstd_of(flat(sq_c), i, bank, t2, 512, HD, eps=1)
                tt(dve, mixed[:, 0:4, cs], y_c, sq_c, MUL, after=[t2])
            for p in range(4):
                m = mixed[:, p, :]
                t = ts(dve, m, m, col("lnx_g", p), MUL, col("lnx_b", p), ADD, after=[dve.last])
                t = tt(dve, m, m, pa[:, p, 1:T + 1], ADD, after=[t])
                i, bank, free = banks.take()
                t2 = mm(bank[:, :], g2[:, p * P:(p + 1) * P], glo, True, True, after=free)
                t = tt(dve, m, bank[:, :], m, MUL, after=[t, t2])
                banks.leave(i, t)
            ends = fence()
            return out_of_mixer("l0_w_out", mixed, ends, "l0_mix_post", Area(at_rw))

        def out_of_mixer(w_name, z, ends, gain, area):
            h_area = Area(h_at)
            z_hi, z_lo = h_area.take(8, T, dtype=f32r), h_area.take(8, T, dtype=f32r)
            y = h_area.take(DT, T)
            t_in = []
            for k in range(8):
                t_in += split_into(z_hi[:, k, :], z_lo[:, k, :], z[:, k, :], ends, e_lo=dve if k % 2 else pool)
            sq = Ring([area.take(T) for _ in range(2)])
            sums = project_out(lambda m: [(w_name, m, 8)], [(z_hi[:, k, :], z_lo[:, k, :]) for k in range(8)],
                               T, y, sq, t_in)
            return add_normed(T, lambda j, s: col(gain, j), y, sums, area)

        def stick_breaking(x_toks):
            ends = fence()
            h, h_ready = norm(T, lambda j, s: col("l1_mix_pre", j), None, x_toks, ends, Area())
            fence()
            area = Area()
            qk, v, o_t = area.take(16, T), area.take(4, D), area.take(8, T)
            vt = Ring([area.take(T) for _ in range(2)])
            names = [("w_qkv", c) for c in range(24)]
            project(names[:16], P, h, h_ready, T, lambda m, c0, c1, b, t:
                    ts(dve, qk[:, m, :], b, HD ** -0.5 if m < 8 else 1.0, MUL, after=[t]))
            project(names[16:], P, h, h_ready, T, to_tokens(v, P, T, vt))
            ready = [act.last, dve.last, pe.last]
            for e in (act, dve, pool):
                e.wait(ready)
            area = Area(h_at)
            e_r = Ring([area.take(T) for _ in range(3)])
            sp_r = Ring([area.take(T) for _ in range(3)])
            at_r = Ring([area.take(T) for _ in range(3)])
            sums = Ring([area.take(T) for _ in range(2)])
            suffix, minus = C("suffix"), C("minus")

            def strictly_before(v, after):
                return pool.do(lambda g: g.affine_select(out=v, in_=v, compare_op=ALU.is_gt, fill=0.0, base=0,
                                                         pattern=[[1, P]], channel_multiplier=-1), after)
            for h in range(SB_HEADS):
                b0, tile = 64 * (h % 2), h // 2
                i_s, acc, afree = sums.take()
                t_acc = memset(pool, acc, 0.0, after=afree)
                i_o, bank_o, free_o = banks.take()
                for j in range(3, -1, -1):
                    q0, n = j * P, T - j * P
                    i, bank, free = banks.take()
                    z = bank[:, 0:n]
                    t = mm(z, qk[b0:b0 + 64, 8 + tile, q0:q0 + P], qk[b0:b0 + 64, tile, q0:T], True, True,
                           after=free + ready)
                    ie, e_t, efree = e_r.take()
                    isp, sp_t, spfree = sp_r.take()
                    t = fn(e_t[:, 0:n], z, ACT.Abs, after=[t] + efree)
                    t = fn(e_t[:, 0:n], e_t[:, 0:n], ACT.Exp, after=[t], scale=-1.0)
                    t = fn(e_t[:, 0:n], e_t[:, 0:n], ACT.Ln, after=[t], bias=ones[:, 0:1])
                    t = stt(sp_t[:, 0:n], z, 0.0, e_t[:, 0:n], MAX, ADD, after=[t] + spfree)
                    e_r.leave(ie, t)
                    t_sp = strictly_before(sp_t[:, 0:P], [t])
                    t = mm(z, suffix, sp_t[:, 0:n], False, j == 3, after=[t_sp], signal=True)
                    if j < 3:
                        t = mm(z[:, P:n], minus, acc[:, q0 + P:T], False, True, after=[t_acc])
                    ia, at_t, atfree = at_r.take()
                    t_acc = tt(pool, acc[:, q0:T], acc[:, q0:T], sp_t[:, 0:n], ADD, after=[t, t_acc, t_sp])
                    sp_r.leave(isp, t_acc, t)
                    t = fn(at_t[:, 0:n], z, ACT.Exp, after=[t] + atfree)
                    banks.leave(i, t)
                    t = strictly_before(at_t[:, 0:P], [t])
                    t = mm(bank_o[b0:b0 + 64, q0:T], v[:, j, h * HD:(h + 1) * HD], at_t[:, 0:n], j == 3, j == 0,
                           after=[t] + free_o, signal=True)
                    at_r.leave(ia, t)
                sums.leave(i_s, t, t_acc)
                t = copy(dve, o_t[b0:b0 + 64, tile, :], bank_o[b0:b0 + 64, :], after=[t])
                banks.leave(i_o, t)
            ends = fence()
            return out_of_mixer("l1_w_out", o_t, ends, "l1_mix_post", Area())

        stage_ends, mod_done = [], {}
        x_toks = [[x_in] for _ in range(DT)]
        plan = [("L0", lambda x: first_layer(0, TA, x)), ("L1", lambda x: first_layer(1, T, x)),
                ("F1", lambda x: ffn("l0_ffn1", 0, x)), ("M0", even_mixer), ("F2", lambda x: ffn("l0_ffn2", 1, x)),
                ("F3", lambda x: ffn("l1_ffn1", 2, x)), ("M1", stick_breaking),
                ("F4", lambda x: ffn("l1_ffn2", 3, x))]
        for name, go in plan:
            x_toks = go(x_toks)
            if upto == name:
                break
        toks = [t for ts_ in x_toks for t in ts_]
        done = sp.dma(out_dram, x_sb[:, :, 0:T], out_q, after=toks)
        sp.wait([done])

        with nc.Block() as block:
            @block.sync
            def _(e):
                sp.run(e)

            @block.tensor
            def _(e):
                pe.run(e)

            @block.vector
            def _(e):
                dve.run(e)

            @block.scalar
            def _(e):
                act.run(e)

            @block.gpsimd
            def _(e):
                pool.run(e)


def constants():
    f = np.float32
    out = np.zeros((P, N_CONST), f)

    def put(name, v):
        at, n = CONSTS[name]
        out[:v.shape[0], at:at + n] = v
    put("ident", np.eye(P, dtype=f))
    put("ones", np.ones((P, P), f))
    h = np.arange(P) // HD
    put("head_ones", (h[:, None] == h[None, :]).astype(f))
    rot = np.zeros((96, 96), f)
    half = 24
    for b in range(0, 96, half):
        for i in range(12):
            rot[b + 12 + i, b + i] = -1.0
            rot[b + i, b + 12 + i] = 1.0
    put("rot", rot)
    put("half", (np.arange(96) >= DF_QK).astype(f)[:, None])
    put("eps", np.tile(np.array([[EPS, GN_EPS]], f), (P, 1)))
    t = np.arange(T)
    inv = (f(10000.0) ** (-np.arange(0, 24, 2, dtype=f) / f(24))).astype(f)
    cs, sn = np.zeros((96, T), f), np.zeros((96, T), f)
    for q in range(2):
        for part, pos in ((0, t // GRID_W), (1, t % GRID_W)):
            ang = (pos.astype(f)[None, :] * inv[:, None]).astype(f)
            for hh in range(2):
                o = q * 48 + part * 24 + hh * 12
                cs[o:o + 12], sn[o:o + 12] = np.cos(ang), np.sin(ang)
    put("cos", cs)
    put("sin", sn)
    qc = GRID_W - 1 - np.arange(P) % GRID_W
    st = np.clip(qc - WIN_W // 2, 0, GRID_W - WIN_W)
    kc = np.arange(GRID_W)
    ok = (kc[None, :] >= st[:, None]) & (kc[None, :] < st[:, None] + WIN_W)
    put("na_mask", np.where(ok, f(0), f(NEG)).astype(f))
    i, j = np.arange(P)[:, None], np.arange(P)[None, :]
    put("upper", np.concatenate([(i < j), (i <= j)], 1).astype(f))
    put("lower", (j < i).astype(f))
    put("suffix", -(i >= j).astype(f))
    put("turn", np.kron(np.eye(2), np.eye(GRID_W)[::-1]).astype(f))
    put("minus", -np.ones((P, P), f))
    return out


def level_mask(n):
    i, j = np.arange(P)[:, None] // n, np.arange(P)[None, :] // n
    m = ((i % 2 == 1) & (j == i - 1)).astype(np.float32)
    return m, m.T


def lay_out(inp):
    f = np.float32
    I = {k: np.asarray(v) for k, v in inp.items()}
    arr = {}
    xt = np.concatenate([I["x"][0], I["ctx"][0]], 0).T
    arr["xt"] = xt.reshape(DT, P, TA).transpose(1, 0, 2)
    par = np.zeros((P, N_COLUMNS), f)

    def put(name, v, rows=P):
        at, n = COLUMNS[name]
        par[:v.shape[0], at:at + n] = v

    def cols(v):
        return v.reshape(-1, P).T
    for l in range(DEPTH):
        put(f"b_mod{l}", cols(I["b_mod"][l]))
        put(f"g_pre{l}", cols(I["g_pre"][l]))
        put(f"g_post{l}", cols(I["g_post"][l]))
        put(f"subln{l}", I["diff_subln_g"][l][:, None])
        put(f"conv_w{l}", I["conv_w"][l].reshape(TAPS, 2, P).transpose(2, 1, 0).reshape(P, 2 * TAPS))
        put(f"conv_b{l}", cols(I["conv_b"][l]))
        put(f"ln_g{l}", cols(I["conv_ln_g"][l]))
        put(f"ln_b{l}", cols(I["conv_ln_b"][l]))
        put(f"lq{l}", np.stack([I["diff_lq1"][l], I["diff_lq2"][l]], 1))
        put(f"lk{l}", np.stack([I["diff_lk1"][l], I["diff_lk2"][l]], 1))
        arr[f"w_mod{l}"] = by_columns(I["w_mod"][l], P)
        w = I["w_in"][l]
        pieces = []
        for g, at in IN_PIECE.items():
            width = GROUP // len(at)
            p = by_columns(w[:, g * GROUP:(g + 1) * GROUP], width)
            pieces.append(np.pad(p, ((0, 0), (0, 0), (0, SLOT - p.shape[2]))))
        arr[f"w_in{l}"] = np.concatenate(pieces, 0)
        wo = I["w_out"][l]
        padded = np.zeros((9, P, D), f)
        padded[0:3] = wo[0:384].reshape(3, P, D)
        padded[3:7, 0:96] = wo[384:768].reshape(4, 96, D)
        padded[7:9] = wo[768:1024].reshape(2, P, D)
        arr[f"w_out{l}"] = by_k_runs(padded, W_OUT_K)
        rp = np.zeros((NA_HEADS * 15, P), f)
        rp[:, 48:79] = I["na_rpb"][l].reshape(NA_HEADS * 15, 31)
        arr[f"rpb{l}"] = rp
    put("cond", np.stack([cols(I["c"][0]), cols(I["c_ctx"])], 2).reshape(P, 16))
    for n in ("l0_ffn1", "l0_ffn2", "l1_ffn1", "l1_ffn2", "l0_mix", "l1_mix"):
        put(n + "_pre", cols(I[n + "_pre_g_2"]))
        put(n + "_post", cols(I[n + "_post_g_2"]))
    for n in ("l0_ffn1", "l0_ffn2", "l1_ffn1", "l1_ffn2"):
        w = I[n + "_w_in_2"]
        g, u = by_columns(w[:, :D_FF], P), by_columns(w[:, D_FF:], P)
        arr[n + "_w_in"] = np.stack([g, u], 1).reshape(2 * FT, P, -1)
        w = I[n + "_w_out_2"].reshape(2, FT // 2, P, D)
        for half in range(2):
            arr[n + f"_w_out{half}"] = by_k_runs(w[half], FFN_K[:2])
    put("mu", cols(I["l0_mu_2"]))
    for a, b in (("w0", "l0_w0_2"), ("a0", "l0_a0_2"), ("k_k", "l0_k_k_2"), ("k_a", "l0_k_a_2"),
                 ("r_k", "l0_r_k_2"), ("lnx_g", "l0_lnx_g_2"), ("lnx_b", "l0_lnx_b_2"), ("rconv_b", "l0_conv_b_2"),
                 ("ga_b", "l0_gate_a_b_2"), ("gx_b", "l0_gate_x_b_2"), ("lam", "l0_lambda_2")):
        put(a, cols(I[b]))
    put("rconv_w", I["l0_conv_w_2"].reshape(4, 4, P).transpose(2, 1, 0).reshape(P, 16))
    arr["l0_w_in"] = by_columns(I["l0_w_in_2"], P)
    arr["l0_w_out"] = by_columns(I["l0_w_out_2"], P)
    arr["lora"] = np.concatenate([np.concatenate([I["l0_w2_2"], I["l0_a2_2"]], 0), I["l0_g2_2"]], 1)
    gates = [I[n].reshape(4, 2, HD, HD).transpose(1, 2, 0, 3).reshape(P, 4 * HD)
             for n in ("l0_gate_a_w_2", "l0_gate_x_w_2")]
    arr["gate_w"] = np.concatenate(gates, 1)
    arr["w_qkv"] = by_columns(I["l1_w_qkv_2"], P)
    arr["l1_w_out"] = by_columns(I["l1_w_out_2"], P)
    arr["par"] = par
    arr["const"] = constants()
    arr["levels"] = np.concatenate([m for n in LEVELS for m in level_mask(n)], 1)
    return {k: np.ascontiguousarray(v) for k, v in arr.items()}


def by_columns(w, width, parts=1):
    k, n = w.shape
    v = w.reshape(parts, k // P // parts, P, n // width, width).transpose(3, 0, 2, 1, 4)
    return v.reshape(n // width * parts, P, -1)


def by_k_runs(w, runs):
    out = np.zeros((D // P, len(runs), P, runs[0] * P), w.dtype)
    at = 0
    for i, n in enumerate(runs):
        v = w[at:at + n].reshape(n, P, D // P, P).transpose(2, 1, 0, 3)
        out[:, i, :, :n * P] = v.reshape(D // P, P, n * P)
        at += n
    return out.reshape(-1, P, runs[0] * P)


def kernel(**inputs):
    import concourse.bacc as bacc
    from concourse.bass_utils import run_bass_kernel_spmd

    arrays = lay_out(inputs)
    nc = bacc.Bacc("TRN2", target_bir_lowering=False, num_devices=1)
    ins = {n: nc.dram_tensor(f"in_{n}", a.shape, mybir.dt.float32, kind="ExternalInput").ap()
           for n, a in arrays.items()}
    out = nc.dram_tensor("out", (P, DT, T), mybir.dt.float32, kind="ExternalOutput").ap()
    build(nc, ins, out, UPTO)
    r = run_bass_kernel_spmd(nc, [{f"in_{n}": a for n, a in arrays.items()}], core_ids=[0])
    y = r.results[0]["out"]
    return np.ascontiguousarray(y.transpose(1, 0, 2).reshape(D, T).T)[None]


UPTO = None
```

```python
import math
from contextlib import ExitStack

import numpy as np
import concourse.bass as bass
from concourse import mybir

P = 128
D = 1024
DT = D // P
T = 512
TC = 256
TA = T + TC
DEPTH = 2
GRID_W = 64
NA_HEADS, NA_DH = 6, 64
NA_W = NA_HEADS * NA_DH
WIN_H, WIN_W = 8, 16
DF_HEADS, DF_QK = 4, 48
DF_V = 2 * DF_QK
GROUP = 384
IN_COLS = 3840
CONV_W, TAPS = 256, 31
PAD = TAPS // 2
CONV_TOK = PAD + T + PAD + TC + PAD
CONV_OUT = T + PAD + TC
BIAS_ROWS = 14
D_FF = 2816
FT = D_FF // P
A_W = 512
RW_HEADS = 8
HD = 64
CH = 128
NCH = T // CH
LEVELS = [1, 2, 4, 8, 16, 32, 64]
SB_HEADS = 16
EPS = 1e-6
GN_EPS = 64e-5
NEG = -1e30
SLOT = 1024
N_RAW, N_SPLIT = 3, 3
AHEAD = 2
WORK = 22300
W_OUT_K = (5, 4)
FFN_K = (6, 5)

def column_table():
    names = []
    for l in range(DEPTH):
        names += [(f"b_mod{l}", 24), (f"g_pre{l}", 8), (f"g_post{l}", 8), (f"subln{l}", 1),
                  (f"conv_w{l}", 2 * TAPS), (f"conv_b{l}", 2), (f"ln_g{l}", 2), (f"ln_b{l}", 2),
                  (f"lq{l}", 2), (f"lk{l}", 2)]
    names += [("cond", 16)]
    for f in ("l0_ffn1", "l0_ffn2", "l1_ffn1", "l1_ffn2", "l0_mix", "l1_mix"):
        names += [(f + "_pre", 8), (f + "_post", 8)]
    names += [("mu", 14), ("w0", 4), ("a0", 4), ("k_k", 4), ("k_a", 4), ("r_k", 4), ("lnx_g", 4),
              ("lnx_b", 4), ("rconv_w", 16), ("rconv_b", 4), ("ga_b", 4), ("gx_b", 4), ("lam", 4)]
    at, out = 0, {}
    for name, n in names:
        out[name] = (at, n)
        at += n
    return out, at


COLUMNS, N_COLUMNS = column_table()

CONSTS, N_CONST = {}, 0
for _name, _n in (("ident", 128), ("ones", 128), ("head_ones", 128), ("rot", 96), ("half", 1), ("eps", 2),
                  ("cos", 512), ("sin", 512), ("na_mask", 64), ("upper", 256), ("pick", 128),
                  ("suffix", 128), ("minus", 128), ("turn", 128)):
    CONSTS[_name] = (N_CONST, _n)
    N_CONST += _n


def weight_order():
    def groups(l, gs, ctx):
        for g in gs:
            for m in range(4 if g in (2, 6, 7) else 3):
                yield (f"w_in{l}", IN_PIECE[g][m], True)
    for l in range(DEPTH):
        if l == 0:
            for c in range(24):
                yield (f"w_mod{l}", c, False)
        yield from groups(l, NA_GROUPS, l == 0)
        yield from groups(l, LATE_GROUPS, l == 0)
        if l == 0:
            for c in range(24):
                yield ("w_mod1", c, False)
        for c in range(16):
            yield (f"w_out{l}", c, True)
    for name in ("l0_ffn1", "mix0", "l0_ffn2", "l1_ffn1", "mix1", "l1_ffn2"):
        if name == "mix0":
            for c in range(22):
                yield ("l0_w_in", c, True)
            for c in range(8):
                yield ("l0_w_out", c, True)
        elif name == "mix1":
            for c in range(24):
                yield ("w_qkv", c, True)
            for c in range(8):
                yield ("l1_w_out", c, True)
        else:
            for half in range(2):
                for c in range(FT):
                    yield (name + "_w_in", half * FT + c, True)
                for c in range(16):
                    yield (name + f"_w_out{half}", c, True)


IN_PIECE, _n = {}, 0
for _g in range(10):
    IN_PIECE[_g] = list(range(_n, _n + (4 if _g in (2, 6, 7) else 3)))
    _n += len(IN_PIECE[_g])
NA_GROUPS = (0, 1, 5, 4)
LATE_GROUPS = (8, 9, 2, 3, 7, 6)


class Engine:

    def __init__(self, sem):
        self.sem, self.count, self.items, self.reached = sem, 0, [], {}

    def wait(self, after):
        for tok in after:
            if tok is None:
                continue
            sem, value = tok
            if self.reached.get(id(sem), 0) < value:
                self.reached[id(sem)] = value
                self.items.append(lambda e, s=sem, v=value: e.wait_ge(s, v))

    def do(self, fn, after=(), signal=True):
        self.wait(after)
        if signal:
            self.count += 1
            self.items.append(lambda e: fn(e).then_inc(self.sem, 1))
            return (self.sem, self.count)
        self.items.append(fn)
        return None

    @property
    def last(self):
        return (self.sem, self.count) if self.count else None

    def dma(self, out, in_, queue, after=()):
        self.wait(after)
        queue[1] += 16
        s = queue[0]
        self.items.append(lambda e: e.dma_start(out, in_).then_inc(s, 16))
        return (s, queue[1])

    def run(self, e):
        for item in self.items:
            item(e)


class Ring:

    def __init__(self, buffers):
        self.buffers, self.n, self.left = buffers, 0, [()] * len(buffers)

    def take(self):
        held = 0
        while self.left[self.n % len(self.buffers)] is None:
            self.n += 1
            held += 1
            assert held < len(self.buffers), "every buffer is held"
        i = self.n % len(self.buffers)
        self.n += 1
        free, self.left[i] = self.left[i], None
        return i, self.buffers[i], list(free)

    def leave(self, i, *tokens):
        self.left[i] = tokens

    def free(self):
        return self.left[self.n % len(self.buffers)] is not None


def build(nc, ins, out_dram):
    f32, f32r = mybir.dt.float32, mybir.dt.float32r
    ALU = mybir.AluOpType
    ACT = mybir.ActivationFunctionType
    X_AXIS = mybir.AxisListType.X
    ADD, SUB, MUL, MAX, MIN = ALU.add, ALU.subtract, ALU.mult, ALU.max, ALU.min
    ctx = ExitStack()
    with ctx:
        def sb(name, shape, dtype=f32):
            return ctx.enter_context(nc.sbuf_tensor(name, shape, dtype))

        def sem(name):
            return ctx.enter_context(nc.semaphore(name))

        x_sb = sb("x_sb", [P, DT, TA])
        raw_sb = [sb(f"w_raw{i}", [P, SLOT]) for i in range(N_RAW)]
        split_sb = [(sb(f"w_hi{i}", [P, SLOT], f32r), sb(f"w_lo{i}", [P, SLOT], f32r)) for i in range(N_SPLIT)]
        const = sb("const", [P, N_CONST])
        par = sb("par", [P, N_COLUMNS])
        small = sb("small", [P, 480])
        h_at = nc.sbuf_base
        sb("h_region", [P, 2 * DT * TA])
        work_at = nc.sbuf_base
        sb("work_region", [P, WORK])
        pairs = [ctx.enter_context(nc.psum_tensor(f"banks{i}", [P, 1024], f32)) for i in range(4)]
        banks = Ring([pairs[i // 2][:, 512 * (i % 2):512 * (i % 2) + 512] for i in range(8)])


        pe, dve, act, pool, sp = (Engine(sem(n)) for n in ("s_pe", "s_dve", "s_act", "s_pool", "s_sp"))
        raws, splits = Ring(raw_sb), Ring(split_sb)
        raw_q = [[sem(f"s_raw{i}"), 0] for i in range(N_RAW)]
        const_q, par_q, x_q, out_q, gate_q, lora_q, level_q = (
            [sem(n), 0] for n in ("s_const", "s_par", "s_x", "s_out", "s_gate", "s_lora", "s_levels"))
        rpb_q = [[sem(f"s_rpb{i}"), 0] for i in range(2)]

        def C(name, rows=P):
            at, n = CONSTS[name]
            return const[0:rows, at:at + n]

        def col(name, i=0, n=1, rows=P, base=0):
            at = COLUMNS[name][0] + i
            return par[base:base + rows, at:at + n]

        ident, ones, head_ones = C("ident"), C("ones"), C("head_ones")

        class Area:
            made = 0

            def __init__(self, at=None, size=WORK):
                self.at = work_at if at is None else at
                self.end = (h_at + 4 * 2 * DT * TA) if at is not None and at < work_at else work_at + 4 * WORK

            def take(self, *shape, dtype=f32):
                Area.made += 1
                t = nc.alloc_sbuf_tensor_at(f"area{Area.made}", [P, *shape], dtype, offset=self.at)
                self.at += 4 * int(np.prod(shape))
                self.at += -self.at % 32
                assert self.at <= self.end, (self.at - self.end) / 4
                return t[tuple(slice(None) for _ in range(len(shape) + 1))]

        def h_tensors():
            area = Area(h_at)
            return area.take(DT, TA, dtype=f32r), area.take(DT, TA, dtype=f32r)

        def fence():
            ends = [e.last for e in (pe, dve, act, pool)]
            for e in (dve, act, pool):
                e.wait(ends)
            return ends

        const_in = sp.dma(const[:, :], ins["const"], const_q)
        par_in = sp.dma(par[:, :], ins["par"], par_q)
        x_in = sp.dma(x_sb[:, :, :], ins["xt"], x_q)
        loaded = [const_in, par_in]
        for e in (dve, act, pool, pe):
            e.wait(loaded)

        order = list(weight_order())
        at = {"dma": 0, "split": 0, "use": 0}
        arriving, prepared = {}, {}

        def issue_loads():
            while at["dma"] < len(order) and raws.free():
                name, index, _ = order[at["dma"]]
                dram = ins[name][index]
                i, slot, free = raws.take()
                arriving[at["dma"]] = (i, slot, sp.dma(slot[:, 0:dram.shape[-1]], dram, raw_q[i], after=free))
                at["dma"] += 1

        def split_next():
            n = at["split"]
            issue_loads()
            i, raw, tok = arriving.pop(n)
            if not order[n][2]:
                prepared[n] = ("raw", i, raw, None, [tok])
            else:
                w = ins[order[n][0]].shape[-1]
                k, (hi, lo), free = splits.take()
                t_hi = copy(act, hi[:, 0:w], raw[:, 0:w], after=[tok] + free)
                t_lo = tt(pool, lo[:, 0:w], raw[:, 0:w], hi[:, 0:w].bitcast(f32), SUB, after=[t_hi, tok] + free)
                raws.leave(i, t_lo)
                prepared[n] = ("split", k, hi, lo, [t_hi, t_lo])
            at["split"] += 1

        def load(name, index):
            n = at["use"]
            assert order[n][:2] == (name, index), (order[n], name, index)
            while at["split"] < min(n + AHEAD + 1, len(order)):
                split_next()
            issue_loads()
            at["use"] += 1
            return prepared.pop(n)

        def used(piece):
            (raws if piece[0] == "raw" else splits).leave(piece[1], pe.last)

        def mm(out, lhsT, rhs, first, last, after=(), signal=None):
            signal = last if signal is None else signal
            return pe.do(lambda e: e.matmul(out, lhsT, rhs, start=first, stop=last, skip_group_check=True),
                         after, signal)

        def mm3(out, w_hi, w_lo, z_hi, z_lo, first, last, after=(), signal=None):
            mm(out, w_hi, z_hi, first, False, after)
            mm(out, w_hi, z_lo, False, False)
            return mm(out, w_lo, z_hi, False, last, signal=signal)

        later = []

        def run_later(n=0):
            while len(later) > n:
                later.pop(0)()

        def tt(e, out, a, b, op, after=()):
            return e.do(lambda g: g.tensor_tensor(out, a, b, op), after)

        def ts(e, out, a, s1, op0, s2=None, op1=None, after=()):
            if op1 is None:
                return e.do(lambda g: g.tensor_scalar(out, a, s1, None, op0), after)
            return e.do(lambda g: g.tensor_scalar(out, a, s1, s2, op0, op1), after)

        def stt(out, a, s, b, op0, op1, after=()):
            return dve.do(lambda g: g.scalar_tensor_tensor(out, a, s, b, op0, op1), after)

        def copy(e, out, a, after=()):
            if e is act:
                return act.do(lambda g: g.activation(out, a, ACT.Copy), after)
            return e.do(lambda g: g.tensor_copy(out, a), after)

        def fn(out, a, f, after=(), scale=1.0, bias=None, accum=None):
            kw = {}
            if bias is not None:
                kw["bias"] = bias
            if accum is not None:
                kw["accum_out"] = accum
            return act.do(lambda g: g.activation(out, a, f, scale=scale, **kw), after)

        def memset(e, out, v, after=()):
            return e.do(lambda g: g.memset(out, v), after)

        def recip(out, a, after=()):
            return dve.do(lambda g: g.reciprocal(out, a), after)

        mods, gs, gp, lam_cols = [], [], [], []
        for l in range(DEPTH):
            o = 96 * l
            mods.append(small[:, o:o + 48].rearrange("p (t s) -> p t s", t=24))
            gs.append(small[:, o + 48:o + 64].rearrange("p (t s) -> p t s", t=8))
            gp.append(small[:, o + 64:o + 80].rearrange("p (t s) -> p t s", t=8))
            lam_cols.append(small[:, o + 80:o + 84])
        half_g, C8 = small[:, 192:224].rearrange("p (f j) -> p f j", f=4), 224
        stat = small[:, 256:480]

        def spans(total):
            return [(0, T), (T, TA)] if total == TA else [(0, total)]

        def mean_square(tiles, n, ring, after, rows=P):
            i, bank, free = banks.take()
            for j, tile in enumerate(tiles):
                k, sq, sfree = ring.take()
                t_sq = fn(sq[0:rows, 0:n], tile, ACT.Square, after=list(after) + sfree)
                t_mm = mm(bank[0:rows, 0:n], ones[0:rows, 0:rows], sq[0:rows, 0:n], j == 0, j == len(tiles) - 1,
                          after=[t_sq] + (free if j == 0 else []), signal=True)
                ring.leave(k, t_mm)
            return i, bank, t_mm

        def rstd_of(out, i, bank, t_mm, n, n_feat, after=(), rows=P, eps=0):
            eps_ap = const[0:rows, CONSTS["eps"][0] + eps:CONSTS["eps"][0] + eps + 1]
            t = fn(out, bank[0:rows, 0:n], ACT.Sqrt, after=[t_mm] + list(after), scale=1.0 / n_feat, bias=eps_ap)
            banks.leave(i, t)
            return recip(out, out, after=[t])

        def norm(total, gain, shift, x_toks, after, area):
            hi, lo = h_tensors()
            sq = Ring([area.take(T) for _ in range(2)])
            rs = area.take(TA)
            full = Ring([area.take(T) for _ in range(3)])
            ready = [[] for _ in range(DT)]
            for s, (c0, c1) in enumerate(spans(total)):
                w = c1 - c0
                i, bank, free = banks.take()
                for j in range(DT):
                    k, sq_t, sfree = sq.take()
                    t_sq = fn(sq_t[:, 0:w], x_sb[:, j, c0:c1], ACT.Square, after=x_toks[j] + sfree)
                    t_mm = mm(bank[:, 0:w], ones, sq_t[:, 0:w], j == 0, j == DT - 1, after=[t_sq] + free, signal=True)
                    sq.leave(k, t_mm)
                t = rstd_of(rs[:, c0:c1], i, bank, t_mm, w, D)
                for j in range(DT):
                    k, f, ffree = full.take()
                    t2 = stt(f[:, 0:w], x_sb[:, j, c0:c1], gain(j, s), rs[:, c0:c1], MUL, MUL,
                             after=[t] + x_toks[j] + ffree)
                    if shift is not None:
                        t2 = fn(f[:, 0:w], f[:, 0:w], ACT.Identity, after=[t2], bias=shift(j, s))
                    t_hi = copy(act, hi[:, j, c0:c1], f[:, 0:w], after=[t2] + list(after))
                    e = dve if j % 2 else pool
                    t_lo = tt(e, lo[:, j, c0:c1], f[:, 0:w], hi[:, j, c0:c1].bitcast(f32), SUB, after=[t_hi])
                    full.leave(k, t_lo)
                    ready[j] += [t_hi, t_lo]
            return (hi, lo), ready

        def add_normed(total, gain, y, sums, area):
            rs = area.take(TA)
            tmp = Ring([area.take(T) for _ in range(3)])
            toks = [[] for _ in range(DT)]
            for s, (c0, c1) in enumerate(spans(total)):
                t = rstd_of(rs[:, c0:c1], *sums[s], c1 - c0, D)
                for j in range(DT):
                    k, u, free = tmp.take()
                    t1 = stt(u[:, 0:c1 - c0], y[:, j, c0:c1], gain(j, s), rs[:, c0:c1], MUL, MUL, after=[t] + free)
                    e = dve if j % 3 == 0 else pool
                    t2 = tt(e, x_sb[:, j, c0:c1], x_sb[:, j, c0:c1], u[:, 0:c1 - c0], ADD, after=[t1])
                    tmp.leave(k, t2)
                    toks[j].append(t2)
            return toks

        def project(names, width, h, h_ready, total, consume):
            hi, lo = h
            for m, (name, index) in enumerate(names):
                piece = load(name, index)
                _, _, w_hi, w_lo, toks = piece
                for (c0, c1) in spans(total):
                    i, bank, free = banks.take()
                    out = bank[0:width, 0:c1 - c0]
                    for k in range(DT):
                        o = k * width
                        t = mm3(out, w_hi[:, o:o + width], w_lo[:, o:o + width], hi[:, k, c0:c1], lo[:, k, c0:c1],
                                k == 0, k == DT - 1, after=toks + h_ready[k] + (free if k == 0 else []))
                    run_later()
                    banks.leave(i, consume(m, c0, c1, out, t))
                used(piece)
            run_later()

        def to_tokens(v, width, n_tok, ring):
            def consume(m, c0, c1, b, t):
                k, vt, free = ring.take()
                t_v = copy(act, vt[0:width, 0:c1 - c0], b, after=[t] + free)

                def turn():
                    n = (c1 - c0) // P
                    i, bank, free = banks.take()
                    for q in range(n):
                        t = transpose(bank[:, q * width:(q + 1) * width], vt[0:width, q * P:(q + 1) * P],
                                      after=[t_v] + free, signal=(q == n - 1))
                    ring.leave(k, t)
                    o = v[:, c0 // P:c1 // P, m * width:(m + 1) * width]
                    banks.leave(i, copy(dve, o, bank[:, 0:n * width].rearrange("p (q w) -> p q w", q=n), after=[t]))
                later.append(turn)
                return t_v
            return consume

        def split_into(hi, lo, src, after, e_hi=None, e_lo=None):
            t_hi = copy(e_hi or act, hi, src, after=after)
            return [t_hi, tt(e_lo or pool, lo, src, hi.bitcast(f32), SUB, after=[t_hi] + list(after))]

        def project_out(names_of, k_tiles, total, y, sq, after, add=False, last=True):
            held = [banks.take() for _ in spans(total)] if last else None
            sums = [None] * len(spans(total))
            for m in range(DT):
                outs = [banks.take() for _ in spans(total)]
                k = 0
                for (name, index, n_k) in names_of(m):
                    piece = load(name, index)
                    _, _, w_hi, w_lo, toks = piece
                    for (c0, c1), (i, bank, free) in zip(spans(total), outs):
                        for kk in range(n_k):
                            z_hi, z_lo = k_tiles[k + kk]
                            r = z_hi.shape[0]
                            w = slice(kk * P, (kk + 1) * P)
                            t = mm3(bank[:, 0:c1 - c0], w_hi[0:r, w], w_lo[0:r, w], z_hi[:, c0:c1], z_lo[:, c0:c1],
                                    k + kk == 0, k + kk == len(k_tiles) - 1,
                                    after=toks + (free + list(after) if k == 0 else []), signal=(kk == n_k - 1))
                    k += n_k
                    used(piece)
                run_later()
                for s, ((c0, c1), (i, bank, free)) in enumerate(zip(spans(total), outs)):
                    yy, b = y[:, m, c0:c1], bank[:, 0:c1 - c0]
                    if add:
                        t_y = tt(dve, yy, yy, b, ADD, after=[pe.last])
                    else:
                        t_y = copy(dve, yy, b, after=[pe.last])
                    banks.leave(i, t_y)
                    if last:
                        q, sq_t, sfree = sq.take()
                        t_sq = fn(sq_t[:, 0:c1 - c0], yy, ACT.Square, after=[t_y] + sfree)

                        def add_up(m=m, s=s, n=c1 - c0, sq_t=sq_t, q=q, t_sq=t_sq):
                            i, bank, free = held[s]
                            t = mm(bank[:, 0:n], ones, sq_t[:, 0:n], m == 0, m == DT - 1, after=[t_sq] + free,
                                   signal=True)
                            sq.leave(q, t)
                            sums[s] = (i, bank, t)
                        later.append(add_up)
            run_later()
            return sums

        def transpose(out, in_, after=(), signal=False):
            k = in_.shape[0]
            return pe.do(lambda e: e.transpose(out, in_, ident[0:k, 0:k]), after, signal)

        def modulation(l, area):
            cond = area.take(8, 2)
            m_l, lam_col = mods[l], lam_cols[l]
            t_c = fn(cond, col("cond", 0, 16).rearrange("p (k s) -> p k s", k=8), ACT.Silu)
            for c in range(24):
                i, bank, free = banks.take()
                piece = load(f"w_mod{l}", c)
                for k in range(DT):
                    t = mm(bank[:, 0:2], piece[2][:, k * P:(k + 1) * P], cond[:, k, :],
                           k == 0, k == DT - 1, after=[t_c] + piece[4] + free)
                used(piece)
                t = ts(dve, m_l[:, c, :], bank[:, 0:2], col(f"b_mod{l}", c), ADD, after=[t])
                banks.leave(i, t)
                yield
            for s in range(2):
                t1 = ts(dve, gs[l][:, :, s], m_l[:, 8:16, s], 1.0, ADD, after=[t])
                t1 = tt(dve, gs[l][:, :, s], gs[l][:, :, s], col(f"g_pre{l}", 0, 8), MUL, after=[t1])
                t2 = tt(dve, gp[l][:, :, s], m_l[:, 16:24, s], col(f"g_post{l}", 0, 8), MUL)
            prod = area.take(2)
            t3 = tt(dve, prod[0:DF_QK], col(f"lq{l}", 0, 2, DF_QK), col(f"lk{l}", 0, 2, DF_QK), MUL)
            i, bank, free = banks.take()
            t3 = mm(bank[:, 0:2], ones[0:DF_QK, :], prod[0:DF_QK], True, True, after=[t3] + free)
            t3 = fn(lam_col[:, 0:2], bank[:, 0:2], ACT.Exp, after=[t3])
            banks.leave(i, t3)
            t3 = tt(dve, lam_col[:, 2:3], lam_col[:, 0:1], lam_col[:, 1:2], SUB, after=[t3])
            lam_init = 0.8 - 0.6 * math.exp(-0.3 * l)
            t3 = ts(dve, lam_col[:, 3:4], lam_col[:, 2:3], -1.0, MUL, -lam_init, ADD, after=[t3])
            t4 = ts(dve, lam_col[:, 0:1], col(f"subln{l}"), 1.0 - lam_init, MUL, after=[t3])
            mod_done[l] = [t1, t2, t3, t4]

        def banks_for_rows():
            if banks.n % 2:
                i, _, free = banks.take()
                banks.leave(i, *free)
            i, _, f1 = banks.take()
            i2, _, f2 = banks.take()
            assert i2 == i + 1 and i % 2 == 0
            return i, i2, pairs[i // 2], f1 + f2

        def attention(jobs, weights, values, pt):
            steps = [(job, n) for job in jobs for n in range(len(job[1]))]
            turned = [[] for _ in range(4)]
            pt_free, made = [], {}

            def turn(job, n):
                nonlocal pt_free
                p_tile, t_p = made.pop((job[0], job[1][n]))
                n_keys = 6 if job[2] else 2
                for j0 in range(0, n_keys, 4):
                    nj = min(4, n_keys - j0)
                    i, bank, free = banks.take()
                    for j in range(nj):
                        t = transpose(bank[:, j * P:(j + 1) * P], p_tile[:, (j0 + j) * P:(j0 + j + 1) * P],
                                      after=free + [t_p], signal=(j == nj - 1))
                    e = act if (j0 == 0 and n % 2) or (j0 and n % 2 == 0) else dve
                    t_c = copy(e, pt[:, j0:j0 + nj, n * P:(n + 1) * P],
                               bank[:, 0:nj * P].rearrange("p (j q) -> p j q", j=nj), after=[t] + pt_free)
                    banks.leave(i, t_c)
                turned[n] = [t]
                if n == len(job[1]) - 1:
                    pt_free = [values(job, n_keys, [act.last, dve.last])]

            for k in range(len(steps) + 2):
                if k >= 2:
                    turn(*steps[k - 2])
                if k < len(steps):
                    job, n = steps[k]
                    made[(job[0], job[1][n])] = weights(job, n, turned[n])

        def times_values(pt, n_q, n_keys, v_of, out_rows, out_base, t_in, finish):
            i, bank, free = banks.take()
            o = bank[out_base:out_base + out_rows, 0:n_q]
            for j in range(n_keys):
                t = mm(o, v_of(j), pt[:, j, 0:n_q], j == 0, j == n_keys - 1, after=t_in + free)
            banks.leave(i, finish(o, t))
            return t

        def all_jobs(heads, total):
            return [(h_, tiles, local) for h_ in range(heads)
                    for tiles, local in (((0, 1, 2, 3), True), ((4, 5), False)) if local or total == TA]

        def na_stage(l, total, area, mix, h, h_ready):
            kT, qT, v = area.take(3, TA), area.take(3, TA), area.take(6, NA_W)
            table = ins[f"rpb{l}"]
            flipped = Ring([area.take(BIAS_ROWS, GRID_W) for _ in range(2)])
            mask = C("na_mask").rearrange("p (a b) -> p a b", a=1).broadcast_to((P, BIAS_ROWS, GRID_W))
            bias_of = {}

            def fetch_bias(hh):
                i, rows, free = flipped.take()
                for r2 in range(2):
                    src = bass.AP(tensor=table.tensor, offset=table.offset + (hh * 15 + 1 - r2) * P,
                                  ap=[[1, GRID_W], [P, BIAS_ROWS], [1, GRID_W]])
                    t = pool.dma(rows[r2 * 64:(r2 + 1) * 64], src, rpb_q[i], after=free + stage_ends)
                bias_of[hh] = (i, rows, tt(pool, rows, rows, mask, ADD, after=[t]))
            fetch_bias(0)
            fetch_bias(1)
            p_sb = area.take(4, TA)
            vt = Ring([p_sb[:, n, 0:T] for n in range(2)])
            pt = area.take(6, T)
            names = lambda g: [(f"w_in{l}", i) for i in IN_PIECE[g]]
            project(names(0), P, h, h_ready, TA, lambda m, c0, c1, b, t: copy(act, kT[:, m, c0:c1], b, after=[t]))
            project(names(1), P, h, h_ready, TA, to_tokens(v, P, TA, vt))
            project(names(5), P, h, h_ready, total,
                    lambda m, c0, c1, b, t: fn(mix[:, m, c0:c1], b, ACT.Silu, after=[t]))
            project(names(4), P, h, h_ready, total,
                    lambda m, c0, c1, b, t: ts(dve, qT[:, m, c0:c1], b, NA_DH ** -0.5, MUL, after=[t]))
            ready = [act.last, dve.last, pe.last]
            bias = {}

            def weights(job, n, free_p):
                h_, tiles, local = job
                p, b0, q, k0 = h_ // 2, 64 * (h_ % 2), tiles[n], 0 if local else T
                st = stat[:, 4 * n:4 * n + 4]
                i1, i2, two, free = banks_for_rows()
                qq = qT[b0:b0 + 64, p, q * P:(q + 1) * P]
                if local:
                    if n == 0:
                        bias[h_] = bias_of.pop(h_)
                    i_b, rows, t_bias = bias[h_]
                    flat = rows.rearrange("p a b -> p (a b)")
                    mm(two[:, 0:T], C("turn"), flat[:, (6 - 2 * q) * GRID_W:(14 - 2 * q) * GRID_W], True, False,
                       after=free + ready + [t_bias])
                    mm(two[:, 0:T], qq, kT[b0:b0 + 64, p, 0:T], False, True)
                t = mm(two[:, T:TA], qq, kT[b0:b0 + 64, p, T:TA], True, True, after=free + ready)
                if local and n == len(tiles) - 1:
                    flipped.leave(i_b, t)
                    if h_ + 2 < NA_HEADS:
                        fetch_bias(h_ + 2)
                s = p_sb[:, n, k0:TA]
                t = dve.do(lambda g, st=st, s_=two[:, k0:TA]: g.reduce_max(st[:, 0:1], s_, X_AXIS),
                           [t] + ready + free_p)
                t = ts(dve, st[:, 3:4], st[:, 0:1], -1.0, MUL, after=[t])
                t = fn(s, two[:, k0:TA], ACT.Exp, after=[t] + free_p, bias=st[:, 3:4], accum=st[:, 1:2])
                banks.leave(i1, t)
                banks.leave(i2, t)
                t = recip(st[:, 2:3], st[:, 1:2], after=[t])
                return s, ts(dve, s, s, st[:, 2:3], MUL, after=[t])

            def values(job, n_keys, t_in):
                h_, tiles, local = job
                p, b0, c0, n_q = h_ // 2, 64 * (h_ % 2), tiles[0] * P, len(tiles) * P
                key0 = 0 if local else 4
                m = mix[b0:b0 + 64, p, c0:c0 + n_q]
                return times_values(pt, n_q, n_keys, lambda j: v[:, key0 + j, h_ * 64:(h_ + 1) * 64], 64, b0, t_in,
                                    lambda o, t: tt(dve, m, o, m, MUL, after=[t]))
            attention(all_jobs(NA_HEADS, total), weights, values, pt)

        def late_stage(l, total, area, mix, h, h_ready, mod_area):
            kd, qd = area.take(4, TA), area.take(4, TA)
            v = area.take(6, NA_W)
            u = area.take(2, CONV_TOK)
            raw = Ring([area.take(T) for _ in range(2)])
            tmp = Ring([area.take(T) for _ in range(2)])
            names = lambda g: [(f"w_in{l}", i) for i in IN_PIECE[g]]
            rot, cos, sin = C("rot", 96), C("cos", 96), C("sin", 96)
            lam_col = lam_cols[l]
            t0 = memset(dve, u, 0.0)
            starts = {0: PAD, T: PAD + T + PAD}

            def glu(base):
                def go(m, c0, c1, b, t):
                    m += base
                    at_ = starts[c0]
                    n = c1 - c0
                    if m < 2:
                        return copy(dve, u[:, m, at_:at_ + n], b, after=[t, t0])
                    if m < 4:
                        k, sg, free = raw.take()
                        t1 = fn(sg[:, 0:n], b, ACT.Sigmoid, after=[t] + free)
                        uu = u[:, m - 2, at_:at_ + n]
                        raw.leave(k, tt(dve, uu, uu, sg[:, 0:n], MUL, after=[t1, dve.last]))
                        return t1
                    return fn(mix[:, 3 + m, c0:c1], b, ACT.Silu, after=[t])
                return go

            def roped(dst):
                def consume(m, c0, c1, b, t):
                    if c0 >= T:
                        return copy(act, dst[0:96, m, c0:c1], b, after=[t])
                    r, raw_t, rfree = raw.take()
                    t_raw = copy(act, raw_t[0:96], b, after=[t] + rfree)

                    def turn():
                        k, tmp_t, ufree = tmp.take()
                        i, bank, free = banks.take()
                        t1 = mm(bank[0:96, 0:T], rot, raw_t[0:96], True, True, after=[t_raw] + free)
                        t1 = tt(dve, tmp_t[0:96], bank[0:96, 0:T], sin, MUL, after=[t1] + ufree)
                        banks.leave(i, t1)
                        t2 = tt(pool, dst[0:96, m, 0:T], raw_t[0:96], cos, MUL, after=[t_raw])
                        raw.leave(r, t2, t1)
                        t3 = tt(pool, dst[0:96, m, 0:T], dst[0:96, m, 0:T], tmp_t[0:96], ADD, after=[t1, t2])
                        tmp.leave(k, t3)
                    later.append(turn)
                    return t_raw
                return consume

            project(names(8), P, h, h_ready, total, glu(0))
            project(names(9), P, h, h_ready, total, glu(3))
            t_u = [dve.last]
            project(names(2), DF_V, h, h_ready, TA, roped(kd))
            project(names(3), P, h, h_ready, TA, to_tokens(v, P, TA, raw))
            project(names(7), DF_V, h, h_ready, total,
                    lambda m, c0, c1, b, t: fn(mix[0:96, 3 + m, c0:c1], b, ACT.Silu, after=[t]))
            project(names(6), DF_V, h, h_ready, total, roped(qd))
            ready = [act.last, dve.last, pool.last, pe.last]
            area = Area(h_at)
            p1, p2 = area.take(4, TA), Ring([area.take(TA) for _ in range(2)])
            pt, q2, y = area.take(6, T), area.take(TA), area.take(2, CONV_OUT)
            sq = Ring([tmp.buffers[0]])
            rs, o_sb = raw.buffers[0], raw.buffers[1]
            half = const[0:96, CONSTS["half"][0]:CONSTS["half"][0] + 1]
            scale = DF_QK ** -0.5
            n_y = T if total == T else CONV_OUT
            other = modulation(1, mod_area) if l == 0 else iter(())

            def taps():
                last = [None, None]
                for k in range(TAPS):
                    for m in range(2):
                        yy = y[:, m, 0:n_y]
                        if k == 0:
                            last[m] = ts(dve, yy, u[:, m, 0:n_y], col(f"conv_w{l}", m * TAPS), MUL,
                                         col(f"conv_b{l}", m), ADD, after=t_u + ready)
                        else:
                            last[m] = stt(yy, u[:, m, k:k + n_y], col(f"conv_w{l}", m * TAPS + k), yy, MUL, ADD,
                                          after=[last[m]])
                        yield
            taps = taps()

            def fill(n):
                for _ in range(n):
                    next(taps, None)

            n_steps = DF_HEADS * (6 if total == TA else 4)
            t_q2 = None

            def weights(job, n, free_p):
                nonlocal t_q2
                h_, tiles, local = job
                q, k0 = tiles[n], 0 if local else T
                if local and n == 0:
                    t_q2 = ts(dve, q2[0:96, 0:total], qd[0:96, h_, 0:total], half, MUL, after=ready + [pe.last])
                done = []
                pi, p2_t, p2_free = p2.take()
                s1, s2 = p1[:, n, k0:TA], p2_t[:, k0:TA]
                for w_, (dst, qq, kk, fr) in enumerate(((s1, qd[0:48, h_], kd[0:48, h_], free_p),
                                                        (s2, q2[0:96], kd[0:96, h_], p2_free))):
                    st = stat[:, 32 * w_ + 4 * n:32 * w_ + 4 * n + 4]
                    i1, i2, two, free = banks_for_rows()
                    for (a, b) in ([(0, T)] if local else []) + [(T, TA)]:
                        t = mm(two[:, a:b], qq[:, q * P:(q + 1) * P], kk[:, a:b], True, True,
                               after=free + ready + [t_q2])
                    t = dve.do(lambda g, st=st, s_=two[:, k0:TA]: g.reduce_max(st[:, 0:1], s_, X_AXIS), [t])
                    t = ts(dve, st[:, 3:4], st[:, 0:1], -scale, MUL, after=[t])
                    t = fn(dst, two[:, k0:TA], ACT.Exp, after=[t] + list(fr), scale=scale, bias=st[:, 3:4],
                           accum=st[:, 1:2])
                    banks.leave(i1, t)
                    banks.leave(i2, t)
                    fill(-(-TAPS // n_steps))
                    done.append(recip(st[:, 2:3], st[:, 1:2], after=[t]))
                st, st2 = stat[:, 4 * n:4 * n + 4], stat[:, 32 + 4 * n:36 + 4 * n]
                t = ts(dve, s1, s1, st[:, 2:3], MUL, after=[done[0]])
                t2 = tt(dve, st2[:, 3:4], st2[:, 2:3], lam_col[:, 3:4], MUL, after=[done[1]])
                t = stt(s1, s2, st2[:, 3:4], s1, MUL, ADD, after=[t, t2])
                p2.leave(pi, t)
                next(other, None)
                return s1, t

            def values(job, n_keys, t_in):
                h_, tiles, local = job
                c0, n_q, key0 = tiles[0] * P, len(tiles) * P, 0 if local else 4

                def finish(o, t):
                    t_o = copy(act, o_sb[0:96, 0:n_q], o, after=[t, dve.last])

                    def rest():
                        b = mean_square([o_sb[0:96, 0:n_q]], n_q, sq, [t_o], rows=96)
                        t2 = rstd_of(rs[0:96, 0:n_q], *b, n_q, DF_V, rows=96, after=[dve.last])
                        t2 = stt(rs[0:96, 0:n_q], o_sb[0:96, 0:n_q], lam_col[0:96, 0:1], rs[0:96, 0:n_q], MUL, MUL,
                                 after=[t2])
                        m = mix[0:96, 3 + h_, c0:c0 + n_q]
                        tt(dve, m, rs[0:96, 0:n_q], m, MUL, after=[t2])
                    later.append(rest)
                    return t_o
                run_later()
                return times_values(pt, n_q, n_keys, lambda j: v[:, key0 + j, h_ * 96:(h_ + 1) * 96], 96, 0, t_in,
                                    finish)
            attention(all_jobs(DF_HEADS, total), weights, values, pt)
            run_later()
            for _ in other:
                pass
            fill(2 * TAPS)
            sq = Ring(tmp.buffers)
            rs = raw.buffers[0]
            for (c0, c1) in spans(total):
                w = c1 - c0
                at_ = 0 if c0 == 0 else T + PAD
                i, bank, free = banks.take()
                for m in range(2):
                    tm = mm(bank[:, 0:w], ones, y[:, m, at_:at_ + w], m == 0, m == 1, after=[dve.last] + free)
                ts_ = []
                for m in range(2):
                    ts_.append(stt(y[:, m, at_:at_ + w], bank[:, 0:w], -1.0 / CONV_W, y[:, m, at_:at_ + w], MUL, ADD,
                                   after=[tm]))
                banks.leave(i, ts_[1])
                b = mean_square([y[:, m, at_:at_ + w] for m in range(2)], w, sq, ts_ + [dve.last])
                t = rstd_of(rs[:, 0:w], *b, w, CONV_W, after=[dve.last])
                for m in range(2):
                    yy = y[:, m, at_:at_ + w]
                    t1 = stt(yy, yy, col(f"ln_g{l}", m), rs[:, 0:w], MUL, MUL, after=[t])
                    t1 = fn(yy, yy, ACT.Silu, after=[t1], bias=col(f"ln_b{l}", m))
                    tt(dve, mix[:, 7 + m, c0:c1], yy, mix[:, 7 + m, c0:c1], MUL, after=[t1])

        def first_layer(l, total, x_toks):
            nonlocal stage_ends
            stage_ends = fence()
            base = Area()
            mod_area = Area(base.at)
            mod_area.take(8, 2), mod_area.take(2)
            base.at = mod_area.at
            if l == 0:
                for _ in modulation(0, Area()):
                    pass
            mix = base.take(9, TA)
            h, h_ready = norm(TA, lambda j, s: gs[l][:, j, s:s + 1], lambda j, s: mods[l][:, j, s:s + 1],
                              [t + mod_done[l] for t in x_toks], stage_ends, Area(base.at))
            stage_ends = fence()
            na_stage(l, total, Area(base.at), mix, h, h_ready)
            stage_ends = fence()
            late_stage(l, total, Area(base.at), mix, h, h_ready, Area())
            ends = fence()
            h_area = Area(h_at)
            rows = [P] * 3 + [96] * 4 + [P] * 2
            m_hi, m_lo = h_area.take(9, total, dtype=f32r), None
            if h_area.at + 4 * 9 * total <= h_area.end:
                m_lo = h_area.take(9, total, dtype=f32r)
            area = Area(base.at)
            if m_lo is None:
                m_lo = area.take(9, total, dtype=f32r)
            y = area.take(DT, total)
            sq = Ring([area.take(T) for _ in range(2)])
            k_tiles, t_in = [], []
            for i, r in enumerate(rows):
                t_in += split_into(m_hi[0:r, i, :], m_lo[0:r, i, :], mix[0:r, i, 0:total], ends,
                                   e_lo=dve if i % 2 else pool)
                k_tiles.append((m_hi[0:r, i, :], m_lo[0:r, i, :]))

            def names_of(m):
                return [(f"w_out{l}", 2 * m, W_OUT_K[0]), (f"w_out{l}", 2 * m + 1, W_OUT_K[1])]
            sums = project_out(names_of, k_tiles, total, y, sq, t_in)
            return add_normed(total, lambda j, s: gp[l][:, j, s:s + 1], y, sums, Area(base.at - 4 * 9 * TA))

        def ffn(name, f, x_toks):
            ends = fence()
            t_half = ts(dve, half_g[:, f, :], col(name + "_post", 0, 8), 0.5, MUL)
            area = Area()
            n_half = FT // 2
            a_hi, a_lo, y = area.take(n_half, T, dtype=f32r), area.take(n_half, T, dtype=f32r), area.take(DT, T)
            mark = area.at
            h, h_ready = norm(T, lambda j, s: col(name + "_pre", j), None, x_toks, ends, Area())
            fence()
            area = Area(mark)
            sg = Ring([area.take(T) for _ in range(2)])
            act_r = Ring([area.take(T) for _ in range(2)])
            sq = Ring([area.take(T) for _ in range(2)])
            for half in range(2):
                gate = {}

                def consume(m, c0, c1, b, t):
                    j = m // 2
                    if m % 2 == 0:
                        r, sg_t, free = sg.take()
                        gate[j] = (r, sg_t, fn(sg_t, b, ACT.Silu, after=[t] + free))
                        return gate[j][2]
                    r, sg_t, t1 = gate.pop(j)
                    k, a_t, free = act_r.take()
                    t2 = tt(dve, a_t, b, sg_t, MUL, after=[t, t1] + free)
                    sg.leave(r, t2)
                    t_hi = copy(dve, a_hi[:, j, :], a_t, after=[t2] + a_free)
                    t_lo = tt(dve, a_lo[:, j, :], a_t, a_hi[:, j, :].bitcast(f32), SUB, after=[t_hi] + a_free)
                    act_r.leave(k, t_lo)
                    return t2
                a_free = [pe.last]
                project([(name + "_w_in", half * FT + c) for c in range(FT)], P, h, h_ready, T, consume)
                sums = project_out(lambda m: [(name + f"_w_out{half}", 2 * m, FFN_K[0]),
                                              (name + f"_w_out{half}", 2 * m + 1, FFN_K[1])],
                                   [(a_hi[:, k, :], a_lo[:, k, :]) for k in range(n_half)], T, y, sq, [dve.last],
                                   add=(half == 1), last=(half == 1))
            return add_normed(T, lambda j, s: half_g[:, f, j:j + 1], y, sums, Area(mark))

        def even_mixer(x_toks):
            ends = fence()
            h, h_ready = norm(T, lambda j, s: col("l0_mix_pre", j), None, x_toks, ends, Area())
            fence()
            area = Area()
            pa = area.take(14, T + 1)
            mixed = area.take(8, T)
            z = memset(pool, pa[:, :, 0:1], 0.0)
            at_rw = area.at
            tmp = Ring([area.take(T) for _ in range(2)])

            def into_pa(base):
                def go(m, c0, c1, b, t):
                    i = base + m
                    t = copy(act, pa[:, i, 1:T + 1], b, after=[t])
                    r, d, free = tmp.take()
                    t1 = tt(pool, d, pa[:, i, 0:T], pa[:, i, 1:T + 1], SUB, after=[t, z] + free)
                    t2 = stt(pa[:, i, 1:T + 1], d, col("mu", i), pa[:, i, 1:T + 1], MUL, ADD, after=[t1])
                    tmp.leave(r, t2)
                    return t
                return go
            names = [("l0_w_in", c) for c in range(22)]
            project(names[:14], P, h, h_ready, T, into_pa(0))
            project(names[14:], P, h, h_ready, T,
                    lambda m, c0, c1, b, t: copy(act if m % 2 else dve, mixed[:, m, :], b, after=[t]))
            t_pa = [act.last, dve.last, pool.last]

            ends = fence()
            h_area = Area(h_at)
            ar = h_area.take(2, 4, T)
            b_t, k_t = h_area.take(4, T), h_area.take(4, T)
            v_c = h_area.take(A_W)
            lora = h_area.take(2, T)
            state, state_mid = h_area.take(4, HD), h_area.take(4, HD)
            gw = h_area.take(2, 4 * HD)
            xc, a_t, u_t = (h_area.take(T) for _ in range(3))
            w2, a2, g2 = lora[0:64, 0, :], lora[64:128, 0, :], lora[:, 1, :]
            area = Area(at_rw)
            glo = area.take(T)
            tot = area.take(4, 3 * NCH)
            levels = area.take(14, P)
            tok_l = sp.dma(lora.rearrange("p a b -> p (a b)"), ins["lora"], lora_q, after=ends)
            t_gw = sp.dma(gw.rearrange("p a b -> p (a b)"), ins["gate_w"], gate_q, after=ends)
            tok_v = sp.dma(levels.rearrange("p a b -> p (a b)"), ins["levels"], level_q, after=ends)

            lam = col("lam", 0, 4)
            c8 = small[:, C8:C8 + 16]
            t = fn(c8[:, 0:4], lam, ACT.Abs)
            t = fn(c8[:, 0:4], c8[:, 0:4], ACT.Exp, after=[t], scale=-1.0)
            t = fn(c8[:, 0:4], c8[:, 0:4], ACT.Ln, after=[t], bias=ones[:, 0:1])
            t1 = ts(dve, c8[:, 4:8], lam, -1.0, MUL, 0.0, MAX)
            t1 = tt(dve, c8[:, 8:12], c8[:, 0:4], c8[:, 4:8], ADD, after=[t, t1])
            t_c8 = ts(dve, c8[:, 12:16], c8[:, 8:12], -8.0, MUL, after=[t1])

            def rglru(free):
                tm = pa[:, 13, 1:T + 1]
                t_end = list(free)
                for p in range(4):
                    xb, gb = mixed[:, p, :], mixed[:, 4 + p, :]
                    t = ts(dve, xc, xb, col("rconv_w", 4 * p + 3), MUL, col("rconv_b", p), ADD, after=t_end)
                    yield
                    for k in range(3):
                        s = 3 - k
                        t = stt(xc[:, s:T], xb[:, 0:T - s], col("rconv_w", 4 * p + k), xc[:, s:T], MUL, ADD,
                                after=[t])
                        yield
                    outs = []
                    for g, bias in ((0, "ga_b"), (1, "gx_b")):
                        i, bank, bfree = banks.take()
                        for b0 in (0, 64):
                            tg = mm(bank[b0:b0 + 64, :], gw[b0:b0 + 64, g, p * HD:(p + 1) * HD], xc[b0:b0 + 64],
                                    True, True, after=[t, t_gw] + bfree)
                        tg = fn(a_t if g == 0 else u_t, bank[:, :], ACT.Sigmoid, after=[tg] + t_end, bias=col(bias, p))
                        banks.leave(i, tg)
                        outs.append(tg)
                    yield
                    t1 = ts(dve, a_t, a_t, c8[:, 12 + p:13 + p], MUL, after=outs + [t_c8])
                    t5 = tt(dve, u_t, u_t, xc, MUL, after=[outs[1]])
                    t2 = fn(tm, a_t, ACT.Tanh, after=[t1] + t_end, scale=-1.0)
                    t3 = fn(a_t, a_t, ACT.Exp, after=[t2])
                    yield
                    t4 = tt(dve, xb, a_t, a_t, MUL, after=[t3])
                    yield
                    t4 = stt(tm, xb, 1.0, tm, ADD, MUL, after=[t4, t2])
                    t4 = fn(tm, tm, ACT.Sqrt, after=[t4])
                    yield
                    t5 = tt(dve, u_t, u_t, tm, MUL, after=[t4, t5])
                    yield
                    t5 = dve.do(lambda g_, o=xb, a=a_t, b=u_t: g_.tensor_tensor_scan(o, a, b, 0.0, MUL, ADD),
                                [t5, t3])
                    t6 = fn(tm, gb, ACT.Square, after=[t5])
                    yield
                    t6 = ts(dve, tm, tm, 0.044715, MUL, 1.0, ADD, after=[t6])
                    yield
                    t6 = tt(dve, tm, tm, gb, MUL, after=[t6])
                    t6 = fn(tm, tm, ACT.Tanh, after=[t6], scale=math.sqrt(2.0 / math.pi))
                    yield
                    t6 = stt(tm, tm, 1.0, gb, ADD, MUL, after=[t6])
                    yield
                    t6 = stt(gb, tm, 0.5, xb, MUL, MUL, after=[t6])
                    t_end = [t6]
                    yield

            chunk_at = area.at
            lo, root = area.take(T), area.take(T)
            wt, at_ = area.take(4, T), area.take(4, T)
            start = area.take(NCH, CH + 1)
            decays = [(area.take(NCH, CH + 1), area.take(NCH, CH + 1)) for _ in range(2)]
            pick = C("pick")
            t_start = memset(pool, start, 0.0)
            t_start = memset(pool, start[:, :, 0:1], 1.0, after=[t_start])
            t_lo = [fn(lo[0:64], pa[0:64, 12, 1:T + 1], ACT.Tanh), copy(act, lo[64:128], pa[64:128, 12, 1:T + 1])]
            t_glo = fn(glo, pa[:, 13, 1:T + 1], ACT.Sigmoid)
            t_w, t_a, t_kk, t_sq = [], [], [], []
            for p in range(4):
                i, bank, free = banks.take()
                t = mm(bank[:, :], w2[:, p * P:(p + 1) * P], lo[0:64], True, True, after=free + [tok_l] + t_lo)
                t_w.append(fn(wt[:, p, :], bank[:, :], ACT.Sigmoid, after=[t], bias=col("w0", p)))
                banks.leave(i, t_w[p])
                i, bank, free = banks.take()
                t = mm(bank[:, :], a2[:, p * P:(p + 1) * P], lo[64:128], True, True, after=free)
                t_a.append(fn(at_[:, p, :], bank[:, :], ACT.Sigmoid, after=[t], bias=col("a0", p)))
                banks.leave(i, t_a[p])
                t_kk.append(ts(dve, b_t[:, p, :], pa[:, 4 + p, 1:T + 1], col("k_k", p), MUL))
                t_sq.append(fn(k_t[:, p, :], b_t[:, p, :], ACT.Square, after=[t_kk[p]]))

            def per_head(src, after):
                i, bank, free = banks.take()
                for p in range(4):
                    t = mm(bank[32 * p:32 * p + 32, :], head_ones[:, 48:80], src(p), True, True,
                           after=free + [after[p]], signal=True)
                return i, bank, t

            def to_heads(v, p, after):
                i, bank, free = banks.take()
                return i, bank, mm(bank[:, :], pick[32 * p:32 * p + 32, :], v[32 * p:32 * p + 32], True, True,
                                   after=free + after)
            i, bank, t = per_head(lambda p: k_t[:, p, :], t_sq)
            t = fn(root, bank[:, :], ACT.Sqrt, after=[t])
            banks.leave(i, t)
            t = ts(dve, root, root, 1e-12, MAX, after=[t])
            t = recip(root, root, after=[t])
            for p in range(4):
                i, bank, t2 = to_heads(root, p, [t])
                t_kk[p] = tt(dve, b_t[:, p, :], b_t[:, p, :], bank[:, :], MUL, after=[t2])
                banks.leave(i, t_kk[p])

            def by_chunk(v):
                return v.rearrange("p (c n) -> p c n", c=NCH)

            def each_token(v):
                return v.rearrange("p (c n) -> p c n", n=1).broadcast_to((P, NCH, CH + 1))
            d_free = [[], []]
            for p in range(4):
                r, k, v = (pa[:, 4 * q + p, 1:T + 1] for q in range(3))
                dec, inv = decays[p % 2]
                kk, a_p = b_t[:, p, :], at_[:, p, :]
                t_zero = memset(pool, dec[:, :, 0:1], 0.0, after=d_free[p % 2])
                t = fn(dec[:, :, 1:CH + 1], by_chunk(wt[:, p, :]), ACT.Exp, after=[t_w[p]] + d_free[p % 2],
                       scale=-math.exp(-0.5))
                t = dve.do(lambda g, d=dec.rearrange("p c n -> p (c n)"): g.tensor_tensor_scan(
                    d, d, start.rearrange("p c n -> p (c n)"), 0.0, MUL, ADD), [t, t_start, t_zero])
                mid, end, inv_mid = (tot[:, p, n * NCH:(n + 1) * NCH] for n in range(3))
                t1 = copy(dve, mid, dec[:, :, CH // 2], after=[t])
                t1 = recip(inv_mid, mid, after=[t1])
                t3 = tt(dve, dec, dec, each_token(inv_mid), MUL, after=[t1])
                t4 = recip(inv, dec, after=[t3] + d_free[p % 2])
                t5 = copy(dve, end, dec[:, :, CH], after=[t3])
                t9 = tt(pool, by_chunk(ar[:, 1, p, :]), by_chunk(r), dec[:, :, 1:CH + 1], MUL, after=[t3])
                t8 = stt(by_chunk(ar[:, 0, p, :]), by_chunk(kk), -1.0, dec[:, :, 0:CH], MUL, MUL, after=[t_kk[p], t3])
                t11 = tt(pool, kk, kk, a_p, MUL, after=[t8, t_a[p]])
                t12 = tt(pool, by_chunk(kk), by_chunk(kk), inv[:, :, 1:CH + 1], MUL, after=[t4, t11])
                t13 = ts(dve, a_p, a_p, -1.0, ADD, col("k_a", p), MUL, after=[t11])
                t13 = stt(k, a_p, 1.0, k, ADD, MUL, after=[t13])
                t14 = tt(dve, by_chunk(k_t[:, p, :]), by_chunk(k), inv[:, :, 1:CH + 1], MUL, after=[t4, t13])
                t15 = stt(r, r, col("r_k", p), k, MUL, MUL, after=[t13, t9])
                i, bank, free = banks.take()
                t15 = mm(bank[:, :], head_ones, r, True, True, after=free + [t15])
                t15 = tt(dve, r, bank[:, :], v, MUL, after=[t15])
                banks.leave(i, t15)
                d_free[p % 2] = [t5, t9, t12, t14, t8]
            ends = fence()
            area = Area(chunk_at)
            x_m, xt_m, m_ab_t, m_ak_t, m_rb_t, m_rk_t, t1_m = (area.take(8, P) for _ in range(7))
            k_area = pa[:, 4:8, 1:T + 1]
            b_tok, k_tok = k_area[:, 0, :], k_area[:, 1, :]
            sa, rhs = k_area[:, 2, :], k_area[:, 3, :]
            m_off = Ring([area.take(4, P) for _ in range(2)])
            upper = C("upper").rearrange("p (a b) -> p a b", a=2)
            for e in (dve, pool):
                e.wait([tok_v])
            lv = lambda n, tr: levels[:, 2 * n + tr, :]
            t_s = memset(dve, state, 0.0)
            beside = rglru(ends)

            def fill(n=1):
                for _ in range(n):
                    next(beside, None)

            def v_tok(h):
                return v_c[:, h * HD:(h + 1) * HD]

            def slot_of(h):
                return 4 * (h % 2) + h // 2

            def rep(m, n):
                return m.rearrange("p (a b) -> p a b", a=1).broadcast_to((P, n, P))

            def halves(v, n, odd):
                return v.rearrange("p g (a t n) -> p g a t n", t=2, n=n)[:, :, :, odd, :]

            def packed(bank, n):
                return bank[:, 0:256].rearrange("p (g a n) -> p g a n", g=4, n=n)

            for c in range(NCH):
                cs = slice(c * CH, (c + 1) * CH)
                for e in (act, dve, pool):
                    e.wait([pe.last])
                for src, dst in ((lambda p: pa[:, 8 + p, 1 + c * CH:1 + (c + 1) * CH], v_c),
                                 (lambda p: b_t[:, p, cs], b_tok), (lambda p: k_t[:, p, cs], k_tok)):
                    i, bank, free = banks.take()
                    for p in range(4):
                        t = transpose(bank[:, p * P:(p + 1) * P], src(p), after=free + ends, signal=(p == 3))
                    t2 = copy(act, dst, bank[:, :], after=[t])
                    banks.leave(i, t2)
                t_tok = t2
                t_m = {}

                def masked(left, m1, m2, half):
                    for odd in range(2):
                        i, bank, free = banks.take()
                        b0 = 64 * odd
                        for n in range(2):
                            pair = 2 * half + n
                            t = mm(bank[:, n * 256:(n + 1) * 256].rearrange("p (a b) -> p a b", a=2),
                                   left[b0:b0 + 64, pair, cs], ar[b0:b0 + 64, :, pair, cs], True, True,
                                   after=free + ends)
                        v4 = bank[:, :].rearrange("p (n a b) -> p n a b", n=2, a=2)
                        at4 = 4 * odd + 2 * half
                        for a_, m in ((0, m1), (1, m2)):
                            t2 = tt(dve, m[:, at4:at4 + 2, :], v4[:, :, a_, :], rep(upper[:, a_, :], 2), MUL,
                                    after=[t])
                        banks.leave(i, t2)
                        t_m[odd] = t2
                for half in range(2):
                    masked(b_t, m_ab_t, m_rb_t, half)
                t_xs = [None, None]
                for g in range(2):
                    i, bank, free = banks.take()
                    for n in range(4):
                        b0 = 64 * g
                        t = mm(bank[:, n * P:(n + 1) * P], ar[b0:b0 + 64, 0, n, cs], b_t[b0:b0 + 64, n, cs],
                               True, True, after=free)
                    xs, xts = x_m[:, 4 * g:4 * g + 4, :], xt_m[:, 4 * g:4 * g + 4, :]
                    t = tt(dve, xs, bank[:, :].rearrange("p (n b) -> p n b", n=4), rep(lv(0, 0), 4), MUL, after=[t])
                    banks.leave(i, t)
                    t = tt(dve, xs, xs, rep(ident, 4), ADD, after=[t])
                    t = tt(dve, xts, m_ab_t[:, 4 * g:4 * g + 4, :], rep(lv(0, 1), 4), MUL, after=[t_m[g]])
                    t_xs[g] = tt(dve, xts, xts, rep(ident, 4), ADD, after=[t])
                for half in range(2):
                    masked(k_t, m_ak_t, m_rk_t, half)
                for n_l in range(1, 7):
                    size = 2 ** n_l
                    t_c = [None, None]
                    for g in range(2):
                        gs4 = slice(4 * g, 4 * g + 4)
                        r_, off, ofree = m_off.take()
                        t_off = tt(pool, off, m_ab_t[:, gs4, :], rep(lv(n_l, 1), 4), MUL, after=[t_m[g]] + ofree)
                        i, bank, free = banks.take()
                        for n in range(4):
                            t = mm(bank[:, n * P:(n + 1) * P], off[:, n, :], x_m[:, 4 * g + n, :], True, True,
                                   after=free + [t_off, t_xs[g]])
                        m_off.leave(r_, pe.last)
                        t_c[g] = copy(act, t1_m[:, gs4, :], bank[:, :].rearrange("p (n b) -> p n b", n=4), after=[t])
                        banks.leave(i, t_c[g])
                    for g in range(2):
                        gs4 = slice(4 * g, 4 * g + 4)
                        one = lambda n: slice(4 * g + n, 4 * g + n + 1)
                        if n_l < 6:
                            i3, bank3, free3 = banks.take()
                            for n in range(4):
                                t3 = mm(packed(bank3, size)[:, n], xt_m[:, 4 * g + n, :],
                                        halves(t1_m[:, one(n), :], size, 0)[:, 0], True, True, after=free3 + [t_c[g]])
                            xe = halves(x_m[:, gs4, :], size, 0)
                            t3 = tt(dve, xe, xe, packed(bank3, size), ADD, after=[t3, t_xs[g]])
                            banks.leave(i3, t3)
                        i2, bank2, free2 = banks.take()
                        for n in range(4):
                            t = mm(packed(bank2, size)[:, n], t1_m[:, 4 * g + n, :],
                                   halves(xt_m[:, one(n), :], size, 1)[:, 0], True, True, after=free2 + [t_c[g]])
                        xo = halves(xt_m[:, gs4, :], size, 1)
                        t_xs[g] = tt(dve, xo, xo, packed(bank2, size), ADD, after=[t, t_xs[g]])
                        banks.leave(i2, t_xs[g])
                        fill()
                for p in range(4):
                    t_sm = ts(dve, state_mid[:, p, :], state[:, p, :], tot[:, p, c:c + 1], MUL, after=[t_s])
                t_r = []
                for odd in range(2):
                    i, bank, free = banks.take()
                    b0 = 64 * odd
                    for n in range(4):
                        o = bank[:, n * HD:(n + 1) * HD]
                        mm(o, ar[b0:b0 + 64, 0, n, cs], state_mid[b0:b0 + 64, n, :], True, False,
                           after=free + [t_sm, t_tok, t_m[1]])
                        t = mm(o, m_ak_t[:, 4 * odd + n, :], v_tok(2 * n + odd), False, True)
                    t = copy(act, rhs[:, 256 * odd:256 * odd + 256], bank[:, 0:256], after=[t])
                    t_r.append(t)
                    banks.leave(i, t)
                fill()
                i, bank, free = banks.take()
                for h in range(8):
                    t2 = mm(bank[:, h * HD:(h + 1) * HD], xt_m[:, h, :], rhs[:, h * HD:(h + 1) * HD], True, True,
                            after=free + t_r + t_xs)
                t_sa = copy(act, sa, bank[:, :], after=[t2])
                banks.leave(i, t_sa)
                i2, bank2, free2 = banks.take()
                for h in range(8):
                    b0 = 64 * (h % 2)
                    o = bank2[b0:b0 + 64, (h // 2) * HD:(h // 2 + 1) * HD]
                    m_h = slot_of(h)
                    mm(o, k_tok[:, h * HD:(h + 1) * HD], v_tok(h), True, False, after=free2)
                    t_n = mm(o, b_tok[:, h * HD:(h + 1) * HD], sa[:, m_h * HD:(m_h + 1) * HD], False, True, after=[t_sa])
                t_s = tt(dve, state, state_mid, bank2[:, 0:256].rearrange("p (a b) -> p a b", a=4), ADD, after=[t_n])
                banks.leave(i2, t_s)
                for p in range(4):
                    t_s2 = ts(dve, state[:, p, :], state[:, p, :], tot[:, p, NCH + c:NCH + c + 1], MUL, after=[t_s])
                t_s = t_s2
                i, bank, free = banks.take()
                for h in range(8):
                    b0 = 64 * (h % 2)
                    o = bank[b0:b0 + 64, (h // 2) * P:(h // 2 + 1) * P]
                    mm(o, state_mid[b0:b0 + 64, h // 2, :], ar[b0:b0 + 64, 1, h // 2, cs], True, False, after=free)
                    m_h = slot_of(h)
                    mm(o, sa[:, m_h * HD:(m_h + 1) * HD], m_rb_t[:, m_h, :], False, False)
                    t_y = mm(o, v_tok(h), m_rk_t[:, m_h, :], False, True)
                t = copy(act, pa[:, 8:12, 1 + c * CH:1 + (c + 1) * CH], bank[:, :].rearrange("p (a b) -> p a b", a=4),
                         after=[t_y])
                banks.leave(i, t)
            fill(100)
            y_at = lambda p: pa[:, 8 + p, 1:T + 1]
            ends = fence()
            sq = [x_m[:, 0:4, :], x_m[:, 4:8, :], xt_m[:, 0:4, :], xt_m[:, 4:8, :]]
            sq = [v.rearrange("p a b -> p (a b)") for v in sq]
            root = t1_m[:, 0:4, :].rearrange("p a b -> p (a b)")
            t_sq = []
            for p in range(4):
                i, bank, free = banks.take()
                t = mm(bank[:, :], head_ones, y_at(p), True, True, after=free + ends)
                t = stt(y_at(p), bank[:, :], -1.0 / HD, y_at(p), MUL, ADD, after=[t])
                banks.leave(i, t)
                t_sq.append(fn(sq[p], y_at(p), ACT.Square, after=[t]))
            i, bank, t = per_head(lambda p: sq[p], t_sq)
            t_rs = rstd_of(root, i, bank, t, T, HD, eps=1)
            for p in range(4):
                m = mixed[:, p, :]
                i, bank, t = to_heads(root, p, [t_rs])
                t = tt(dve, m, bank[:, :], y_at(p), MUL, after=[t])
                banks.leave(i, t)
                t = ts(dve, m, m, col("lnx_g", p), MUL, col("lnx_b", p), ADD, after=[t])
                t = tt(pool, m, m, pa[:, p, 1:T + 1], ADD, after=[t])
                i, bank, free = banks.take()
                t2 = mm(bank[:, :], g2[:, p * P:(p + 1) * P], glo, True, True, after=free)
                t = tt(dve, m, bank[:, :], m, MUL, after=[t, t2])
                banks.leave(i, t)
            ends = fence()
            return out_of_mixer("l0_w_out", mixed, ends, "l0_mix_post", Area(at_rw))

        def out_of_mixer(w_name, z, ends, gain, area):
            h_area = Area(h_at)
            z_hi, z_lo = h_area.take(8, T, dtype=f32r), h_area.take(8, T, dtype=f32r)
            y = h_area.take(DT, T)
            t_in = []
            for k in range(8):
                t_in += split_into(z_hi[:, k, :], z_lo[:, k, :], z[:, k, :], ends, e_lo=dve if k % 2 else pool)
            sq = Ring([area.take(T) for _ in range(2)])
            sums = project_out(lambda m: [(w_name, m, 8)], [(z_hi[:, k, :], z_lo[:, k, :]) for k in range(8)],
                               T, y, sq, t_in)
            return add_normed(T, lambda j, s: col(gain, j), y, sums, area)

        def stick_breaking(x_toks):
            ends = fence()
            h, h_ready = norm(T, lambda j, s: col("l1_mix_pre", j), None, x_toks, ends, Area())
            fence()
            area = Area()
            qk, v, o_t = area.take(16, T), area.take(4, D), area.take(8, T)
            vt = Ring([area.take(T) for _ in range(2)])
            names = [("w_qkv", c) for c in range(24)]
            project(names[:16], P, h, h_ready, T, lambda m, c0, c1, b, t:
                    ts(dve, qk[:, m, :], b, HD ** -0.5 if m < 8 else 1.0, MUL, after=[t]))
            project(names[16:], P, h, h_ready, T, to_tokens(v, P, T, vt))
            ready = [act.last, dve.last, pe.last]
            for e in (act, dve, pool):
                e.wait(ready)
            area = Area(h_at)
            at_j = {0: (0, 0), 1: (1, 0), 3: (1, 3 * P), 2: (2, 0)}
            width = (T, T, 2 * P)
            parts = lambda: [area.take(w) for w in width]
            e_r, sp_r, at_r = (Ring([parts() for _ in range(2)]) for _ in range(3))
            sums = Ring([(area.take(3 * P), area.take(2 * P)) for _ in range(2)])
            suffix, minus = C("suffix"), C("minus")
            act.do(lambda g: g.preload_act_table_set("natural_log_exp_and_others"), signal=False)

            def block(tiles, j):
                i, at_ = at_j[j]
                return tiles[i][:, at_:at_ + T - j * P]

            def strictly_before(v, after):
                return pool.do(lambda g: g.affine_select(out=v, in_=v, compare_op=ALU.is_gt, fill=0.0, base=0,
                                                         pattern=[[1, P]], channel_multiplier=-1), after)
            heads = {}

            def scores(h):
                b0, tile = 64 * (h % 2), h // 2
                held = [banks.take() for _ in range(3)]
                i_s, acc, acc_free = sums.take()
                i_e, e_t, e_free = e_r.take()
                i_sp, sp_t, sp_free = sp_r.take()
                z = [bank[:, 0:w] for (_, bank, _), w in zip(held, width)]
                t_z = {}
                for j in (1, 3, 2, 0):
                    t_z[j] = mm(block(z, j), qk[b0:b0 + 64, 8 + tile, j * P:(j + 1) * P], qk[b0:b0 + 64, tile, j * P:T],
                                j != 3, True, after=held[at_j[j][0]][2] + ready)
                t_sp = {}
                for g, js in ((1, (1, 3)), (2, (2,)), (0, (0,))):
                    t = fn(e_t[g], z[g], ACT.Abs, after=[t_z[js[-1]]] + e_free)
                    t = fn(e_t[g], e_t[g], ACT.Exp, after=[t], scale=-1.0)
                    t = fn(e_t[g], e_t[g], ACT.Ln, after=[t], bias=ones[:, 0:1])
                    t_s = stt(sp_t[g], z[g], 0.0, e_t[g], MAX, ADD, after=[t] + sp_free)
                    for j in js:
                        t_sp[j] = strictly_before(block(sp_t, j)[:, 0:P], [t_s])
                e_r.leave(i_e, t_s)
                below, t_sum = {2: block(sp_t, 3)}, {2: t_sp[3]}
                for j in (1, 0):
                    this, a = block(sp_t, j + 1), acc[j]
                    t = copy(dve, a[:, 0:P], this[:, 0:P], after=[t_sp[j + 1]] + acc_free)
                    t_sum[j] = tt(dve, a[:, P:], this[:, P:], below[j + 1], ADD, after=[t, t_sum[j + 1]])
                    below[j] = a
                heads[h] = (held, z, sp_t, t_sp, (i_s, i_sp), below, t_sum)

            def weights(h):
                held, z, sp_t, t_sp, (i_s, i_sp), below, t_sum = heads[h]
                i_a, at_t, at_free = at_r.take()
                t_in = {}
                for j in (3, 2, 1, 0):
                    zz = block(z, j)
                    t_in[j] = mm(zz, suffix, block(sp_t, j), False, j == 3, after=[t_sp[j]], signal=(j == 3))
                    if j < 3:
                        t_in[j] = mm(zz[:, P:], minus, below[j], False, True, after=[t_sum[j]])
                sums.leave(i_s, t_in[0])
                sp_r.leave(i_sp, t_in[0], t_sum[0])
                t_at = {}
                for g, js in ((2, (2,)), (1, (1, 3)), (0, (0,))):
                    t = fn(at_t[g], z[g], ACT.Exp, after=[t_in[js[0]]] + at_free)
                    banks.leave(held[g][0], t)
                    for j in js:
                        t_at[j] = strictly_before(block(at_t, j)[:, 0:P], [t])
                heads[h] = (i_a, at_t, t_at)

            def values(h):
                i_a, at_t, t_at = heads.pop(h)
                b0 = 64 * (h % 2)
                i_o, bank_o, free_o = banks.take()
                for j in (3, 2, 1, 0):
                    t = mm(bank_o[b0:b0 + 64, j * P:T], v[:, j, h * HD:(h + 1) * HD], block(at_t, j), j == 3, j == 0,
                           after=[t_at[j]] + free_o, signal=True)
                at_r.leave(i_a, t)
                t = copy(dve, o_t[b0:b0 + 64, h // 2, :], bank_o[b0:b0 + 64, :], after=[t])
                banks.leave(i_o, t)
            for n in range(SB_HEADS + 2):
                if n < SB_HEADS:
                    scores(n)
                if n >= 2:
                    values(n - 2)
                if 1 <= n <= SB_HEADS:
                    weights(n - 1)
            ends = fence()
            return out_of_mixer("l1_w_out", o_t, ends, "l1_mix_post", Area())

        stage_ends, mod_done = [], {}
        x_toks = [[x_in] for _ in range(DT)]
        x_toks = first_layer(0, TA, x_toks)
        x_toks = first_layer(1, T, x_toks)
        x_toks = ffn("l0_ffn1", 0, x_toks)
        x_toks = even_mixer(x_toks)
        x_toks = ffn("l0_ffn2", 1, x_toks)
        x_toks = ffn("l1_ffn1", 2, x_toks)
        x_toks = stick_breaking(x_toks)
        x_toks = ffn("l1_ffn2", 3, x_toks)
        for j in range(DT):
            done = sp.dma(out_dram[:, j, :], x_sb[:, j, 0:T], out_q, after=x_toks[j])
        sp.wait([done])

        with nc.Block() as block:
            @block.sync
            def _(e):
                sp.run(e)

            @block.tensor
            def _(e):
                pe.run(e)

            @block.vector
            def _(e):
                dve.run(e)

            @block.scalar
            def _(e):
                act.run(e)

            @block.gpsimd
            def _(e):
                pool.run(e)


def constants():
    f = np.float32
    out = np.zeros((P, N_CONST), f)

    def put(name, v):
        at, n = CONSTS[name]
        out[:v.shape[0], at:at + n] = v
    put("ident", np.eye(P, dtype=f))
    put("ones", np.ones((P, P), f))
    h = np.arange(P) // HD
    put("head_ones", (h[:, None] == h[None, :]).astype(f))
    rot = np.zeros((96, 96), f)
    half = 24
    for b in range(0, 96, half):
        for i in range(12):
            rot[b + 12 + i, b + i] = -1.0
            rot[b + i, b + 12 + i] = 1.0
    put("rot", rot)
    put("half", (np.arange(96) >= DF_QK).astype(f)[:, None])
    put("eps", np.tile(np.array([[EPS, GN_EPS]], f), (P, 1)))
    t = np.arange(T)
    inv = (f(10000.0) ** (-np.arange(0, 24, 2, dtype=f) / f(24))).astype(f)
    cs, sn = np.zeros((96, T), f), np.zeros((96, T), f)
    for q in range(2):
        for part, pos in ((0, t // GRID_W), (1, t % GRID_W)):
            ang = (pos.astype(f)[None, :] * inv[:, None]).astype(f)
            for hh in range(2):
                o = q * 48 + part * 24 + hh * 12
                cs[o:o + 12], sn[o:o + 12] = np.cos(ang), np.sin(ang)
    put("cos", cs)
    put("sin", sn)
    qc = GRID_W - 1 - np.arange(P) % GRID_W
    st = np.clip(qc - WIN_W // 2, 0, GRID_W - WIN_W)
    kc = np.arange(GRID_W)
    ok = (kc[None, :] >= st[:, None]) & (kc[None, :] < st[:, None] + WIN_W)
    put("na_mask", np.where(ok, f(0), f(NEG)).astype(f))
    i, j = np.arange(P)[:, None], np.arange(P)[None, :]
    put("upper", np.concatenate([(i < j), (i <= j)], 1).astype(f))
    put("pick", (i % 32 == 16 * (j // HD)).astype(f))
    put("suffix", -(i >= j).astype(f))
    put("turn", np.kron(np.eye(2), np.eye(GRID_W)[::-1]).astype(f))
    put("minus", -np.ones((P, P), f))
    return out


def level_mask(n):
    i, j = np.arange(P)[:, None] // n, np.arange(P)[None, :] // n
    m = ((i % 2 == 1) & (j == i - 1)).astype(np.float32)
    return m, m.T


def lay_out(inp):
    f = np.float32
    I = {k: np.asarray(v) for k, v in inp.items()}
    arr = {}
    xt = np.concatenate([I["x"][0], I["ctx"][0]], 0).T
    arr["xt"] = xt.reshape(DT, P, TA).transpose(1, 0, 2)
    par = np.zeros((P, N_COLUMNS), f)

    def put(name, v, rows=P):
        at, n = COLUMNS[name]
        par[:v.shape[0], at:at + n] = v

    def cols(v):
        return v.reshape(-1, P).T
    for l in range(DEPTH):
        put(f"b_mod{l}", cols(I["b_mod"][l]))
        put(f"g_pre{l}", cols(I["g_pre"][l]))
        put(f"g_post{l}", cols(I["g_post"][l]))
        put(f"subln{l}", I["diff_subln_g"][l][:, None])
        put(f"conv_w{l}", I["conv_w"][l].reshape(TAPS, 2, P).transpose(2, 1, 0).reshape(P, 2 * TAPS))
        put(f"conv_b{l}", cols(I["conv_b"][l]))
        put(f"ln_g{l}", cols(I["conv_ln_g"][l]))
        put(f"ln_b{l}", cols(I["conv_ln_b"][l]))
        put(f"lq{l}", np.stack([I["diff_lq1"][l], I["diff_lq2"][l]], 1))
        put(f"lk{l}", np.stack([I["diff_lk1"][l], I["diff_lk2"][l]], 1))
        arr[f"w_mod{l}"] = by_columns(I["w_mod"][l], P)
        w = I["w_in"][l]
        pieces = []
        for g, at in IN_PIECE.items():
            width = GROUP // len(at)
            p = by_columns(w[:, g * GROUP:(g + 1) * GROUP], width)
            pieces.append(np.pad(p, ((0, 0), (0, 0), (0, SLOT - p.shape[2]))))
        arr[f"w_in{l}"] = np.concatenate(pieces, 0)
        wo = I["w_out"][l]
        padded = np.zeros((9, P, D), f)
        padded[0:3] = wo[0:384].reshape(3, P, D)
        padded[3:7, 0:96] = wo[384:768].reshape(4, 96, D)
        padded[7:9] = wo[768:1024].reshape(2, P, D)
        arr[f"w_out{l}"] = by_k_runs(padded, W_OUT_K)
        rp = np.zeros((NA_HEADS * 15, P), f)
        rp[:, 48:79] = I["na_rpb"][l].reshape(NA_HEADS * 15, 31)
        arr[f"rpb{l}"] = rp
    put("cond", np.stack([cols(I["c"][0]), cols(I["c_ctx"])], 2).reshape(P, 16))
    for n in ("l0_ffn1", "l0_ffn2", "l1_ffn1", "l1_ffn2", "l0_mix", "l1_mix"):
        put(n + "_pre", cols(I[n + "_pre_g_2"]))
        put(n + "_post", cols(I[n + "_post_g_2"]))
    for n in ("l0_ffn1", "l0_ffn2", "l1_ffn1", "l1_ffn2"):
        w = I[n + "_w_in_2"]
        g, u = by_columns(w[:, :D_FF], P), by_columns(w[:, D_FF:], P)
        arr[n + "_w_in"] = np.stack([g, u], 1).reshape(2 * FT, P, -1)
        w = I[n + "_w_out_2"].reshape(2, FT // 2, P, D)
        for half in range(2):
            arr[n + f"_w_out{half}"] = by_k_runs(w[half], FFN_K[:2])
    put("mu", cols(I["l0_mu_2"]))
    for a, b in (("w0", "l0_w0_2"), ("a0", "l0_a0_2"), ("k_k", "l0_k_k_2"), ("k_a", "l0_k_a_2"),
                 ("r_k", "l0_r_k_2"), ("lnx_g", "l0_lnx_g_2"), ("lnx_b", "l0_lnx_b_2"), ("rconv_b", "l0_conv_b_2"),
                 ("ga_b", "l0_gate_a_b_2"), ("gx_b", "l0_gate_x_b_2"), ("lam", "l0_lambda_2")):
        put(a, cols(I[b]))
    put("rconv_w", I["l0_conv_w_2"].reshape(4, 4, P).transpose(2, 1, 0).reshape(P, 16))
    arr["l0_w_in"] = by_columns(I["l0_w_in_2"], P)
    arr["l0_w_out"] = by_columns(I["l0_w_out_2"], P)
    arr["lora"] = np.concatenate([np.concatenate([I["l0_w2_2"], I["l0_a2_2"]], 0), I["l0_g2_2"]], 1)
    gates = [I[n].reshape(4, 2, HD, HD).transpose(1, 2, 0, 3).reshape(P, 4 * HD)
             for n in ("l0_gate_a_w_2", "l0_gate_x_w_2")]
    arr["gate_w"] = np.concatenate(gates, 1)
    arr["w_qkv"] = by_columns(I["l1_w_qkv_2"], P)
    arr["l1_w_out"] = by_columns(I["l1_w_out_2"], P)
    arr["par"] = par
    arr["const"] = constants()
    arr["levels"] = np.concatenate([m for n in LEVELS for m in level_mask(n)], 1)
    return {k: np.ascontiguousarray(v) for k, v in arr.items()}


def by_columns(w, width, parts=1):
    k, n = w.shape
    v = w.reshape(parts, k // P // parts, P, n // width, width).transpose(3, 0, 2, 1, 4)
    return v.reshape(n // width * parts, P, -1)


def by_k_runs(w, runs):
    out = np.zeros((D // P, len(runs), P, runs[0] * P), w.dtype)
    at = 0
    for i, n in enumerate(runs):
        v = w[at:at + n].reshape(n, P, D // P, P).transpose(2, 1, 0, 3)
        out[:, i, :, :n * P] = v.reshape(D // P, P, n * P)
        at += n
    return out.reshape(-1, P, runs[0] * P)


def kernel(**inputs):
    import concourse.bacc as bacc
    from concourse.bass_utils import run_bass_kernel_spmd

    arrays = lay_out(inputs)
    nc = bacc.Bacc("TRN2", target_bir_lowering=False, num_devices=1)
    ins = {n: nc.dram_tensor(f"in_{n}", a.shape, mybir.dt.float32, kind="ExternalInput").ap()
           for n, a in arrays.items()}
    out = nc.dram_tensor("out", (P, DT, T), mybir.dt.float32, kind="ExternalOutput").ap()
    build(nc, ins, out)
    r = run_bass_kernel_spmd(nc, [{f"in_{n}": a for n, a in arrays.items()}], core_ids=[0])
    y = r.results[0]["out"]
    return np.ascontiguousarray(y.transpose(1, 0, 2).reshape(D, T).T)[None]
```
